# Optimizing a Trainium2 kernel written in Bass

```python
import math
import jax, jax.numpy as jnp
from jax import lax
import numpy as np

D_MODEL = 1024
BATCH = 1
SEQ = 1024
DEPTH = 1

N_META = 16
ATT_HEADS = 8
ATT_KV_HEADS = 2
ATT_GROUP = ATT_HEADS // ATT_KV_HEADS
HEAD_DIM = 64
WINDOW = 128
BLOCK = 128
RWKV_HEADS = 8
RWKV_HEAD_DIM = 64
RWKV_DIM = RWKV_HEADS * RWKV_HEAD_DIM
DECAY_LORA = 64
AAA_LORA = 64
GATE_LORA = 128
LN_X_EPS = 64e-5
N_BRANCH = 2
ATT_Q = ATT_HEADS * HEAD_DIM
ATT_KV = ATT_KV_HEADS * HEAD_DIM
ATT_COLS = ATT_Q + 2 * ATT_KV
RWKV_COLS = 3 * RWKV_DIM + DECAY_LORA + AAA_LORA + GATE_LORA
GATE_COLS = N_BRANCH * D_MODEL
IN_COLS = ATT_COLS + RWKV_COLS + GATE_COLS
N_GROUPS = 4
EXPERTS_PER_GROUP = 8
N_EXPERTS = N_GROUPS * EXPERTS_PER_GROUP
TOP_K = 2
D_EXPERT = 256
MOE_BLOCK = 128
NORM_EPS = 1e-6

kernel_name = "hybrid_swa_rwkv7_hiermoe_block"

def rmsnorm(x, g):
    x32 = x.astype(jnp.float32)
    y = x32 * lax.rsqrt(jnp.mean(x32 * x32, axis=-1, keepdims=True) + NORM_EPS)
    return y.astype(x.dtype) * g

def alibi_slopes(n_heads):
    return jnp.asarray(np.array([2.0 ** (-8.0 * (i + 1) / n_heads) for i in range(n_heads)], dtype=np.float32))

def sliding_window_attention(q, k, v, sinks):
    B, T = q.shape[0], q.shape[1]
    pad_front = (-N_META) % BLOCK
    pad_tail = (-(T + pad_front)) % BLOCK
    Tp = T + pad_front + pad_tail
    nb = Tp // BLOCK
    pw = ((0, 0), (pad_front, pad_tail), (0, 0), (0, 0))
    qb = jnp.pad(q, pw).reshape(B, nb, BLOCK, ATT_KV_HEADS, ATT_GROUP, HEAD_DIM)
    kb = jnp.pad(k, pw).reshape(B, nb, BLOCK, ATT_KV_HEADS, HEAD_DIM)
    vb = jnp.pad(v, pw).reshape(B, nb, BLOCK, ATT_KV_HEADS, HEAD_DIM)
    zero_blk = jnp.zeros_like(kb[:, :1])
    k_band = jnp.concatenate([jnp.concatenate([zero_blk, kb[:, :-1]], axis=1), kb], axis=2)
    v_band = jnp.concatenate([jnp.concatenate([zero_blk, vb[:, :-1]], axis=1), vb], axis=2)
    k_meta = k[:, :N_META]
    v_meta = jnp.broadcast_to(v[:, None, :N_META], (B, nb, N_META, ATT_KV_HEADS, HEAD_DIM))

    meta_start = pad_front
    real_start = pad_front + N_META
    qpos = jnp.arange(Tp, dtype=jnp.int32).reshape(nb, BLOCK)
    kpos = (jnp.arange(nb, dtype=jnp.int32)[:, None] - 1) * BLOCK + jnp.arange(2 * BLOCK, dtype=jnp.int32)[None, :]
    diff = qpos[:, :, None] - kpos[:, None, :]
    band_mask = (diff >= 0) & (diff < WINDOW) & (kpos >= real_start)[:, None, :]
    mpos = meta_start + jnp.arange(N_META, dtype=jnp.int32)
    diff_m = qpos[:, :, None] - mpos[None, None, :]
    meta_mask = diff_m >= 0
    dist_m = jnp.minimum(diff_m, WINDOW)

    slopes = alibi_slopes(ATT_HEADS).reshape(1, ATT_KV_HEADS, ATT_GROUP, 1, 1)
    neg_inf = jnp.float32(-jnp.inf)
    bias_band = jnp.where(band_mask[:, None, None], -slopes * diff[:, None, None].astype(jnp.float32), neg_inf)
    bias_meta = jnp.where(meta_mask[:, None, None], -slopes * dist_m[:, None, None].astype(jnp.float32), neg_inf)

    scale = HEAD_DIM ** -0.5
    s_band = jnp.einsum('bnqhgd,bnkhd->bnhgqk', qb, k_band).astype(jnp.float32) * scale + bias_band[None]
    s_meta = jnp.einsum('bnqhgd,bmhd->bnhgqm', qb, k_meta).astype(jnp.float32) * scale + bias_meta[None]
    logits = jnp.concatenate([s_band, s_meta], axis=-1)
    sink = sinks.astype(jnp.float32).reshape(1, 1, ATT_KV_HEADS, ATT_GROUP, 1, 1)
    m = jnp.maximum(jnp.max(logits, axis=-1, keepdims=True), sink)
    p = jnp.exp(logits - m)
    probs = p / (jnp.sum(p, axis=-1, keepdims=True) + jnp.exp(sink - m))
    v_all = jnp.concatenate([v_band, v_meta], axis=2)
    o = jnp.einsum('bnhgqk,bnkhd->bnqhgd', probs.astype(v.dtype), v_all)
    o = o.reshape(B, Tp, ATT_Q)
    return o[:, pad_front:pad_front + T]

def rwkv7_time_mix(c, shift_mu, w0, w_decay_up, a0, w_aaa_up, w_gate_up, k_k, k_a, r_k, ln_x_g, ln_x_b):
    B, T, _ = c.shape
    c_prev = jnp.pad(c, ((0, 0), (1, 0), (0, 0)))[:, :-1]
    c = c + shift_mu * (c_prev - c)
    r, k, v, xw, xa, xg = jnp.split(c, np.cumsum([RWKV_DIM, RWKV_DIM, RWKV_DIM, DECAY_LORA, AAA_LORA]).tolist(), axis=-1)
    r, k, v = (t.astype(jnp.float32) for t in (r, k, v))
    w = -jax.nn.softplus(-(w0 + jnp.tanh(xw) @ w_decay_up).astype(jnp.float32)) - 0.5
    decay = jnp.exp(-jnp.exp(w))
    a = jax.nn.sigmoid((a0 + xa @ w_aaa_up).astype(jnp.float32))
    g = jax.nn.sigmoid(xg) @ w_gate_up

    hs = (B, T, RWKV_HEADS, RWKV_HEAD_DIM)
    r, k, v, decay, a = (t.reshape(hs) for t in (r, k, v, decay, a))
    k_k = k_k.astype(jnp.float32).reshape(RWKV_HEADS, RWKV_HEAD_DIM)
    k_a = k_a.astype(jnp.float32).reshape(RWKV_HEADS, RWKV_HEAD_DIM)
    kk = k * k_k
    kk = kk / jnp.maximum(jnp.sqrt(jnp.sum(kk * kk, axis=-1, keepdims=True)), 1e-12)
    k = k * (1.0 + (a - 1.0) * k_a)

    def step(S, inp):
        r_t, w_t, k_t, v_t, a_t, b_t = inp
        sa = jnp.einsum('bhij,bhj->bhi', S, a_t)
        S = S * w_t[:, :, None, :] + sa[..., None] * b_t[:, :, None, :] + v_t[..., None] * k_t[:, :, None, :]
        return S, jnp.einsum('bhij,bhj->bhi', S, r_t)

    to_t = lambda t: jnp.swapaxes(t, 0, 1)
    S0 = jnp.zeros((B, RWKV_HEADS, RWKV_HEAD_DIM, RWKV_HEAD_DIM), jnp.float32)
    _, y = lax.scan(step, S0, (to_t(r), to_t(decay), to_t(k), to_t(v), to_t(-kk), to_t(kk * a)))
    y = jnp.swapaxes(y, 0, 1)
    mu = jnp.mean(y, axis=-1, keepdims=True)
    var = jnp.mean(jnp.square(y - mu), axis=-1, keepdims=True)
    y = ((y - mu) * lax.rsqrt(var + LN_X_EPS)).reshape(B, T, RWKV_DIM)
    y = y * ln_x_g.astype(jnp.float32) + ln_x_b.astype(jnp.float32)
    bonus = jnp.sum(r * k * r_k.astype(jnp.float32), axis=-1, keepdims=True) * v
    y = y + bonus.reshape(B, T, RWKV_DIM)
    return y.astype(c.dtype) * g

def hierarchical_moe(x, w_grp, b_grp, w_exp, b_exp, e_gate, e_up, e_down):
    B, T, D = x.shape
    xf = x.reshape(-1, D)
    N = xf.shape[0]
    grp_logits = (xf @ w_grp + b_grp).astype(jnp.float32)
    p_grp = jax.nn.softmax(grp_logits, axis=-1)
    g_sel = jnp.argmax(grp_logits, axis=-1).astype(jnp.int32)
    exp_logits = (xf @ w_exp + b_exp).astype(jnp.float32).reshape(N, N_GROUPS, EXPERTS_PER_GROUP)
    in_grp = jnp.take_along_axis(exp_logits, g_sel[:, None, None], axis=1)[:, 0]
    top_v, top_i = lax.top_k(in_grp, TOP_K)
    gate = jax.nn.softmax(top_v, axis=-1) * jnp.take_along_axis(p_grp, g_sel[:, None], axis=1)
    expert_id = g_sel[:, None] * EXPERTS_PER_GROUP + top_i.astype(jnp.int32)

    A = N * TOP_K
    eid = expert_id.reshape(-1)
    tok = jnp.repeat(jnp.arange(N, dtype=jnp.int32), TOP_K)
    wt = gate.reshape(-1)
    order = jnp.argsort(eid)
    s_eid, s_tok, s_wt = eid[order], tok[order], wt[order]
    counts = jax.ops.segment_sum(jnp.ones_like(eid), eid, num_segments=N_EXPERTS)
    starts = jnp.cumsum(counts) - counts
    padded = ((counts + MOE_BLOCK - 1) // MOE_BLOCK) * MOE_BLOCK
    pends = jnp.cumsum(padded)
    pstarts = pends - padded
    dest = pstarts[s_eid] + jnp.arange(A, dtype=jnp.int32) - starts[s_eid]
    n_blocks = -(-(A + N_EXPERTS * (MOE_BLOCK - 1)) // MOE_BLOCK)
    cap = n_blocks * MOE_BLOCK
    slot_tok = jnp.full((cap,), N, dtype=jnp.int32).at[dest].set(s_tok)
    slot_wt = jnp.zeros((cap,), jnp.float32).at[dest].set(s_wt)
    block_start = jnp.arange(n_blocks, dtype=jnp.int32) * MOE_BLOCK
    block_expert = jnp.minimum(jnp.sum(block_start[:, None] >= pends[None, :], axis=1), N_EXPERTS - 1)

    x_pad = jnp.concatenate([xf, jnp.zeros((1, D), xf.dtype)], axis=0)
    xb = x_pad[slot_tok].reshape(n_blocks, MOE_BLOCK, D)

    def expert_block(args):
        xblk, e = args
        hmid = jax.nn.silu(xblk @ e_gate[e]) * (xblk @ e_up[e])
        return hmid @ e_down[e]

    yb = lax.map(expert_block, (xb, block_expert)).reshape(cap, D)
    y = jnp.zeros((N + 1, D), jnp.float32).at[slot_tok].add(yb.astype(jnp.float32) * slot_wt[:, None])
    return y[:N].astype(x.dtype).reshape(B, T, D)

def setup_inputs(seed: int = 0) -> dict:
    key = jax.random.key(seed)
    ks = jax.random.split(key, 32)
    L, D = DEPTH, D_MODEL
    nrm = lambda k, shape, s: jax.random.normal(k, shape, jnp.float32) * s
    return {
        "x": nrm(ks[0], (BATCH, SEQ, D), 1.0),
        "meta_tokens": nrm(ks[1], (N_META, D), 1.0),
        "norm_mix_g": 1.0 + nrm(ks[2], (L, D), 0.05),
        "w_in": nrm(ks[3], (L, D, IN_COLS), D ** -0.5),
        "shift_mu": jax.random.uniform(ks[4], (L, RWKV_COLS), jnp.float32),
        "w0": jax.random.uniform(ks[5], (L, RWKV_DIM), jnp.float32, minval=-6.0, maxval=-1.0),
        "w_decay_up": nrm(ks[6], (L, DECAY_LORA, RWKV_DIM), DECAY_LORA ** -0.5),
        "a0": nrm(ks[7], (L, RWKV_DIM), 0.5),
        "w_aaa_up": nrm(ks[8], (L, AAA_LORA, RWKV_DIM), 0.5 * AAA_LORA ** -0.5),
        "w_gate_up": nrm(ks[9], (L, GATE_LORA, RWKV_DIM), GATE_LORA ** -0.5),
        "k_k": 0.85 + nrm(ks[10], (L, RWKV_DIM), 0.1),
        "k_a": 1.0 + nrm(ks[11], (L, RWKV_DIM), 0.1),
        "r_k": nrm(ks[12], (L, RWKV_HEADS, RWKV_HEAD_DIM), 0.1),
        "ln_x_g": 1.0 + nrm(ks[13], (L, RWKV_DIM), 0.1),
        "ln_x_b": nrm(ks[14], (L, RWKV_DIM), 0.01),
        "attn_sinks": nrm(ks[15], (L, ATT_HEADS), 1.0),
        "w_o_attn": nrm(ks[16], (L, ATT_Q, D), ATT_Q ** -0.5),
        "w_o_rwkv": nrm(ks[17], (L, RWKV_DIM, D), RWKV_DIM ** -0.5),
        "w_out": nrm(ks[18], (L, D, D), D ** -0.5),
        "norm_ffn_g": 1.0 + nrm(ks[19], (L, D), 0.05),
        "w_grp": nrm(ks[20], (L, D, N_GROUPS), D ** -0.5),
        "b_grp": nrm(ks[21], (L, N_GROUPS), 0.01),
        "w_exp": nrm(ks[22], (L, D, N_EXPERTS), D ** -0.5),
        "b_exp": nrm(ks[23], (L, N_EXPERTS), 0.01),
        "e_gate": nrm(ks[24], (L, N_EXPERTS, D, D_EXPERT), D ** -0.5),
        "e_up": nrm(ks[25], (L, N_EXPERTS, D, D_EXPERT), D ** -0.5),
        "e_down": nrm(ks[26], (L, N_EXPERTS, D_EXPERT, D), D_EXPERT ** -0.5),
        "norm_final_g": 1.0 + nrm(ks[27], (D,), 0.05),
    }

def reference(x, meta_tokens, norm_mix_g, w_in, shift_mu, w0, w_decay_up, a0, w_aaa_up, w_gate_up,
              k_k, k_a, r_k, ln_x_g, ln_x_b, attn_sinks, w_o_attn, w_o_rwkv, w_out, norm_ffn_g,
              w_grp, b_grp, w_exp, b_exp, e_gate, e_up, e_down, norm_final_g):
    B = x.shape[0]
    meta = jnp.broadcast_to(meta_tokens.astype(x.dtype)[None], (B, N_META, D_MODEL))
    h = jnp.concatenate([meta, x], axis=1)
    T = h.shape[1]
    for l in range(DEPTH):
        xn = rmsnorm(h, norm_mix_g[l])
        cols = xn @ w_in[l]
        att_c = cols[..., :ATT_COLS]
        rwkv_c = cols[..., ATT_COLS:ATT_COLS + RWKV_COLS]
        gate_c = cols[..., ATT_COLS + RWKV_COLS:]
        q = att_c[..., :ATT_Q].reshape(B, T, ATT_HEADS, HEAD_DIM)
        k = att_c[..., ATT_Q:ATT_Q + ATT_KV].reshape(B, T, ATT_KV_HEADS, HEAD_DIM)
        v = att_c[..., ATT_Q + ATT_KV:].reshape(B, T, ATT_KV_HEADS, HEAD_DIM)
        att_out = sliding_window_attention(q, k, v, attn_sinks[l]) @ w_o_attn[l]
        rwkv_out = rwkv7_time_mix(rwkv_c, shift_mu[l], w0[l], w_decay_up[l], a0[l], w_aaa_up[l], w_gate_up[l],
                                  k_k[l], k_a[l], r_k[l], ln_x_g[l], ln_x_b[l]) @ w_o_rwkv[l]
        gates = jax.nn.sigmoid(gate_c.reshape(B, T, N_BRANCH, D_MODEL))
        merged = gates[:, :, 0] * att_out + gates[:, :, 1] * rwkv_out
        h = h + merged @ w_out[l]
        h = h + hierarchical_moe(rmsnorm(h, norm_ffn_g[l]), w_grp[l], b_grp[l], w_exp[l], b_exp[l],
                                 e_gate[l], e_up[l], e_down[l])
    h = rmsnorm(h, norm_final_g)
    return h[:, N_META:]


_drawn_inputs = setup_inputs


def setup_inputs(seed=0):
    import zlib

    import numpy as np

    out = dict(_drawn_inputs(seed))
    spreads = {}
    factors = {'ln_x_b': 5.476, 'attn_sinks': 2.701, 'b_grp': 28.641, 'b_exp': 4.253}
    for name, (base, spread) in spreads.items():
        noise = np.random.default_rng([zlib.crc32(name.encode()), seed]).standard_normal(out[name].shape)
        drawn = base * np.exp(spread * noise) if base else spread * noise
        out[name] = __import__('jax').numpy.asarray(drawn.astype(out[name].dtype))
    for name, factor in factors.items():
        out[name] = (out[name] * factor).astype(out[name].dtype)
    return out
```

```python
from contextlib import ExitStack

import numpy as np
import concourse.bass as bass
from concourse import mybir

F32 = mybir.dt.float32
I32 = mybir.dt.int32
U32 = mybir.dt.uint32
U8 = mybir.dt.uint8
ACT = mybir.ActivationFunctionType
ALU = mybir.AluOpType
AX = mybir.AxisListType

P = 128
D = 1024
KD = D // P
SEQ = 1024
META = 16
NB = SEQ // P
T = META + SEQ
PAD = P - META
TP = T + PAD
NBLK = TP // P
GROUP = 347
NGROUPS = 3
TG = GROUP * NGROUPS
HEADS = 8
HD = 64
PAIRS = HEADS // 2
KV = 2
RD = HEADS * HD
SCALE = HD ** -0.5
BAND = 2 * P + META
CH_Q, CH_K, CH_V, CH_RR, CH_RK, CH_RV, CH_WA, CH_G, CHUNKS = 0, 4, 5, 6, 10, 14, 18, 19, 20
CH_MIX = CH_RK
GATE0 = CHUNKS * P
EPS = 1e-6
LN_EPS = 64e-5
DECAY = float(np.exp(-0.5))
E = 32
NG = 4
EG = E // NG
F = 256
TOPK = 2
BLOCKS = -(-(SEQ * TOPK + E * (P - 1)) // P)
NEG = -1e30
LEVELS = [1, 2, 4, 8, 16]


def constants():
    i = np.arange(P)
    row, col = i[:, None], i[None, :]
    c = {}
    c["ident"] = np.eye(P, dtype=np.float32)
    c["headones"] = (row // HD == col // HD).astype(np.float32)
    upper = np.stack([row < col, row <= col], 1)
    c["upper"] = upper.astype(np.float32)
    c["lower"] = (row > col).astype(np.float32)
    low = [((row // n) % 2 == 1) & (col // n == row // n - 1) for n in LEVELS]
    c["lev"] = np.stack([np.stack([m, m.T], 1) for m in low], 1).astype(np.float32)
    q, k = np.arange(P)[:, None], np.arange(2 * P)[None, :]
    diff = q + P - k
    m = np.arange(META)[None, :]
    slopes = 2.0 ** (-8.0 * (np.arange(HEADS) + 1) / HEADS)
    bias = np.zeros((NBLK, P, HEADS, BAND), np.float32)
    for b in range(NBLK):
        seen = (diff >= 0) & (diff < P) & (((b - 1) * P + k) >= P)
        far = np.minimum(b * P + q - PAD - m, P)
        for h in range(HEADS):
            bias[b, :, h, :2 * P] = np.where(seen, -slopes[h] * diff, NEG)
            bias[b, :, h, 2 * P:] = np.where(far >= 0, -slopes[h] * far, NEG)
    c["bias"] = bias.reshape(NBLK * P, HEADS * BAND)
    reset = np.ones((P, PAIRS, P), np.float32)
    reset[:, :, 0] = 0.0
    c["reset"] = reset.reshape(P, PAIRS * P)
    c["iota"] = np.tile(np.arange(E, dtype=np.float32), (P, 1))
    c["blockno"] = np.tile(np.arange(BLOCKS, dtype=np.float32), (P, 1))
    c["over"] = np.tile(P * np.arange(NB, dtype=np.float32), (P, 1))
    c["tokno"] = (np.arange(NB)[None, :] * P + np.arange(P)[:, None]).astype(np.int32)
    return c


class Chain:

    def __init__(self, eng, sem, base=0):
        self.eng, self.sem, self.base, self.n = eng, sem, base, 0

    def add(self, ins):
        self.n += 1
        return ins.then_inc(self.sem, 1)

    def join(self):
        self.eng.wait_ge(self.sem, self.base + self.n)

    def __call__(self, ins):
        self.add(ins)
        self.join()


def norm_and_turn(nc, sems, t, d):
    loaded, squared, scaled, turned, taken, own, spilled = sems(
        "loaded", "squared", "scaled", "turned", "taken", "own", "spilled")
    with ExitStack() as ctx:
        sb = lambda n, s, dt=F32: ctx.enter_context(nc.sbuf_tensor(n, s, dt))
        xall = sb("xall", [P, NB, D])
        xmeta = sb("xmeta", [META, D])
        gmix = sb("gmix", [P, KD])
        sq = sb("sq", [P, D])
        ssq = sb("ssq", [P, NB + 1])
        rstd = sb("rstd", [P, NB + 1])
        xs = sb("xs", [P, D])
        ps = ctx.enter_context(nc.psum_tensor("turn_ps", [P, KD, P], F32))
        ident, xnT = t["ident"], t["xnT"]
        block = ctx.enter_context(nc.Block())

        def tiles(eng):
            yield META, xmeta[:, :], 0, 0
            with eng.Fori(0, NB) as i:
                yield P, xall[:, bass.ds(i, 1), :].rearrange("p a d -> p (a d)"), META + i * P, i + 1

        @block.sync
        def _(sp):
            sp.dma_start(xmeta[:, :], d["meta_tokens"][:, :]).then_inc(loaded, 16)
            sp.dma_start(gmix[:, :], d["norm_mix_g"].rearrange("l (c p) -> p (l c)", p=P), allow_slow_non_contiguous=True).then_inc(loaded, 16)
            sp.dma_start(xall[:, :, :], d["x"].rearrange("b (n p) d -> p (b n) d", p=P)).then_inc(loaded, 16)
            sp.dma_start(ident[:, :], d["c_ident"]).then_inc(loaded, 16)
            sp.wait_ge(taken, 1 + 2 * (NB + 1))
            sp.dma_start(d["xn_spill"].rearrange("p (c j) -> p c j", c=KD), xnT[:, :, META:T]).then_inc(spilled, 16)
            sp.wait_ge(spilled, 16)

        n_loads = 16 * 4

        @block.scalar
        def _(act):
            act.wait_ge(loaded, n_loads)
            act.wait_ge(own, 2)
            for rows, src, _, n in tiles(act):
                act.wait_ge(squared, n + 1)
                act.activation(sq[0:rows, :], src, ACT.Square, accum_out=ssq[0:rows, bass.ds(n, 1)]).then_inc(squared, 1)
            act.wait_ge(own, 3)
            act.activation(rstd[:, :], ssq[:, :], ACT.Sqrt).then_inc(own, 1)

        @block.vector
        def _(v):
            v.memset(xnT[:, :, T:TG], 0.0).then_inc(own, 1)
            v.memset(ssq[:, :], 1.0).then_inc(own, 1)
            v.sem_inc(squared, 1)
            v.sem_inc(scaled, 1)
            v.wait_ge(loaded, n_loads)
            v.wait_ge(squared, 1 + NB + 1)
            v.tensor_scalar(ssq[:, :], ssq[:, :], 1.0 / D, EPS, ALU.mult, ALU.add).then_inc(own, 1)
            v.wait_ge(own, 4)
            v.reciprocal(rstd[:, :], rstd[:, :]).then_inc(own, 1)
            v.wait_ge(own, 5)
            for rows, src, col, n in tiles(v):
                v.wait_ge(turned, n + 1)
                v.tensor_scalar(xs[0:rows, :], src, rstd[0:rows, bass.ds(n, 1)], None, ALU.mult).then_inc(scaled, 1)
                v.wait_ge(turned, n + 2)
                for h in range(2):
                    c0 = h * KD // 2
                    out = xnT[:, c0:c0 + KD // 2, bass.ds(col, rows)]
                    v.tensor_tensor(out, ps[:, c0:c0 + KD // 2, 0:rows],
                                    gmix[:, c0:c0 + KD // 2].unsqueeze(2).broadcast_to([P, KD // 2, rows]),
                                    ALU.mult).then_inc(taken, 1)

        @block.tensor
        def _(pe):
            pe.sem_inc(turned, 1)
            pe.sem_inc(taken, 1)
            pe.wait_ge(loaded, n_loads)
            for rows, _, _, n in tiles(pe):
                pe.wait_ge(scaled, n + 2)
                pe.wait_ge(taken, 2 * n + 1)
                for c in range(KD):
                    last = pe.transpose(ps[:, c, 0:rows], xs[0:rows, c * P:(c + 1) * P], ident[0:rows, 0:rows])
                last.then_inc(turned, 1)


def project(nc, sems, t, d):
    wl, mm, ev, sh, used, own = sems("p_wl", "p_mm", "p_ev", "p_sh", "p_used", "p_own")
    wl2, = sems("p_wl2")
    CPL = 2
    STEPS = CHUNKS // (2 * CPL)
    with ExitStack() as ctx:
        sb = lambda n, s, dt=F32: ctx.enter_context(nc.sbuf_tensor(n, s, dt))
        w = sb("w_in_sb", [P, 2, KD, CPL * P])
        raw = sb("raw", [P, 2, 1 + TG])
        tmp = sb("shift_tmp", [P, T])
        mu = sb("mu", [P, CHUNKS])
        ps = ctx.enter_context(nc.psum_tensor("proj_ps", [P, 2, NGROUPS, 512], F32))
        xnT, cT = t["xnT"], t["cT"]
        wv = d["w_in"].rearrange("l (c p) n -> p (l c) n", p=P)
        block = ctx.enter_context(nc.Block())

        @block.sync
        def _(sp):
            sp.wait_ge(own, 3)
            sp.dma_start(mu[:, CH_RR:CHUNKS], d["shift_mu"].rearrange("l (c p) -> p (l c)", p=P), allow_slow_non_contiguous=True).then_inc(own, 16)
            for half, sem in enumerate((wl, wl2)):
                sp.dma_start(w[:, half], wv[:, :, half * CPL * P:(half + 1) * CPL * P]).then_inc(sem, 16)
            with sp.Fori(1, STEPS) as i:
                for half, sem in enumerate((wl, wl2)):
                    sp.wait_ge(mm, (i - 1) * 2 * CPL + (half + 1) * CPL)
                    sp.dma_start(w[:, half], wv[:, :, bass.ds(i * (2 * CPL * P) + half * CPL * P, CPL * P)]).then_inc(sem, 16)

        @block.tensor
        def _(pe):
            with pe.Fori(0, STEPS) as i:
                for half in range(2):
                    pe.wait_ge(wl2 if half else wl, (i + 1) * 16)
                    for c in range(CPL):
                        n = half * CPL + c
                        pe.wait_ge(ev, i * (2 * CPL) + n + 1)
                        for g in range(NGROUPS):
                            for k in range(KD):
                                last = pe.matmul(ps[:, n % 2, g, 0:GROUP], w[:, half, k, c * P:(c + 1) * P],
                                                 xnT[:, k, g * GROUP:(g + 1) * GROUP], start=(k == 0), stop=(k == KD - 1))
                        last.then_inc(mm, 1)

        @block.scalar
        def _(act):
            act.sem_inc(ev, 2)
            with act.Fori(0, STEPS) as i:
                for n in range(2 * CPL):
                    act.wait_ge(mm, i * (2 * CPL) + n + 1)
                    act.wait_ge(sh, i * (2 * CPL) + n + 1)
                    act.activation(raw[:, n % 2, 1:1 + TG].rearrange("p (g j) -> p g j", g=NGROUPS),
                                   ps[:, n % 2, :, 0:GROUP], ACT.Copy).then_inc(ev, 1)

        @block.vector
        def _(v):
            v.memset(raw[:, :, 0:1], 0.0).then_inc(own, 1)
            v.memset(mu[:, 0:CH_RR], 0.0).then_inc(own, 1)
            v.memset(cT[:, :, 0:PAD], 0.0).then_inc(own, 1)
            v.sem_inc(sh, 2)
            v.wait_ge(own, 3 + 16)
            with v.Fori(0, STEPS) as i:
                for n in range(2 * CPL):
                    v.wait_ge(ev, i * (2 * CPL) + n + 3)
                    v.wait_ge(sh, i * (2 * CPL) + n + 2)
                    v.tensor_tensor(tmp[:, :], raw[:, n % 2, 0:T], raw[:, n % 2, 1:1 + T], ALU.subtract).then_inc(used, 1)
                    v.wait_ge(used, i * (2 * CPL) + n + 1)
                    out = cT[:, bass.ds(i * (2 * CPL) + n, 1), PAD:TP].rearrange("p a j -> p (a j)")
                    col = i * (2 * CPL) + n
                    v.scalar_tensor_tensor(out, tmp[:, :], mu[:, bass.ds(col, 1)], raw[:, n % 2, 1:1 + T],
                                           ALU.mult, ALU.add).then_inc(sh, 1)


def mix(nc, sems, t, d):
    names = ("x_par x_bias x_st x_lora x_sg x_mmw x_mma x_mmg x_th x_tha x_qk x_lgt x_va x_ss x_rn x_kkr x_rec "
             "x_exp x_csd x_ar x_bk x_mmM x_msk x_mmA x_tt x_tok x_tinit x_x1 x_x1c x_yy x_tup x_W x_Wc x_U x_Uc "
             "x_Y x_Yc x_S x_S0 x_Sn x_mean x_sqr x_var x_vr x_sd x_bon x_rk x_mx x_pe x_pn x_tp x_tpc x_O x_att "
             "x_y x_v x_a x_p x_init x_kb x_es x_yc x_gc x_vm x_lgt0")
    s = dict(zip([n[2:] for n in names.split()], sems(*names.split())))
    NV, NA = t["mix_counts"]
    with ExitStack() as ctx:
        sb = lambda n, sh, dt=F32: ctx.enter_context(nc.sbuf_tensor(n, sh, dt))
        ident, cT = t["ident"], t["cT"]
        headones, upper, lower = sb("headones", [P, P]), sb("upper", [P, 2, P]), sb("lower", [P, P])
        lev = sb("lev", [P, len(LEVELS), 2, P], U8)
        reset = sb("reset", [P, PAIRS * P])
        wup, gup = sb("wup", [P, RD]), sb("gup", [P, RD])
        par = sb("par", [P, 9, PAIRS])
        hw0, ha0, kkw, hka, rkw, lng, lnb, omk = (par[:, n] for n in range(8))
        sink = sb("sink", [P, HEADS])
        bias = sb("bias", [P, HEADS, BAND])
        qs, kb = sb("qs", [P, PAIRS, P]), sb("kb", [P, KV, BAND])
        lg = sb("lg", [P, HEADS, BAND])
        lev_in = lg[:, :, :].rearrange("p h k -> p (h k)")[:, 0:len(LEVELS) * 2 * P].rearrange("p (l a j) -> p l a j", l=len(LEVELS), a=2)
        st8 = sb("st8", [P, 5, HEADS])
        mx, nmx, dsk, es, ls = (st8[:, n] for n in range(5))
        vas, vtok = sb("vas", [P, P]), sb("vtok", [P, 3, P])
        pT, pTm = sb("pT", [P, 2, HEADS, P]), sb("pTm", [META, HEADS, P])
        lora, sg = sb("lora", [P, P]), sb("sg", [P, P])
        wide = lambda n: sb(n, [P, PAIRS, P])
        th, tha, lw, cs, gT, rv = wide("th"), wide("tha"), wide("lw"), wide("cs"), wide("gT"), wide("rv")
        ep, em, kk, kp, tmp = wide("ep"), wide("em"), wide("kk"), wide("kp"), wide("tmp")
        ar, bt, kt = sb("ar", [P, PAIRS, 2, P]), wide("bt"), wide("kt")
        el4 = sb("el4", [P, 2, PAIRS])
        ecm, elast = el4[:, 0], el4[:, 1]
        mats = sb("mats", [P, HEADS, 2, 2, P])
        A, Tm, TT, X1 = (sb(n, [P, HEADS, P]) for n in ("A_m", "T_m", "TT_m", "X1_m"))
        btok, ktok, rvtok = wide("btok"), wide("ktok"), wide("rvtok")
        W, U = (A[:, 4 * n:4 * n + 4].rearrange("p a (b k) -> p (a b) k", k=HD) for n in range(2))
        S, S0 = sb("S_m", [P, PAIRS, HD]), sb("S0_m", [P, PAIRS, HD])
        yT = X1[:, 0:4]
        bank = [ctx.enter_context(nc.psum_tensor(f"mix_ps{n}", [P, 512], F32)) for n in range(8)]
        wide_ps = lambda n: bank[n][:, :].rearrange("p (c j) -> p c j", c=PAIRS)
        block = ctx.enter_context(nc.Block())

        def cols(ch, i, n=1):
            return cT[:, ch:ch + n, bass.ds(i * P, P)]

        def apart(eng):
            eng.sem_inc(t["tick"], 1)

        def blk(ch, i):
            return cols(ch, i).rearrange("p a j -> p (a j)")

        def hp(h):
            return slice(HD * (h % 2), HD * (h % 2) + HD)

        @block.sync
        def _(sp):
            for dst, name in ((headones[:, :], "c_headones"), (upper[:, :, :], "c_upper"), (lower[:, :], "c_lower"),
                              (lev_in, "c_lev"), (reset[:, :], "c_reset")):
                sp.dma_start(dst, d[name]).then_inc(s["par"], 16)
            sp.dma_start(wup[0:64, :], d["w_decay_up"][0]).then_inc(s["par"], 16)
            sp.dma_start(wup[64:128, :], d["w_aaa_up"][0]).then_inc(s["par"], 16)
            sp.dma_start(gup[:, :], d["w_gate_up"][0]).then_inc(s["par"], 16)
            for dst, name in ((hw0, "w0"), (ha0, "a0"), (kkw, "k_k"), (hka, "k_a"), (lng, "ln_x_g"), (lnb, "ln_x_b")):
                sp.dma_start(dst, d[name].rearrange("l (c p) -> p (l c)", p=P), allow_slow_non_contiguous=True).then_inc(s["par"], 16)
            sp.dma_start(rkw, d["r_k"].rearrange("l (c a) k -> (a k) (l c)", a=2), allow_slow_non_contiguous=True).then_inc(s["par"], 16)
            sp.dma_start(sink[:, :], d["attn_sinks"][0:1, :].broadcast_to([P, HEADS])).then_inc(s["par"], 16)
            bv = d["c_bias"].rearrange("(b p) n -> b p n", p=P)
            sp.dma_start(bias[:, :, :], bv[0]).then_inc(s["bias"], 16)
            with sp.Fori(1, NBLK) as i:
                sp.wait_ge(s["lgt"], i * HEADS)
                sp.dma_start(bias[:, :, :], bv[bass.ds(i, 1)]).then_inc(s["bias"], 16)

        N_PAR = 16 * 16

        @block.scalar
        def _(act):
            act.wait_ge(s["par"], N_PAR)
            for g in range(KV):
                for half in range(2):
                    act.activation(kb[HD * half:HD * half + HD, g, 2 * P:BAND], cT[HD * g:HD * g + HD, CH_K, PAD:P], ACT.Copy).then_inc(s["a"], 1)
            act.wait_ge(s["init"], 3)
            act.wait_ge(s["qk"], 1)
            act.activation(vtok[0:META, 2], bank[0][0:META, 0:P], ACT.Copy).then_inc(s["vm"], 1)
            base = 4
            with act.Fori(0, NBLK) as i:
                link = Chain(act, s["a"], i * NA + base)
                act.wait_ge(s["init"], 6)
                act.wait_ge(s["v"], i * NV + 1)
                act.wait_ge(s["qk"], i * HEADS + 1)
                link.join()
                apart(act)
                act.activation(qs[:, :, :], cols(CH_Q, i, 4), ACT.Copy).then_inc(s["st"], 1)
                link(act.activation(kb[:, :, 0:P], kb[:, :, P:2 * P], ACT.Copy))
                apart(act)
                for g in range(KV):
                    for half in range(2):
                        act.activation(kb[HD * half:HD * half + HD, g, P:2 * P], cT[HD * g:HD * g + HD, CH_K, bass.ds(i * P, P)],
                                       ACT.Copy).then_inc(s["kb"], 1)
                act.activation(lora[0:64, :], cT[0:64, CH_WA, bass.ds(i * P, P)], ACT.Tanh).then_inc(s["lora"], 1)
                act.activation(lora[64:128, :], cT[64:128, CH_WA, bass.ds(i * P, P)], ACT.Copy).then_inc(s["lora"], 1)
                link(act.activation(sg[:, :], blk(CH_G, i), ACT.Tanh, scale=0.5))
                act.activation(sg[:, :], sg[:, :], ACT.Copy, scale=0.5, bias=0.5).then_inc(s["sg"], 1)
                act.activation(vas[:, :], blk(CH_V, i), ACT.Copy).then_inc(s["va"], 1)
                act.activation(rv[:, :, :], cols(CH_RV, i, 4), ACT.Copy).then_inc(s["va"], 1)
                act.wait_ge(s["mmw"], i + 1)
                for p in range(PAIRS):
                    act.activation(th[:, p], wide_ps(0)[:, p], ACT.Tanh, scale=0.5, bias=hw0[:, p:p + 1]).then_inc(s["th"], 1)
                act.wait_ge(s["mma"], i + 1)
                for p in range(PAIRS):
                    act.activation(tha[:, p], wide_ps(1)[:, p], ACT.Tanh, scale=0.5, bias=ha0[:, p:p + 1]).then_inc(s["tha"], 1)
                act.wait_ge(s["mmg"], i + 1)
                act.activation(gT[:, :, :], wide_ps(2), ACT.Copy).then_inc(s["gc"], 1)
                act.wait_ge(s["csd"], i + 1)
                act.activation(ecm, cs[:, :, P // 2 - 1], ACT.Exp).then_inc(s["exp"], 1)
                act.activation(ep[:, :, :], lw[:, :, :], ACT.Exp).then_inc(s["exp"], 1)
                act.activation(em[:, :, :], tmp[:, :, :], ACT.Exp, scale=-1.0).then_inc(s["exp"], 1)
                act.wait_ge(s["exp"], 4 * i + 1)
                act.activation(cs[:, :, :], tmp[:, :, :], ACT.Exp).then_inc(s["exp"], 1)
                act.wait_ge(s["mx"], i + 1)
                act.activation(es, dsk, ACT.Exp).then_inc(s["es"], 1)
                for h in range(HEADS):
                    act.activation(lg[:, h], lg[:, h], ACT.Exp, bias=nmx[:, h:h + 1], accum_out=ls[:, h:h + 1]).then_inc(s["pe"], 1)
                act.wait_ge(s["rn"], 2 * i + 1)
                act.activation(kp[:, :, :], kp[:, :, :], ACT.Sqrt).then_inc(s["rec"], 1)
                act.wait_ge(s["tt"], 4 * i + 2)
                act.activation(rvtok[:, :, :], wide_ps(0), ACT.Copy).then_inc(s["tok"], 1)
                link(act.activation(vtok[:, 0], vtok[:, 1], ACT.Copy))
                act.activation(vtok[:, 1], bank[1][:, 0:P], ACT.Copy).then_inc(s["tok"], 1)
                act.wait_ge(s["tt"], 4 * i + 4)
                act.activation(btok[:, :, :], wide_ps(0), ACT.Copy).then_inc(s["tok"], 1)
                act.activation(ktok[:, :, :], wide_ps(1), ACT.Copy).then_inc(s["tok"], 1)
                for l in range(6):
                    for g in range(2):
                        act.wait_ge(s["x1"], 12 * i + 2 * l + g + 1)
                        act.activation(X1[:, 4 * g:4 * g + 4], wide_ps(3 + g), ACT.Copy).then_inc(s["x1c"], 1)
                    if l >= 4:
                        n = 2 << l
                        for g in range(2):
                            act.wait_ge(s["yy"], 12 * i + 2 * l + g + 1)
                            hs = slice(4 * g, 4 * g + 4)
                            y, yt = wide_ps(5 + g), wide_ps(7 if g == 0 else 2)
                            for b in range(0, P, 2 * n):
                                if l == 4:
                                    act.activation(Tm[b + n:b + 2 * n, hs, b:b + n], y[b + n:b + 2 * n, :, b:b + n], ACT.Copy).then_inc(s["tinit"], 1)
                                act.activation(TT[b:b + n, hs, b + n:b + 2 * n], yt[b:b + n, :, b + n:b + 2 * n], ACT.Copy).then_inc(s["tinit"], 1)
                act.wait_ge(s["W"], i + 1)
                for e in range(2):
                    act.activation(W[:, e:HEADS:2], bank[5 * e][:, 0:PAIRS * HD].rearrange("p (h k) -> p h k", h=PAIRS), ACT.Copy).then_inc(s["Wc"], 1)
                act.wait_ge(s["U"], i + 1)
                act.activation(U[:, :, :], bank[1][:, :].rearrange("p (h k) -> p h k", h=HEADS), ACT.Copy).then_inc(s["Uc"], 1)
                act.wait_ge(s["Y"], i + 1)
                act.activation(yT, wide_ps(3), ACT.Copy).then_inc(s["Yc"], 1)
                for n in range(4):
                    act.wait_ge(s["tp"], 6 * i + n + 1)
                    act.activation(pT[:, n // 2, 4 * (n % 2):4 * (n % 2) + 4], wide_ps((0, 1, 2, 7)[n]), ACT.Copy).then_inc(s["tpc"], 1)
                for n in range(2):
                    act.wait_ge(s["tp"], 6 * i + 5 + n)
                    act.activation(pTm[:, 4 * n:4 * n + 4], wide_ps(3 + 1 * n)[0:META], ACT.Copy).then_inc(s["tpc"], 1)
                act.wait_ge(s["yc"], i + 1)
                act.activation(tmp[:, :, :], yT, ACT.Square).then_inc(s["sqr"], 1)
                act.wait_ge(s["vr"], i + 1)
                act.activation(th[:, :, :], th[:, :, :], ACT.Sqrt).then_inc(s["sd"], 1)
                act.wait_ge(s["O"], i + 1)
                apart(act)
                act.activation(cols(CH_Q, i, 4), wide_ps(1), ACT.Copy).then_inc(s["att"], 1)
            assert link.n == NA, link.n

        @block.vector
        def _(v):
            v.memset(kb[:, :, P:2 * P], 0.0).then_inc(s["init"], 1)
            v.memset(vtok[:, 1], 0.0).then_inc(s["init"], 1)
            v.memset(S[:, :, :], 0.0).then_inc(s["init"], 1)
            v.wait_ge(s["par"], N_PAR)
            v.tensor_scalar(par[:, 0:2], par[:, 0:2], 0.5, None, ALU.mult).then_inc(s["init"], 1)
            v.tensor_scalar(hka, hka, 0.5, None, ALU.mult).then_inc(s["init"], 1)
            v.wait_ge(s["init"], 5)
            v.tensor_copy(lev[:, :, :, :], lev_in).then_inc(s["lgt0"], 1)
            v.wait_ge(s["lgt0"], 1)
            v.tensor_scalar(omk, hka, -1.0, 1.0, ALU.mult, ALU.add).then_inc(s["init"], 1)
            v.wait_ge(s["init"], 6)
            v.sem_inc(s["v"], 1)
            with v.Fori(0, NBLK) as i:
                link = Chain(v, s["v"], i * NV + 1)

                def each(step):
                    for p in range(PAIRS):
                        link.add(step(p))
                    link.join()

                v.wait_ge(s["bias"], 16 * i + 16)
                for h in range(HEADS):
                    v.wait_ge(s["qk"], HEADS * i + h + 2)
                    v.scalar_tensor_tensor(lg[:, h], bank[3 + h % 4][:, 0:BAND], SCALE, bias[:, h], ALU.mult, ALU.add).then_inc(s["lgt"], 1)
                v.wait_ge(s["lgt"], HEADS * i + HEADS)
                link(v.tensor_reduce(mx, lg[:, :, :], AX.X, ALU.max))
                link(v.tensor_tensor(mx, mx, sink[:, :], ALU.max))
                link(v.tensor_scalar(nmx, mx, -1.0, None, ALU.mult))
                v.tensor_tensor(dsk, sink[:, :], mx, ALU.subtract).then_inc(s["mx"], 1)
                v.wait_ge(s["th"], 4 * i + 4)
                link(v.tensor_scalar(lw[:, :, :], th[:, :, :], -0.5 * DECAY, -0.5 * DECAY, ALU.mult, ALU.add))
                flat = lambda x: x[:, :, :].rearrange("p c j -> p (c j)")
                link(v.tensor_tensor_scan(flat(cs), reset[:, :], flat(lw), 0.0, ALU.mult, ALU.add))
                for p in range(PAIRS):
                    link.add(v.tensor_scalar(tmp[:, p], cs[:, p], cs[:, p, P // 2 - 1:P // 2], None, ALU.subtract))
                link.join()
                v.tensor_tensor(lw[:, :, :], tmp[:, :, :], lw[:, :, :], ALU.subtract).then_inc(s["csd"], 1)
                r, k = cols(CH_RR, i, 4), cols(CH_RK, i, 4)
                for p in range(PAIRS):
                    link.add(v.tensor_scalar(kk[:, p], blk(CH_RK + p, i), kkw[:, p:p + 1], None, ALU.mult))
                link.join()
                v.tensor_tensor(kp[:, :, :], kk[:, :, :], kk[:, :, :], ALU.mult).then_inc(s["kkr"], 1)
                v.wait_ge(s["ss"], i + 1)
                v.tensor_scalar(kp[:, :, :], wide_ps(7), 1e-24, None, ALU.max).then_inc(s["rn"], 1)
                v.wait_ge(s["rec"], i + 1)
                link(v.reciprocal(kp[:, :, :], kp[:, :, :]))
                v.tensor_tensor(kk[:, :, :], kk[:, :, :], kp[:, :, :], ALU.mult).then_inc(s["rn"], 1)
                v.wait_ge(s["rn"], 2 * i + 2)
                v.wait_ge(s["tha"], 4 * i + 4)
                for p in range(PAIRS):
                    link.add(v.tensor_scalar(kp[:, p], tha[:, p], hka[:, p:p + 1], omk[:, p:p + 1], ALU.mult, ALU.add))
                link.add(v.tensor_scalar(th[:, :, :], tha[:, :, :], 0.5, 0.5, ALU.mult, ALU.add))
                link.join()
                link(v.tensor_tensor(kp[:, :, :], kp[:, :, :], k, ALU.mult))
                v.wait_ge(s["exp"], 4 * i + 4)
                v.scalar_tensor_tensor(ar[:, :, 0], kk[:, :, :], -1.0, ep[:, :, :], ALU.mult, ALU.mult).then_inc(s["ar"], 1)
                v.tensor_tensor(ar[:, :, 1], r, cs[:, :, :], ALU.mult).then_inc(s["ar"], 1)
                link.add(v.tensor_copy(elast, cs[:, :, P - 1]))
                link(v.tensor_tensor(th[:, :, :], th[:, :, :], kk[:, :, :], ALU.mult))
                v.tensor_tensor(bt[:, :, :], th[:, :, :], em[:, :, :], ALU.mult).then_inc(s["bk"], 1)
                v.tensor_tensor(kt[:, :, :], kp[:, :, :], em[:, :, :], ALU.mult).then_inc(s["bk"], 1)
                v.tensor_tensor(S0[:, :, :], S[:, :, :], ecm.unsqueeze(2).broadcast_to([P, PAIRS, HD]), ALU.mult).then_inc(s["S0"], 1)
                for h in range(HEADS):
                    v.wait_ge(s["mmM"], HEADS * i + h + 1)
                    src = bank[3 + h % 4][:, :].rearrange("p (m c) -> p m c", m=2)
                    v.tensor_tensor(mats[:, h].rearrange("p m a j -> p m (a j)"), src,
                                    upper[:, :, :].rearrange("p a j -> p (a j)").unsqueeze(1).broadcast_to([P, 2, 2 * P]),
                                    ALU.mult).then_inc(s["msk"], 1)
                for g in range(2):
                    hs = slice(4 * g, 4 * g + 4)
                    v.wait_ge(s["mmA"], 2 * i + g + 1)
                    link.add(v.tensor_tensor(A[:, g:HEADS:2], wide_ps(7 if g == 0 else 2), lower[:, :].unsqueeze(1).broadcast_to([P, 4, P]), ALU.mult))
                    link.add(v.tensor_copy(Tm[:, hs], ident[:, :].unsqueeze(1).broadcast_to([P, 4, P])))
                    link.add(v.tensor_copy(TT[:, hs], ident[:, :].unsqueeze(1).broadcast_to([P, 4, P])))
                v.wait_ge(s["msk"], HEADS * i + HEADS)
                link.join()
                mask = lambda l, tr: lev[:, l, tr].unsqueeze(1).broadcast_to([P, 4, P])
                apart(v)
                for g in range(2):
                    hs = slice(4 * g, 4 * g + 4)
                    v.copy_predicated(Tm[:, hs], mask(0, 0), A[:, hs]).then_inc(s["tup"], 1)
                    v.copy_predicated(TT[:, hs], mask(0, 1), mats[:, hs, 0, 0]).then_inc(s["tup"], 1)
                for l in range(1, 5):
                    for g in range(2):
                        hs = slice(4 * g, 4 * g + 4)
                        v.wait_ge(s["yy"], 12 * i + 2 * (l - 1) + g + 1)
                        apart(v)
                        v.copy_predicated(Tm[:, hs], mask(l, 0), wide_ps(5 + g)).then_inc(s["tup"], 1)
                        v.copy_predicated(TT[:, hs], mask(l, 1), wide_ps(7 if g == 0 else 2)).then_inc(s["tup"], 1)
                v.wait_ge(s["pe"], HEADS * i + HEADS)
                v.wait_ge(s["es"], i + 1)
                link(v.tensor_tensor(ls, ls, es, ALU.add))
                link(v.reciprocal(ls, ls))
                v.tensor_tensor(lg[:, :, :], lg[:, :, :], ls.unsqueeze(2).broadcast_to([P, HEADS, BAND]), ALU.mult).then_inc(s["pn"], 1)
                link(v.tensor_tensor(kp[:, :, :], kp[:, :, :], r, ALU.mult))
                for p in range(PAIRS):
                    v.tensor_scalar(kp[:, p], kp[:, p], rkw[:, p:p + 1], None, ALU.mult).then_inc(s["rk"], 1)
                v.wait_ge(s["S"], i + 1)
                v.tensor_tensor(S[:, :, :], S0[:, :, :], bank[4][:, 0:PAIRS * HD].rearrange("p (c k) -> p c k", c=PAIRS), ALU.add).then_inc(s["Sn"], 1)
                v.wait_ge(s["Sn"], i + 1)
                link(v.tensor_tensor(S[:, :, :], S[:, :, :], elast.unsqueeze(2).broadcast_to([P, PAIRS, HD]), ALU.mult))
                v.wait_ge(s["mean"], i + 1)
                v.scalar_tensor_tensor(yT, wide_ps(5), -1.0 / HD, yT, ALU.mult, ALU.add).then_inc(s["yc"], 1)
                v.wait_ge(s["var"], i + 1)
                v.tensor_scalar(th[:, :, :], wide_ps(6), 1.0 / HD, LN_EPS, ALU.mult, ALU.add).then_inc(s["vr"], 1)
                v.wait_ge(s["bon"], i + 1)
                link(v.tensor_tensor(lw[:, :, :], rv[:, :, :], wide_ps(5), ALU.mult))
                v.wait_ge(s["sd"], i + 1)
                link(v.reciprocal(th[:, :, :], th[:, :, :]))
                link(v.tensor_tensor(yT, yT, th[:, :, :], ALU.mult))
                each(lambda p: v.tensor_scalar(yT[:, p], yT[:, p], lng[:, p:p + 1], lnb[:, p:p + 1], ALU.mult, ALU.add))
                link(v.tensor_tensor(yT, yT, lw[:, :, :], ALU.add))
                link(v.tensor_tensor(cols(CH_RR, i, 4), yT, gT[:, :, :], ALU.mult))
            assert link.n == NV, link.n

        @block.tensor
        def _(pe):
            pe.wait_ge(s["par"], N_PAR)
            pe.transpose(bank[0][0:META, 0:P], cT[:, CH_V, PAD:P], ident[:, :]).then_inc(s["qk"], 1)
            with pe.Fori(0, NBLK) as i:
                pe.wait_ge(s["vm"], 1)
                pe.wait_ge(s["lora"], 2 * i + 2)
                for p in range(PAIRS):
                    last = pe.matmul(wide_ps(0)[:, p], wup[0:64, p * P:(p + 1) * P], lora[0:64, :], start=True, stop=True)
                last.then_inc(s["mmw"], 1)
                for p in range(PAIRS):
                    last = pe.matmul(wide_ps(1)[:, p], wup[64:128, p * P:(p + 1) * P], lora[64:128, :], start=True, stop=True)
                last.then_inc(s["mma"], 1)
                pe.wait_ge(s["sg"], i + 1)
                for p in range(PAIRS):
                    last = pe.matmul(wide_ps(2)[:, p], gup[:, p * P:(p + 1) * P], sg[:, :], start=True, stop=True)
                last.then_inc(s["mmg"], 1)
                pe.wait_ge(s["st"], i + 1)
                pe.wait_ge(s["kb"], 4 * i + 4)
                for h in range(HEADS):
                    if h >= 4:
                        pe.wait_ge(s["lgt"], HEADS * i + h - 3)
                    pe.matmul(bank[3 + h % 4][:, 0:BAND], qs[hp(h), h // 2, :], kb[hp(h), h // 4, :], start=True, stop=True).then_inc(s["qk"], 1)
                pe.wait_ge(s["kkr"], i + 1)
                pe.matmul(bank[7][:, :], headones[:, :], kp[:, :, :].rearrange("p c j -> p (c j)"), start=True, stop=True).then_inc(s["ss"], 1)
                pe.wait_ge(s["va"], 2 * i + 2)
                pe.wait_ge(s["th"], 4 * i + 4)
                for p in range(PAIRS):
                    last = pe.transpose(wide_ps(0)[:, p], rv[:, p], ident[:, :])
                last.then_inc(s["tt"], 1)
                pe.wait_ge(s["tha"], 4 * i + 4)
                pe.transpose(bank[1][:, 0:P], vas[:, :], ident[:, :]).then_inc(s["tt"], 1)
                pe.wait_ge(s["ar"], 2 * i + 2)
                pe.wait_ge(s["bk"], 2 * i + 2)
                for h in range(HEADS):
                    p, q = h // 2, hp(h)
                    if h < 4:
                        pe.wait_ge(s["lgt"], HEADS * i + 5 + h)
                    else:
                        pe.wait_ge(s["msk"], HEADS * i + h - 3)
                    both = ar[q, p].rearrange("k a j -> k (a j)")
                    pe.matmul(bank[3 + h % 4][:, 0:2 * P], bt[q, p], both, start=True, stop=True)
                    pe.matmul(bank[3 + h % 4][:, 2 * P:4 * P], kt[q, p], both, start=True, stop=True).then_inc(s["mmM"], 1)
                pe.wait_ge(s["rn"], 2 * i + 2)
                pe.wait_ge(s["gc"], i + 1)
                apart(pe)
                for g in range(2):
                    for h in range(g, HEADS, 2):
                        last = pe.matmul(wide_ps(7 if g == 0 else 2)[:, h // 2], ar[hp(h), h // 2, 0], bt[hp(h), h // 2], start=True, stop=True)
                    last.then_inc(s["mmA"], 1)
                pe.wait_ge(s["tok"], 4 * i + 2)
                for n, src in enumerate((bt, kt)):
                    for p in range(PAIRS):
                        last = pe.transpose(wide_ps(n)[:, p], src[:, p], ident[:, :])
                    last.then_inc(s["tt"], 1)
                pe.wait_ge(s["msk"], HEADS * i + HEADS)
                for l in range(6):
                    for g in range(2):
                        if l < 5:
                            pe.wait_ge(s["tup"], 20 * i + 4 * l + 2 * g + 2)
                        else:
                            pe.wait_ge(s["tinit"], 10 * i + 4 * g + 4)
                        for h in range(4 * g, 4 * g + 4):
                            last = pe.matmul(wide_ps(3 + g)[:, h % 4], mats[:, h, 0, 0], Tm[:, h], start=True, stop=True)
                        last.then_inc(s["x1"], 1)
                    for g in range(2):
                        pe.wait_ge(s["x1c"], 12 * i + 2 * l + g + 1)
                        for h in range(4 * g, 4 * g + 4) if l < 5 else ():
                            pe.matmul(wide_ps(5 + g)[:, h % 4], TT[:, h], X1[:, h], start=True, stop=True)
                        for h in range(4 * g, 4 * g + 4):
                            last = pe.matmul(wide_ps(7 if g == 0 else 2)[:, h % 4], X1[:, h], TT[:, h], start=True, stop=True)
                        last.then_inc(s["yy"], 1)
                pe.wait_ge(s["tok"], 4 * i + 4)
                pe.wait_ge(s["S0"], i + 1)
                for h in range(HEADS):
                    wo = bank[5 * (h % 2)][:, HD * (h // 2):HD * (h // 2) + HD]
                    v_h = rvtok[:, h // 2, hp(h)]
                    pe.matmul(wo, ar[hp(h), h // 2, 0], S0[hp(h), h // 2], start=True, stop=False)
                    last = pe.matmul(wo, mats[:, h, 1, 0], v_h, start=False, stop=True)
                last.then_inc(s["W"], 1)
                pe.wait_ge(s["Wc"], 2 * i + 2)
                pe.wait_ge(s["tinit"], 10 * i + 10)
                for h in range(HEADS):
                    last = pe.matmul(bank[1][:, HD * h:HD * h + HD], TT[:, h], W[:, h], start=True, stop=True)
                last.then_inc(s["U"], 1)
                pe.wait_ge(s["Uc"], i + 1)
                apart(pe)
                for h in range(HEADS):
                    v_h = rvtok[:, h // 2, hp(h)]
                    o = wide_ps(3)[hp(h), h // 2]
                    pe.matmul(o, S0[hp(h), h // 2], ar[hp(h), h // 2, 1], start=True, stop=False)
                    pe.matmul(o, U[:, h], mats[:, h, 0, 1], start=False, stop=False)
                    last = pe.matmul(o, v_h, mats[:, h, 1, 1], start=False, stop=True)
                last.then_inc(s["Y"], 1)
                for h in range(HEADS):
                    o = bank[4][hp(h), HD * (h // 2):HD * (h // 2) + HD]
                    pe.matmul(o, btok[:, h // 2, hp(h)], U[:, h], start=True, stop=False)
                    last = pe.matmul(o, ktok[:, h // 2, hp(h)], rvtok[:, h // 2, hp(h)], start=False, stop=True)
                last.then_inc(s["S"], 1)
                pe.wait_ge(s["Yc"], i + 1)
                pe.matmul(bank[5][:, :], headones[:, :], yT.rearrange("p c j -> p (c j)"), start=True, stop=True).then_inc(s["mean"], 1)
                pe.wait_ge(s["pn"], i + 1)
                for n in range(4):
                    part, g = n // 2, n % 2
                    for h in range(4 * g, 4 * g + 4):
                        last = pe.transpose(wide_ps((0, 1, 2, 7)[n])[:, h % 4], lg[:, h, part * P:(part + 1) * P], ident[:, :])
                    last.then_inc(s["tp"], 1)
                for g in range(2):
                    if g == 1:
                        pe.wait_ge(s["Sn"], i + 1)
                    for h in range(4 * g, 4 * g + 4):
                        last = pe.transpose(wide_ps(3 + g)[0:META, h % 4], lg[:, h, 2 * P:BAND], ident[:, :])
                    last.then_inc(s["tp"], 1)
                pe.wait_ge(s["sqr"], i + 1)
                pe.matmul(bank[6][:, :], headones[:, :], tmp[:, :, :].rearrange("p c j -> p (c j)"), start=True, stop=True).then_inc(s["var"], 1)
                pe.wait_ge(s["rk"], 4 * i + 4)
                pe.matmul(bank[5][:, :], headones[:, :], kp[:, :, :].rearrange("p c j -> p (c j)"), start=True, stop=True).then_inc(s["bon"], 1)
                pe.wait_ge(s["tpc"], 6 * i + 6)
                for g in range(KV):
                    for e in range(2):
                        o = wide_ps(1)[HD * e:HD * e + HD, 2 * g:2 * g + 2]
                        hs = slice(4 * g + e, 4 * g + 4, 2)
                        vc = slice(HD * g, HD * g + HD)
                        pe.matmul(o, vtok[:, 0, vc], pT[:, 0, hs], start=True, stop=False)
                        pe.matmul(o, vtok[:, 1, vc], pT[:, 1, hs], start=False, stop=False)
                        last = pe.matmul(o, vtok[0:META, 2, vc], pTm[:, hs], start=False, stop=True)
                last.then_inc(s["O"], 1)


def merge(nc, sems, t, d):
    ld0, ld1, xld, mm, th, sm, dn = sems("g_ld0", "g_ld1", "g_xld", "g_mm", "g_th", "g_sm", "g_dn")
    HALF = SEQ // 2
    CPL = 2
    UNITS = 2 * CPL * 2
    STEPS = KD // (2 * CPL)
    K2 = RD // P
    with ExitStack() as ctx:
        sb = lambda n, s, dt=F32: ctx.enter_context(nc.sbuf_tensor(n, s, dt))
        xnT = sb("xnT2", [P, KD, SEQ])
        w = sb("w_merge", [P, 2, 2 * KD + 2 * K2, CPL * P])
        g2 = sb("gates", [P, 2, 2, HALF])
        m2 = sb("gated", [P, 2, HALF])
        bank = [ctx.enter_context(nc.psum_tensor(f"mrg_ps{n}", [P, 4, 512], F32)) for n in range(2)]
        cT = t["cT"]
        gates = d["w_in"].rearrange("l (c p) n -> p (l c) n", p=P)
        woa = d["w_o_attn"].rearrange("l (c p) n -> p (l c) n", p=P)
        wor = d["w_o_rwkv"].rearrange("l (c p) n -> p (l c) n", p=P)
        block = ctx.enter_context(nc.Block())

        @block.sync
        def _(sp):
            def load(half, sem, j):
                c = bass.ds(j * P, CPL * P)
                sp.dma_start(w[:, half, 0:KD], gates[:, :, bass.ds(GATE0 + j * P, CPL * P)]).then_inc(sem, 16)
                sp.dma_start(w[:, half, KD:2 * KD], gates[:, :, bass.ds(GATE0 + D + j * P, CPL * P)]).then_inc(sem, 16)
                sp.dma_start(w[:, half, 2 * KD:2 * KD + K2], woa[:, :, c]).then_inc(sem, 16)
                sp.dma_start(w[:, half, 2 * KD + K2:], wor[:, :, c]).then_inc(sem, 16)

            load(0, ld0, 0)
            sp.dma_start(xnT[:, :, :], d["xn_spill"].rearrange("p (c j) -> p c j", c=KD)).then_inc(xld, 16)
            load(1, ld1, CPL)
            with sp.Fori(1, STEPS) as i:
                for half, sem in enumerate((ld0, ld1)):
                    sp.wait_ge(mm, (i - 1) * UNITS + (half + 1) * UNITS // 2)
                    load(half, sem, i * (2 * CPL) + half * CPL)

        @block.tensor
        def _(pe):
            pe.wait_ge(xld, 16)
            pe.sem_inc(dn, 2)
            with pe.Fori(0, STEPS) as i:
                for n in range(UNITS):
                    half, c, part = n // (2 * CPL), (n // 2) % CPL, n % 2
                    if n % (2 * CPL) == 0:
                        pe.wait_ge(ld1 if half else ld0, (i + 1) * 64)
                    pe.wait_ge(dn, i * UNITS + n + 1)
                    wc = slice(c * P, (c + 1) * P)
                    rows = slice(part * HALF, (part + 1) * HALF)
                    real = slice(P + part * HALF, P + (part + 1) * HALF)
                    ps = bank[n % 2]
                    for b in range(2):
                        for k in range(KD):
                            pe.matmul(ps[:, b], w[:, half, b * KD + k, wc], xnT[:, k, rows], start=(k == 0), stop=(k == KD - 1))
                    for b, ch in enumerate((CH_Q, CH_RR)):
                        for k in range(K2):
                            last = pe.matmul(ps[:, 2 + b], w[:, half, 2 * KD + b * K2 + k, wc], cT[:, ch + k, real],
                                             start=(k == 0), stop=(k == K2 - 1))
                    last.then_inc(mm, 1)

        @block.scalar
        def _(act):
            with act.Fori(0, STEPS) as i:
                for n in range(UNITS):
                    act.wait_ge(mm, i * UNITS + n + 1)
                    act.wait_ge(dn, i * UNITS + n + 1)
                    act.activation(g2[:, n % 2], bank[n % 2][:, 0:2], ACT.Tanh, scale=0.5).then_inc(th, 1)

        @block.vector
        def _(v):
            with v.Fori(0, STEPS) as i:
                for n in range(UNITS):
                    c, part = n // 2, n % 2
                    v.wait_ge(th, i * UNITS + n + 1)
                    v.wait_ge(dn, i * UNITS + n + 2)
                    for b in range(2):
                        v.scalar_tensor_tensor(m2[:, b], g2[:, n % 2, b], 1.0, bank[n % 2][:, 2 + b], ALU.add, ALU.mult).then_inc(sm, 1)
                    v.wait_ge(sm, (i * UNITS + n) * 2 + 2)
                    out = cT[:, bass.ds(CH_MIX + i * (2 * CPL) + c, 1), P + part * HALF:P + (part + 1) * HALF]
                    v.tensor_tensor(out.rearrange("p a j -> p (a j)"), m2[:, 0], m2[:, 1], ALU.add).then_inc(dn, 1)


def route(nc, sems, t, d):
    names = "r_ld r_x0 r_x1 r_ms r_mm r_h r_sq r_m r_sd r_xn r_st0 r_st1 r_tp r_xt r_lg r_e r_ex r_oh r_rk r_v"
    ld, x0, x1, msr, mm, hd, sqd, msd, sdd, xnd, st0, st1, tp, xt, lgd, eg, ex, oh, rk, own = sems(*names.split())
    NV = t["route_count"]
    tick = t["tick"]
    with ExitStack() as ctx:
        sb = lambda n, s, dt=F32: ctx.enter_context(nc.sbuf_tensor(n, s, dt))
        ident, cT = t["ident"], t["cT"]
        wout = sb("wout", [P, KD, D])
        wr = sb("w_router", [P, KD, NG + E])
        br = sb("b_router", [P, NG + E])
        gf = sb("g_ffn", [P, D])
        iota, before, ones = sb("iota", [P, E]), sb("before", [P, P]), sb("ones", [P, P])
        ms = sb("ms", [P, 2, KD, P])
        xb = sb("xb", [P, 2, D])
        h1 = sb("h1", [P, 2, D])
        xn = sb("xn2", [P, 2, D])
        sq = sb("sq2", [P, D])
        x2T = sb("x2T", [P, KD, P])
        sc = sb("sc", [P, 16])
        ss, rs, m0, sg, e2, dv, exv, g1, gidx, ones1 = (sc[:, n:n + 1] for n in range(10))
        gl8, el, m8 = sb("gl8", [P, 8]), sb("el", [P, NG, EG]), sb("m8", [P, 8])
        i8 = sb("i8", [P, 8], U32)
        pen, junk = sb("pen", [P, NG]), sb("junk", [P, 8])
        o12, om, pr = sb("o12", [P, TOPK, E]), sb("om", [P, E]), sb("pr", [P, TOPK, E])
        R, carry = sb("R", [P, E]), t["carry"]
        ps_h = [ctx.enter_context(nc.psum_tensor(f"h_ps{n}", [P, D], F32)) for n in range(2)]
        ps_t = ctx.enter_context(nc.psum_tensor("t_ps", [P, KD, P], F32))
        ps_l = ctx.enter_context(nc.psum_tensor("l_ps", [P, 512], F32))
        ps_r = ctx.enter_context(nc.psum_tensor("r_ps", [P, 512], F32))
        xv = d["x"].rearrange("b (n p) d -> (b n) p d", p=P)
        h1v, xn2v = (d[n].rearrange("(n p) d -> n p d", p=P) for n in ("h1_rows", "xn2_rows"))
        block = ctx.enter_context(nc.Block())
        STEPS = NB // 2

        @block.sync
        def _(sp):
            sp.dma_start(wout[:, :, :], d["w_out"].rearrange("l (c p) n -> p (l c) n", p=P)).then_inc(ld, 16)
            sp.dma_start(wr[:, :, 0:NG], d["w_grp"].rearrange("l (c p) n -> p (l c) n", p=P)).then_inc(ld, 16)
            sp.dma_start(wr[:, :, NG:], d["w_exp"].rearrange("l (c p) n -> p (l c) n", p=P)).then_inc(ld, 16)
            sp.dma_start(br[:, 0:NG], d["b_grp"][0:1, :].broadcast_to([P, NG])).then_inc(ld, 16)
            sp.dma_start(br[:, NG:], d["b_exp"][0:1, :].broadcast_to([P, E])).then_inc(ld, 16)
            sp.dma_start(gf[:, :], d["norm_ffn_g"][0:1, :].broadcast_to([P, D])).then_inc(ld, 16)
            sp.dma_start(iota[:, :], d["c_iota"]).then_inc(ld, 16)
            sp.dma_start(before[:, :], d["c_upper"][:, 0]).then_inc(ld, 16)
            with sp.Fori(0, STEPS) as i:
                for u, (sx, st) in enumerate(((x0, st0), (x1, st1))):
                    sp.wait_ge(hd, 2 * i + u + 1)
                    sp.dma_start(xb[:, u], xv[bass.ds(2 * i + u, 1)]).then_inc(sx, 16)
                for u, st in enumerate((st0, st1)):
                    sp.wait_ge(hd, 2 * i + u + 3)
                    sp.dma_start(h1v[bass.ds(2 * i + u, 1)], h1[:, u]).then_inc(st, 16)
                    sp.wait_ge(xnd, 2 * i + u + 1)
                    sp.dma_start(xn2v[bass.ds(2 * i + u, 1)], xn[:, u]).then_inc(st, 16)
            sp.wait_ge(st0, 32 * STEPS + 32)
            sp.wait_ge(st1, 32 * STEPS + 32)

        @block.scalar
        def _(act):
            act.sem_inc(mm, 2)
            with act.Fori(0, STEPS) as i:
                for u in range(2):
                    n = 2 * i + u
                    act.wait_ge(mm, n + 1)
                    act.sem_inc(tick, 1)
                    act.activation(ms[:, u], cT[:, CH_MIX:CH_MIX + KD, bass.ds(P + n * P, P)], ACT.Copy).then_inc(msr, 1)
                    act.wait_ge(hd, n + 3)
                    act.activation(sq[:, :], h1[:, u], ACT.Square, accum_out=ss).then_inc(sqd, 1)
                    act.wait_ge(msd, n + 1)
                    act.activation(rs, ss, ACT.Sqrt).then_inc(sdd, 1)
                    act.wait_ge(tp, n + 1)
                    act.wait_ge(lgd, n + 1)
                    act.activation(x2T[:, :, :], ps_t[:, :, :], ACT.Copy).then_inc(xt, 1)
                    act.wait_ge(eg, n + 1)
                    act.activation(junk[:, :], gl8[:, :], ACT.Exp, bias=m0, accum_out=sg).then_inc(ex, 1)
                    act.activation(exv, dv, ACT.Exp).then_inc(ex, 1)

        @block.vector
        def _(v):
            v.memset(gl8[:, :], NEG).then_inc(own, 1)
            v.memset(ones[:, :], 1.0).then_inc(own, 1)
            v.memset(carry[:, :], 0.0).then_inc(own, 1)
            v.sem_inc(hd, 2)
            v.sem_inc(sdd, 1)
            v.sem_inc(lgd, 1)
            v.wait_ge(ld, 8 * 16)
            with v.Fori(0, STEPS) as i:
                link = Chain(v, own, i * NV + 3)
                for u in range(2):
                    n = 2 * i + u
                    v.wait_ge(x1 if u else x0, 16 * i + 16)
                    v.wait_ge(mm, n + 3)
                    v.wait_ge(st1 if u else st0, 32 * i + 32)
                    for hf in range(2):
                        c = slice(hf * 512, hf * 512 + 512)
                        link.add(v.scalar_tensor_tensor(h1[:, u, c], ps_h[u][:, c], 0.5, xb[:, u, c], ALU.mult, ALU.add))
                    link.join()
                    v.sem_inc(hd, 1)
                    v.wait_ge(sqd, n + 1)
                    v.tensor_scalar(ss, ss, 1.0 / D, EPS, ALU.mult, ALU.add).then_inc(msd, 1)
                    v.wait_ge(sdd, n + 2)
                    link(v.reciprocal(rs, rs))
                    v.scalar_tensor_tensor(xn[:, u], h1[:, u], rs, gf[:, :], ALU.mult, ALU.mult).then_inc(xnd, 1)
                    v.wait_ge(lgd, n + 2)
                    link.add(v.tensor_tensor(gl8[:, 0:NG], ps_l[:, 0:NG], br[:, 0:NG], ALU.add))
                    link(v.tensor_tensor(el[:, :, :].rearrange("p g e -> p (g e)"), ps_l[:, NG:NG + E], br[:, NG:], ALU.add))
                    v.sem_inc(tick, 1)
                    link(v.max(m8[:, :], gl8[:, :]))
                    v.sem_inc(tick, 1)
                    link.add(v.max_index(i8[:, :], m8[:, :], gl8[:, :]))
                    link(v.tensor_scalar(m0, m8[:, 0:1], -1.0, None, ALU.mult))
                    link(v.tensor_copy(gidx, i8[:, 0:1]))
                    link(v.tensor_scalar(pen[:, :], iota[:, 0:NG], gidx, NEG, ALU.not_equal, ALU.mult))
                    link(v.tensor_tensor(el[:, :, :], el[:, :, :], pen[:, :].unsqueeze(2).broadcast_to([P, NG, EG]), ALU.add))
                    flat = el[:, :, :].rearrange("p g e -> p (g e)")
                    v.sem_inc(tick, 1)
                    link(v.max(m8[:, :], flat))
                    v.sem_inc(tick, 1)
                    link.add(v.max_index(i8[:, :], m8[:, :], flat))
                    link(v.tensor_tensor(dv, m8[:, 1:2], m8[:, 0:1], ALU.subtract))
                    v.sem_inc(eg, 1)
                    e_n = t["eids"][:, bass.ds(n, 1), :].rearrange("p a k -> p (a k)")
                    link(v.tensor_copy(e_n, i8[:, 0:TOPK]))
                    for k in range(TOPK):
                        link.add(v.tensor_scalar(o12[:, k], iota[:, :], t["eids"][:, bass.ds(n, 1), k], None, ALU.is_equal))
                    link.join()
                    v.tensor_tensor(om[:, :], o12[:, 0], o12[:, 1], ALU.add).then_inc(oh, 1)
                    v.wait_ge(ex, 2 * n + 2)
                    link(v.tensor_scalar(g1, exv, 1.0, None, ALU.add))
                    link(v.tensor_tensor(g1, g1, sg, ALU.mult))
                    link(v.reciprocal(g1, g1))
                    link.add(v.tensor_scalar(t["wts"][:, bass.ds(n, 1), 0], g1, 0.5, None, ALU.mult))
                    link(v.tensor_scalar(t["wts"][:, bass.ds(n, 1), 1], g1, exv, 0.5, ALU.mult, ALU.mult))
                    v.wait_ge(rk, n + 1)
                    link(v.tensor_tensor(R[:, :], ps_r[:, 0:E], carry[:, :], ALU.add))
                    link.add(v.tensor_tensor(pr[:, :, :], o12[:, :, :], R[:, :].unsqueeze(1).broadcast_to([P, TOPK, E]), ALU.mult))
                    link(v.tensor_tensor(carry[:, :], carry[:, :], ps_r[:, E:2 * E], ALU.add))
                    link(v.tensor_reduce(t["ranks"][:, bass.ds(n, 1), :].rearrange("p a k -> p (a k)"), pr[:, :, :], AX.X, ALU.add))
            assert link.n == NV, link.n

        @block.gpsimd
        def _(pool):
            pool.sem_inc(st0, 32)
            pool.sem_inc(st1, 32)

        @block.tensor
        def _(pe):
            pe.wait_ge(ld, 8 * 16)
            pe.wait_ge(own, 3)
            with pe.Fori(0, STEPS) as i:
                for u in range(2):
                    n = 2 * i + u
                    pe.wait_ge(msr, n + 1)
                    pe.wait_ge(hd, n + 1)
                    for hf in range(2):
                        for k in range(KD):
                            last = pe.matmul(ps_h[u][:, hf * 512:hf * 512 + 512], ms[:, u, k], wout[:, k, hf * 512:hf * 512 + 512],
                                             start=(k == 0), stop=(k == KD - 1))
                    last.then_inc(mm, 1)
                    pe.wait_ge(xnd, n + 1)
                    for k in range(KD):
                        last = pe.transpose(ps_t[:, k], xn[:, u, k * P:(k + 1) * P], ident[:, :])
                    last.then_inc(tp, 1)
                    pe.wait_ge(xt, n + 1)
                    for k in range(KD):
                        last = pe.matmul(ps_l[:, 0:NG + E], x2T[:, k], wr[:, k], start=(k == 0), stop=(k == KD - 1))
                    last.then_inc(lgd, 1)
                    pe.wait_ge(oh, n + 1)
                    pe.matmul(ps_r[:, 0:E], before[:, :], om[:, :], start=True, stop=True)
                    pe.matmul(ps_r[:, E:2 * E], ones[:, :], om[:, :], start=True, stop=True).then_inc(rk, 1)


def table(nc, sems, t, d):
    ld, own, zs, sc, sl = sems("t_ld", "t_own", "t_zs", "t_sc", "t_sl")
    R2 = NB * TOPK
    with ExitStack() as ctx:
        sb = lambda n, s, dt=F32: ctx.enter_context(nc.sbuf_tensor(n, s, dt))
        iota, over, blockno = sb("iota_t", [P, E]), sb("over", [P, NB]), sb("blockno", [P, BLOCKS])
        tokno = sb("tokno", [P, NB], I32)
        zero = sb("zero", [P, BLOCKS], I32)
        cmp, nblk, end, start = sb("cmp", [P, E, NB]), sb("nblk", [P, E]), sb("end", [P, E]), sb("start", [P, E])
        one = sb("one_t", [P, E])
        oh, rb, pos = sb("oh_t", [P, R2, E]), sb("rb", [P, R2]), sb("pos", [P, R2])
        rc = sb("rc", [P, R2, NB])
        sidx = sb("sidx", [P, R2], I32)
        be, bc = sb("be", [1, BLOCKS]), sb("bc", [1, BLOCKS, E])
        block = ctx.enter_context(nc.Block())
        eids, ranks = (t[n][:, :, :].rearrange("p n k -> p (n k)") for n in ("eids", "ranks"))

        @block.sync
        def _(sp):
            sp.dma_start(iota[:, :], d["c_iota"]).then_inc(ld, 16)
            sp.dma_start(over[:, :], d["c_over"]).then_inc(ld, 16)
            sp.dma_start(blockno[:, :], d["c_blockno"]).then_inc(ld, 16)
            sp.dma_start(tokno[:, :], d["c_tokno"]).then_inc(ld, 16)
            sp.wait_ge(own, 1)
            sp.dma_start(d["slot_tok"].rearrange("(p b) a -> p (b a)", p=P), zero[:, :]).then_inc(zs, 16)
            sp.wait_ge(sc, 16 * R2)
            sp.dma_start(t["slots"][:, 0:BLOCKS], d["slot_tok"].rearrange("(p b) a -> p (b a)", p=P)).then_inc(sl, 16)
            sp.wait_ge(sl, 16)

        @block.vector
        def _(v):
            link = Chain(v, own)
            link.add(v.memset(zero[:, :], 0))
            link.add(v.memset(t["slots"][:, BLOCKS:], 0))
            link(v.memset(one[:, :], 1.0))
            v.wait_ge(ld, 64)
            wide = lambda x, n: x.unsqueeze(2).broadcast_to([P, x.shape[1], n])
            rows = lambda x, n: x.unsqueeze(1).broadcast_to([P, n, x.shape[1]])
            link(v.tensor_tensor(cmp[:, :, :], wide(t["carry"][:, :], NB), rows(over[:, :], E), ALU.is_gt))
            link(v.tensor_reduce(nblk[:, :], cmp[:, :, :], AX.X, ALU.add))
            link(v.tensor_tensor_scan(end[:, :], one[:, :], nblk[:, :], 0.0, ALU.mult, ALU.add))
            link(v.tensor_tensor(start[:, :], end[:, :], nblk[:, :], ALU.subtract))
            link(v.tensor_tensor(bc[:, :, :], end[0:1, :].unsqueeze(1).broadcast_to([1, BLOCKS, E]),
                                 blockno[0:1, :].unsqueeze(2).broadcast_to([1, BLOCKS, E]), ALU.is_le))
            link(v.tensor_reduce(be[:, :], bc[:, :, :], AX.X, ALU.add))
            link(v.tensor_scalar(t["bexp"][:, :], be[:, :], float(E - 1), None, ALU.min))
            link(v.tensor_tensor(oh[:, :, :], wide(eids, E), rows(iota[:, :], R2), ALU.is_equal))
            link(v.tensor_tensor(oh[:, :, :], oh[:, :, :], rows(start[:, :], R2), ALU.mult))
            link(v.tensor_reduce(rb[:, :], oh[:, :, :], AX.X, ALU.add))
            link(v.tensor_tensor(rc[:, :, :], wide(ranks, NB), rows(over[:, :], R2), ALU.is_ge))
            link(v.tensor_reduce(pos[:, :], rc[:, :, :], AX.X, ALU.add))
            link(v.tensor_scalar(pos[:, :], pos[:, :], 1.0, None, ALU.subtract))
            link(v.tensor_tensor(rb[:, :], rb[:, :], pos[:, :], ALU.add))
            link(v.scalar_tensor_tensor(pos[:, :], pos[:, :], -float(P), ranks, ALU.mult, ALU.add))
            link.add(v.scalar_tensor_tensor(sidx[:, :], pos[:, :], float(BLOCKS), rb[:, :], ALU.mult, ALU.add))
            link(v.scalar_tensor_tensor(t["ydest"][:, :], rb[:, :], float(P), pos[:, :], ALU.mult, ALU.add))
            t["table_own"] = link.n

        @block.gpsimd
        def _(pool):
            pool.wait_ge(own, t["table_own"])
            pool.wait_ge(zs, 16)
            for n in range(R2):
                pool.indirect_dma_start(d["slot_tok"], bass.IndirectOffsetOnAxis(sidx[:, n:n + 1], 0),
                                        tokno[:, n // TOPK:n // TOPK + 1], None).then_inc(sc, 16)


def experts(nc, sems, t, d):
    DEPTH_W = 4
    wgu, wdn, xg, yst = ([sems(f"e_{k}{u}")[0] for u in range(DEPTH_W)] for k in ("wgu", "wdn", "xg", "yst"))
    ix, tp, xt, mm, th, hm, ht, hc, dm, ye, own = sems(*(f"e_{k}" for k in "ix tp xt mm th hm ht hc dm ye own".split()))
    FK = F // P
    tick = t["tick"]
    with ExitStack() as ctx:
        sb = lambda n, s, dt=F32: ctx.enter_context(nc.sbuf_tensor(n, s, dt))
        ident = t["ident"]
        w = sb("w_gu", [P, DEPTH_W, 2, KD, F])
        wd = sb("w_dn", [P, DEPTH_W, FK, D])
        idx = [sb(f"idx{u}", [P, 1], I32) for u in range(DEPTH_W)]
        xr = [sb(f"xr{u}", [P, D]) for u in range(DEPTH_W)]
        xT = sb("xT", [P, 2, KD, P])
        sg, hmid = sb("sg_e", [P, 2, F]), sb("hmid", [P, 2, F])
        hT = sb("hT", [P, 2, FK, P])
        y = sb("y", [P, 2, D])
        ps_x = ctx.enter_context(nc.psum_tensor("x_ps", [P, KD, P], F32))
        ps_h = ctx.enter_context(nc.psum_tensor("hh_ps", [P, 2, 2, F], F32))
        ps_t = ctx.enter_context(nc.psum_tensor("ht_ps", [P, 512], F32))
        ps_y = ctx.enter_context(nc.psum_tensor("y_ps", [P, D], F32))
        eg, eu = (d[n].rearrange("l e (p c) f -> (l e) p (c f)", p=P) for n in ("e_gate", "e_up"))
        ed = d["e_down"].rearrange("l e (p c) n -> (l e) p (c n)", p=P)
        yv = d["y_rows"].rearrange("(n p) d -> n p d", p=P)
        block = ctx.enter_context(nc.Block())

        def turns(n):
            return n // DEPTH_W + 1

        @block.sync
        def _(sp):
            def load(e, u):
                sp.dma_start(w[:, u, 0].rearrange("p c f -> p (c f)"), eg[bass.ds(e, 1)]).then_inc(wgu[u], 16)
                sp.dma_start(w[:, u, 1].rearrange("p c f -> p (c f)"), eu[bass.ds(e, 1)]).then_inc(wgu[u], 16)
                sp.dma_start(wd[:, u].rearrange("p c n -> p (c n)"), ed[bass.ds(e, 1)]).then_inc(wdn[u], 16)

            def store(n, u):
                sp.wait_ge(ye, 2 * n + 3)
                sp.dma_start(yv[bass.ds(n, 1)], y[:, u % 2]).then_inc(yst[u % 2], 16)

            sp.sem_inc(yst[0], 16)
            sp.sem_inc(yst[1], 16)
            for u in range(DEPTH_W):
                load(sp.value_load(t["bexp"][0:1, u:u + 1], min_val=0, max_val=E - 1), u)
            with sp.Fori(1, BLOCKS // DEPTH_W) as i:
                for u in range(DEPTH_W):
                    n = i * DEPTH_W + u
                    e = sp.value_load(t["bexp"][0:1, bass.ds(n, 1)], min_val=0, max_val=E - 1)
                    sp.wait_ge(dm, n - 1)
                    load(e, u)
                    store(n - DEPTH_W, u)
            for n in range(BLOCKS - DEPTH_W, BLOCKS):
                store(n, n % DEPTH_W)
            for k in range(2):
                sp.wait_ge(yst[k], 16 * (BLOCKS // 2 + 1))

        @block.gpsimd
        def _(pool):
            for u in range(DEPTH_W):
                pool.tensor_copy(idx[u][:, :], t["slots"][:, u:u + 1]).then_inc(ix, 1)
            with pool.Fori(0, BLOCKS // DEPTH_W) as i:
                for u in range(DEPTH_W):
                    n = i * DEPTH_W + u
                    pool.wait_ge(ix, n + 1)
                    pool.wait_ge(tp, n + 1)
                    pool.sem_inc(tick, 1)
                    pool.indirect_dma_start(xr[u][:, :], None, d["xn2_rows"], bass.IndirectOffsetOnAxis(idx[u][:, :], 0)).then_inc(xg[u], 16)
                    pool.wait_ge(xg[u], 16 * i + 16)
                    nxt = t["slots"][:, bass.ds(n + DEPTH_W, 1)]
                    pool.tensor_copy(idx[u][:, :], nxt).then_inc(ix, 1)

        @block.tensor
        def _(pe):
            pe.sem_inc(tp, DEPTH_W)
            pe.sem_inc(dm, 2)
            pe.sem_inc(xt, 2)

            def turn(n, u, i):
                pe.wait_ge(xg[u], i)
                pe.wait_ge(xt, 2 * n + 2)
                for k in range(KD):
                    last = pe.transpose(ps_x[:, k], xr[u][:, k:D:KD], ident[:, :])
                last.then_inc(tp, 1)

            def up(n, u, i):
                pe.wait_ge(wgu[u], i)
                pe.wait_ge(xt, 2 * n + 4)
                pe.wait_ge(hm, n + 1)
                for k in range(KD):
                    last = pe.matmul(ps_h[:, u % 2].rearrange("p a f -> p (a f)"), xT[:, u % 2, k], w[:, u, :, k], start=(k == 0), stop=(k == KD - 1))
                last.then_inc(mm, 1)

            def turn_hidden(n, u):
                pe.wait_ge(hm, n + 3)
                pe.wait_ge(hc, n + 1)
                for k in range(FK):
                    last = pe.transpose(ps_t[:, k * P:(k + 1) * P], hmid[:, u % 2, k:F:FK], ident[:, :])
                last.then_inc(ht, 1)

            def down(n, u, i):
                pe.wait_ge(wdn[u], i)
                pe.wait_ge(hc, n + 2)
                pe.wait_ge(ye, 2 * n + 1)
                for hf in range(2):
                    c = slice(hf * 512, hf * 512 + 512)
                    for k in range(FK):
                        last = pe.matmul(ps_y[:, c], hT[:, u % 2, k], wd[:, u, k, c], start=(k == 0), stop=(k == FK - 1))
                last.then_inc(dm, 1)

            turn(0, 0, 16)
            up(0, 0, 32)
            turn(1, 1, 16)
            turn_hidden(0, 0)

            def step(n, u, rounds):
                up(n, u, 32 * rounds[0])
                down(n - 1, (u - 1) % DEPTH_W, 16 * rounds[1])
                if rounds[2] is not None:
                    turn(n + 1, (u + 1) % DEPTH_W, 16 * rounds[2])
                turn_hidden(n, u)

            loops = BLOCKS // DEPTH_W - 1
            with pe.Fori(0, loops) as i:
                for u in range(1, DEPTH_W + 1):
                    n = i * DEPTH_W + u
                    step(n, u % DEPTH_W, [i + 1 + (u + k) // DEPTH_W for k in (0, -1, 1)])
            for n in range(loops * DEPTH_W + 1, BLOCKS):
                step(n, n % DEPTH_W, [turns(n), turns(n - 1), turns(n + 1) if n + 1 < BLOCKS else None])
            down(BLOCKS - 1, (BLOCKS - 1) % DEPTH_W, 16 * turns(BLOCKS - 1))

        @block.scalar
        def _(act):
            def take_x(n, u):
                act.wait_ge(tp, n + DEPTH_W + 1)
                act.wait_ge(mm, n + 1)
                for hf in range(2):
                    c = slice(hf * KD // 2, (hf + 1) * KD // 2)
                    act.activation(xT[:, u % 2, c], ps_x[:, c], ACT.Copy).then_inc(xt, 1)

            act.sem_inc(mm, 2)
            act.sem_inc(hc, 1)
            take_x(0, 0)

            def body(n, u, i, more=True):
                act.wait_ge(mm, n + 3)
                act.wait_ge(hm, n + 1)
                act.activation(sg[:, u % 2], ps_h[:, u % 2, 0], ACT.Tanh, scale=0.5).then_inc(th, 1)
                if more:
                    take_x(n + 1, u + 1)
                act.wait_ge(ht, n + 1)
                act.wait_ge(dm, n + 1)
                act.activation(hT[:, u % 2].rearrange("p k j -> p (k j)"), ps_t[:, 0:F], ACT.Copy).then_inc(hc, 1)

            with act.Fori(0, BLOCKS // DEPTH_W - 1) as i:
                for u in range(DEPTH_W):
                    body(i * DEPTH_W + u, u, i)
            for n in range(BLOCKS - DEPTH_W, BLOCKS):
                body(n, n % DEPTH_W, None, n + 1 < BLOCKS)

        @block.vector
        def _(v):
            v.sem_inc(hm, 2)
            v.sem_inc(ye, 1)
            link_n = [0]

            def hidden(n, u):
                v.wait_ge(th, n + 1)
                v.scalar_tensor_tensor(sg[:, u % 2], sg[:, u % 2], 1.0, ps_h[:, u % 2, 0], ALU.add, ALU.mult).then_inc(own, 1)
                v.wait_ge(own, n + 1)
                v.tensor_tensor(hmid[:, u % 2], sg[:, u % 2], ps_h[:, u % 2, 1], ALU.mult).then_inc(hm, 1)

            def take_y(n, u, rounds):
                v.wait_ge(dm, n + 3)
                v.wait_ge(yst[u % 2], 16 * rounds)
                for hf in range(2):
                    c = slice(hf * 512, hf * 512 + 512)
                    v.tensor_copy(y[:, u % 2, c], ps_y[:, c]).then_inc(ye, 1)

            hidden(0, 0)
            loops = BLOCKS // DEPTH_W - 1
            with v.Fori(0, loops) as i:
                for u in range(1, DEPTH_W + 1):
                    n = i * DEPTH_W + u
                    hidden(n, u % DEPTH_W)
                    take_y(n - 1, (u - 1) % DEPTH_W, i * 2 + (u - 1) // 2 + 1)
            for n in range(loops * DEPTH_W + 1, BLOCKS):
                hidden(n, n % DEPTH_W)
                take_y(n - 1, (n - 1) % DEPTH_W, (n - 1) // 2 + 1)
            take_y(BLOCKS - 1, (BLOCKS - 1) % DEPTH_W, (BLOCKS - 1) // 2 + 1)


def combine(nc, sems, t, d):
    ld, h0, h1s, ga, gb, s0, s1, sqd, sdd, own, msd, ixs = sems(
        *(f"c_{k}" for k in "ld h0 h1 ga gb s0 s1 sq sd own ms ix".split()))
    tick = t["tick"]
    NV = t["combine_count"]
    with ExitStack() as ctx:
        sb = lambda n, s, dt=F32: ctx.enter_context(nc.sbuf_tensor(n, s, dt))
        g = sb("g_final", [P, D])
        h = sb("h_c", [P, 2, D])
        ya = [[sb(f"y{k}{u}", [P, D]) for k in range(TOPK)] for u in range(2)]
        idx = [[sb(f"yi{k}{u}", [P, 1], I32) for k in range(TOPK)] for u in range(2)]
        o = sb("o_c", [P, 2, D])
        sq = sb("sq_c", [P, D])
        sc = sb("sc_c", [P, 2])
        ss, rs = sc[:, 0:1], sc[:, 1:2]
        h1v = d["h1_rows"].rearrange("(n p) d -> n p d", p=P)
        ov = d["out"].rearrange("b (n p) d -> (b n) p d", p=P)
        block = ctx.enter_context(nc.Block())
        STEPS = NB // 2
        xs = (ga, gb)

        @block.sync
        def _(sp):
            sp.dma_start(g[:, :], d["norm_final_g"].rearrange("(a n) -> a n", a=1).broadcast_to([P, D])).then_inc(ld, 16)
            with sp.Fori(0, STEPS) as i:
                for u, sh in enumerate((h0, h1s)):
                    sp.wait_ge(msd, 2 * i + u + 1)
                    sp.dma_start(h[:, u], h1v[bass.ds(2 * i + u, 1)]).then_inc(sh, 16)
                for u, st in enumerate((s0, s1)):
                    sp.wait_ge(msd, 2 * i + u + 3)
                    sp.dma_start(ov[bass.ds(2 * i + u, 1)], o[:, u]).then_inc(st, 16)
            sp.wait_ge(s0, 16 * STEPS + 16)
            sp.wait_ge(s1, 16 * STEPS + 16)

        @block.gpsimd
        def _(pool):
            pool.sem_inc(s0, 16)
            pool.sem_inc(s1, 16)
            with pool.Fori(0, STEPS) as i:
                for u in range(2):
                    pool.wait_ge(msd, 2 * i + u + 1)
                    for k in range(TOPK):
                        col = (2 * i + u) * TOPK + k
                        pool.tensor_copy(idx[u][k][:, :], t["ydest"][:, bass.ds(col, 1)]).then_inc(ixs, 1)
                    pool.wait_ge(ixs, (2 * i + u) * TOPK + TOPK)
                    pool.sem_inc(tick, 1)
                    for k in range(TOPK):
                        pool.indirect_dma_start(ya[u][k][:, :], None, d["y_rows"], bass.IndirectOffsetOnAxis(idx[u][k][:, :], 0)).then_inc(xs[u], 16)

        @block.scalar
        def _(act):
            with act.Fori(0, STEPS) as i:
                for u in range(2):
                    n = 2 * i + u
                    act.wait_ge(sqd, 2 * n + 1)
                    act.activation(sq[:, :], h[:, u], ACT.Square, accum_out=ss).then_inc(sdd, 1)
                    act.wait_ge(sqd, 2 * n + 2)
                    act.activation(rs, ss, ACT.Sqrt).then_inc(sdd, 1)

        @block.vector
        def _(v):
            v.sem_inc(msd, 2)
            v.wait_ge(ld, 16)
            with v.Fori(0, STEPS) as i:
                link = Chain(v, own, i * NV)
                for u in range(2):
                    n = 2 * i + u
                    v.wait_ge(h1s if u else h0, 16 * i + 16)
                    v.wait_ge(xs[u], 32 * i + 32)
                    link(v.scalar_tensor_tensor(h[:, u], ya[u][0][:, :], t["wts"][:, bass.ds(n, 1), 0], h[:, u], ALU.mult, ALU.add))
                    v.scalar_tensor_tensor(h[:, u], ya[u][1][:, :], t["wts"][:, bass.ds(n, 1), 1], h[:, u], ALU.mult, ALU.add).then_inc(sqd, 1)
                    v.wait_ge(sdd, 2 * n + 1)
                    v.tensor_scalar(ss, ss, 1.0 / D, EPS, ALU.mult, ALU.add).then_inc(sqd, 1)
                    v.wait_ge(sdd, 2 * n + 2)
                    link(v.reciprocal(rs, rs))
                    v.wait_ge(s1 if u else s0, 16 * i + 16)
                    v.scalar_tensor_tensor(o[:, u], h[:, u], rs, g[:, :], ALU.mult, ALU.mult).then_inc(msd, 1)
            assert link.n == NV, link.n


def program(nc, d):
    with ExitStack() as ctx:
        def sems(*names):
            return [ctx.enter_context(nc.semaphore(n)) for n in names]

        sb = lambda n, s, dt=F32: ctx.enter_context(nc.sbuf_tensor(n, s, dt))

        t = {"ident": sb("ident", [P, P]), "carry": sb("carry", [P, E]), "eids": sb("eids", [P, NB, TOPK]),
             "ranks": sb("ranks", [P, NB, TOPK]), "wts": sb("wts", [P, NB, TOPK]), "bexp": sb("bexp", [1, BLOCKS], I32),
             "slots": sb("slots", [P, BLOCKS + 4], I32), "ydest": sb("ydest", [P, NB * TOPK], I32)}
        t["tick"], = sems("tick")
        t["mix_counts"] = (41, 3)
        t["route_count"] = 52
        t["combine_count"] = 4
        with nc.sbuf_tensor("cT", [P, CHUNKS, TP], F32) as cT:
            t["cT"] = cT
            with nc.sbuf_tensor("xnT", [P, KD, TG], F32) as xnT:
                t["xnT"] = xnT
                norm_and_turn(nc, sems, t, d)
                project(nc, sems, t, d)
            mix(nc, sems, t, d)
            merge(nc, sems, t, d)
            route(nc, sems, t, d)
        table(nc, sems, t, d)
        experts(nc, sems, t, d)
        combine(nc, sems, t, d)


_INS = ["x", "meta_tokens", "norm_mix_g", "w_in", "shift_mu", "w0", "w_decay_up", "a0", "w_aaa_up", "w_gate_up",
        "k_k", "k_a", "r_k", "ln_x_g", "ln_x_b", "attn_sinks", "w_o_attn", "w_o_rwkv", "w_out", "norm_ffn_g",
        "w_grp", "b_grp", "w_exp", "b_exp", "e_gate", "e_up", "e_down", "norm_final_g"]


def kernel(**inputs):
    import numpy as _np
    import concourse.bacc as _bacc
    from concourse import mybir as _mybir
    from concourse.bass_utils import run_bass_kernel_spmd as _run

    nc = _bacc.Bacc("TRN2", target_bir_lowering=False, num_devices=1)
    arrays, d = {}, {}
    named = [(n, inputs[n]) for n in _INS] + [("c_" + n, a) for n, a in constants().items()]
    for name, a in named:
        a = _np.ascontiguousarray(a)
        arrays["in_" + name] = a
        d[name] = nc.dram_tensor("in_" + name, a.shape, _mybir.dt.from_np(a.dtype), kind="ExternalInput").ap()
    d["out"] = nc.dram_tensor("out", (1, SEQ, D), F32, kind="ExternalOutput").ap()
    for name, shape, dt in SCRATCH:
        d[name] = nc.dram_tensor(name, shape, dt, kind="Internal").ap()
    program(nc, d)
    r = _run(nc, [arrays], core_ids=[0])
    return r.results[0]["out"]


SCRATCH = [("xn_spill", (P, KD * SEQ), F32), ("xn2_rows", (SEQ, D), F32), ("h1_rows", (SEQ, D), F32),
           ("slot_tok", (BLOCKS * P, 1), I32), ("y_rows", (BLOCKS * P, D), F32)]
```

```python
from contextlib import ExitStack

import numpy as np
import concourse.bass as bass
from concourse import mybir

F32 = mybir.dt.float32
I32 = mybir.dt.int32
U32 = mybir.dt.uint32
U8 = mybir.dt.uint8
ACT = mybir.ActivationFunctionType
ALU = mybir.AluOpType
AX = mybir.AxisListType

P = 128
D = 1024
KD = D // P
SEQ = 1024
META = 16
NB = SEQ // P
T = META + SEQ
PAD = P - META
TP = T + PAD
NBLK = TP // P
GROUP = 347
NGROUPS = 3
TG = GROUP * NGROUPS
HEADS = 8
HD = 64
PAIRS = HEADS // 2
KV = 2
RD = HEADS * HD
SCALE = HD ** -0.5
BAND = 2 * P + META
CH_Q, CH_K, CH_V, CH_RR, CH_RK, CH_RV, CH_WA, CH_G, CHUNKS = 0, 4, 5, 6, 10, 14, 18, 19, 20
CH_MIX = CH_RK
GATE0 = CHUNKS * P
EPS = 1e-6
LN_EPS = 64e-5
DECAY = float(np.exp(-0.5))
E = 32
NG = 4
EG = E // NG
F = 256
TOPK = 2
BLOCKS = -(-(SEQ * TOPK + E * (P - 1)) // P)
SURE = E
DEPTH_W = 4
EARLY = 2
NEG = -1e30
LEVELS = [1, 2, 4, 8, 16]


def constants():
    i = np.arange(P)
    row, col = i[:, None], i[None, :]
    c = {}
    c["ident"] = np.eye(P, dtype=np.float32)
    c["headones"] = (row // HD == col // HD).astype(np.float32)
    upper = np.stack([row < col, row <= col], 1)
    c["upper"] = upper.astype(np.float32)
    c["lower"] = (row > col).astype(np.float32)
    low = [((row // n) % 2 == 1) & (col // n == row // n - 1) for n in LEVELS]
    c["lev"] = np.stack([np.stack([m, m.T], 1) for m in low], 1).astype(np.float32)
    q, k = np.arange(P)[:, None], np.arange(2 * P)[None, :]
    diff = q + P - k
    m = np.arange(META)[None, :]
    slopes = 2.0 ** (-8.0 * (np.arange(HEADS) + 1) / HEADS)
    bias = np.zeros((NBLK, P, HEADS, BAND), np.float32)
    for b in range(NBLK):
        seen = (diff >= 0) & (diff < P) & (((b - 1) * P + k) >= P)
        far = np.minimum(b * P + q - PAD - m, P)
        for h in range(HEADS):
            bias[b, :, h, :2 * P] = np.where(seen, -slopes[h] * diff, NEG)
            bias[b, :, h, 2 * P:] = np.where(far >= 0, -slopes[h] * far, NEG)
    c["bias"] = bias.reshape(NBLK * P, HEADS * BAND)
    reset = np.ones((P, PAIRS, P), np.float32)
    reset[:, :, 0] = 0.0
    c["reset"] = reset.reshape(P, PAIRS * P)
    c["iota"] = np.tile(np.arange(E, dtype=np.float32), (P, 1))
    c["blockno"] = np.tile(np.arange(BLOCKS, dtype=np.float32), (P, 1))
    c["over"] = np.tile(P * np.arange(NB, dtype=np.float32), (P, 1))
    c["tokno"] = (np.arange(NB)[None, :] * P + np.arange(P)[:, None]).astype(np.int32)
    return c


class Chain:

    def __init__(self, eng, sem, base=0):
        self.eng, self.sem, self.base, self.n = eng, sem, base, 0

    def add(self, ins):
        self.n += 1
        return ins.then_inc(self.sem, 1)

    def join(self):
        self.eng.wait_ge(self.sem, self.base + self.n)

    def __call__(self, ins):
        self.add(ins)
        self.join()


def norm_and_turn(nc, sems, t, d):
    loaded, xa, xb, squared, scaled, turned, taken, own = sems(
        "loaded", "n_xa", "n_xb", "squared", "scaled", "turned", "taken", "own")
    GROUPS = 2
    PER = NB // GROUPS
    with ExitStack() as ctx:
        sb = lambda n, s, dt=F32: ctx.enter_context(nc.sbuf_tensor(n, s, dt))
        xall = sb("xall", [P, NB, D])
        xmeta = sb("xmeta", [META, D])
        gmix = sb("gmix", [P, KD])
        sq = sb("sq", [P, D])
        ssq = sb("ssq", [P, NB + 1])
        rstd = sb("rstd", [P, NB + 1])
        xs = sb("xs", [P, 2, D])
        ps = ctx.enter_context(nc.psum_tensor("turn_ps", [P, 2, KD, P], F32))
        ident, xnT = t["ident"], t["xnT"]
        block = ctx.enter_context(nc.Block())

        def tiles(eng, g):
            if g == 0:
                yield META, xmeta[:, :], 0, 0, 0
            with eng.Fori(g * PER // 2, (g + 1) * PER // 2) as j:
                for u in range(2):
                    i = 2 * j + u
                    yield P, xall[:, bass.ds(i, 1), :].rearrange("p a d -> p (a d)"), META + i * P, i + 1, (u + 1) % 2

        @block.sync
        def _(sp):
            xv = d["x"].rearrange("b (n p) d -> p (b n) d", p=P)
            sp.dma_start(xmeta[:, :], d["meta_tokens"][:, :]).then_inc(xa, 16)
            sp.dma_start(xall[:, 0:PER], xv[:, 0:PER]).then_inc(xa, 16)
            sp.dma_start(gmix[:, :], d["norm_mix_g"].rearrange("l (c p) -> p (l c)", p=P), allow_slow_non_contiguous=True).then_inc(loaded, 16)
            sp.dma_start(ident[:, :], d["c_ident"]).then_inc(loaded, 16)
            sp.dma_start(xall[:, PER:], xv[:, PER:]).then_inc(xb, 16)
            for half in range(2):
                load_w_in(sp, t, d, half, half * t["w_cols"])
            sp.wait_ge(taken, 4 + 2 * (NB + 1))
            sp.dma_start(d["xn_spill"].rearrange("p (c j) -> p c j", c=KD), xnT[:, :, META:T]).then_inc(t["spilled"], 16)

        @block.scalar
        def _(act):
            act.wait_ge(own, 2)
            for g in range(GROUPS):
                act.wait_ge(xb if g else xa, 16 if g else 32)
                for rows, src, _, n, _ in tiles(act, g):
                    act.wait_ge(squared, n + 1)
                    act.activation(sq[0:rows, :], src, ACT.Square, accum_out=ssq[0:rows, bass.ds(n, 1)]).then_inc(squared, 1)
                cols = slice(0 if g == 0 else 1 + g * PER, 1 + (g + 1) * PER)
                act.wait_ge(own, 2 + 3 * g + 1)
                act.activation(rstd[:, cols], ssq[:, cols], ACT.Sqrt).then_inc(own, 1)

        def scale(v, rows, src, n, u):
            v.wait_ge(turned, n + 1)
            v.tensor_scalar(xs[0:rows, u], src, rstd[0:rows, bass.ds(n, 1)], None, ALU.mult).then_inc(scaled, 1)

        def take(v, rows, col, n, u):
            v.wait_ge(turned, n + 3)
            for h in range(2):
                c0 = h * KD // 2
                v.tensor_tensor(xnT[:, c0:c0 + KD // 2, bass.ds(col, rows)], ps[:, u, c0:c0 + KD // 2, 0:rows],
                                gmix[:, c0:c0 + KD // 2].unsqueeze(2).broadcast_to([P, KD // 2, rows]),
                                ALU.mult).then_inc(taken, 1)

        @block.vector
        def _(v):
            v.memset(xnT[:, :, T:TG], 0.0).then_inc(own, 1)
            v.memset(ssq[:, :], 1.0).then_inc(own, 1)
            v.sem_inc(squared, 1)
            v.sem_inc(scaled, 1)
            v.wait_ge(loaded, 32)
            for g in range(GROUPS):
                cols = slice(0 if g == 0 else 1 + g * PER, 1 + (g + 1) * PER)
                v.wait_ge(squared, 1 + 1 + (g + 1) * PER)
                v.tensor_scalar(ssq[:, cols], ssq[:, cols], 1.0 / D, EPS, ALU.mult, ALU.add).then_inc(own, 1)
                v.wait_ge(own, 2 + 3 * g + 2)
                v.reciprocal(rstd[:, cols], rstd[:, cols]).then_inc(own, 1)
                v.wait_ge(own, 2 + 3 * g + 3)
                if g == 0:
                    scale(v, META, xmeta[:, :], 0, 0)
                    take(v, META, 0, 0, 0)
                with v.Fori(g * PER // 2, (g + 1) * PER // 2) as j:
                    for u in range(2):
                        i = 2 * j + u
                        scale(v, P, xall[:, bass.ds(i, 1), :].rearrange("p a d -> p (a d)"), i + 1, (u + 1) % 2)
                    for u in range(2):
                        i = 2 * j + u
                        take(v, P, META + i * P, i + 1, (u + 1) % 2)

        @block.tensor
        def _(pe):
            pe.sem_inc(turned, 2)
            pe.sem_inc(taken, 4)
            pe.wait_ge(loaded, 32)
            for g in range(GROUPS):
                for rows, _, _, n, u in tiles(pe, g):
                    pe.wait_ge(scaled, n + 2)
                    pe.wait_ge(taken, 2 * n + 2)
                    for c in range(KD):
                        last = pe.transpose(ps[:, u, c, 0:rows], xs[0:rows, u, c * P:(c + 1) * P], ident[0:rows, 0:rows])
                    last.then_inc(turned, 1)


def load_w_in(sp, t, d, half, col):
    wv = d["w_in"].rearrange("l (c p) n -> p (l c) n", p=P)
    sp.dma_start(t["w_in_sb"][:, half], wv[:, :, bass.ds(col, t["w_cols"])]).then_inc(t["w_in_loaded"][half], 16)


def project(nc, sems, t, d):
    mm, ev, sh, used, own, mus = sems("p_mm", "p_ev", "p_sh", "p_used", "p_own", "p_mu")
    wl, wl2 = t["w_in_loaded"]
    CPL = t["w_cols"] // P
    STEPS = CHUNKS // (2 * CPL)
    with ExitStack() as ctx:
        sb = lambda n, s, dt=F32: ctx.enter_context(nc.sbuf_tensor(n, s, dt))
        w = t["w_in_sb"]
        raw = sb("raw", [P, 2, 1 + TG])
        tmp = sb("shift_tmp", [P, T])
        mu = sb("mu", [P, CHUNKS])
        ps = ctx.enter_context(nc.psum_tensor("proj_ps", [P, 2, NGROUPS, 512], F32))
        xnT, cT = t["xnT"], t["cT"]
        block = ctx.enter_context(nc.Block())

        @block.sync
        def _(sp):
            sp.dma_start(mu[:, CH_RR:CHUNKS], d["shift_mu"].rearrange("l (c p) -> p (l c)", p=P), allow_slow_non_contiguous=True).then_inc(mus, 16)
            with sp.Fori(1, STEPS) as i:
                for half in range(2):
                    sp.wait_ge(mm, (i - 1) * 2 * CPL + (half + 1) * CPL)
                    load_w_in(sp, t, d, half, i * (2 * CPL * P) + half * CPL * P)
            sp.wait_ge(t["spilled"], 16)

        @block.tensor
        def _(pe):
            with pe.Fori(0, STEPS) as i:
                for half in range(2):
                    pe.wait_ge(wl2 if half else wl, (i + 1) * 16)
                    for c in range(CPL):
                        n = half * CPL + c
                        pe.wait_ge(ev, i * (2 * CPL) + n + 1)
                        for g in range(NGROUPS):
                            for k in range(KD):
                                last = pe.matmul(ps[:, n % 2, g, 0:GROUP], w[:, half, k, c * P:(c + 1) * P],
                                                 xnT[:, k, g * GROUP:(g + 1) * GROUP], start=(k == 0), stop=(k == KD - 1))
                        last.then_inc(mm, 1)

        @block.scalar
        def _(act):
            act.sem_inc(ev, 2)
            with act.Fori(0, STEPS) as i:
                for n in range(2 * CPL):
                    act.wait_ge(mm, i * (2 * CPL) + n + 1)
                    act.wait_ge(sh, i * (2 * CPL) + n + 1)
                    act.activation(raw[:, n % 2, 1:1 + TG].rearrange("p (g j) -> p g j", g=NGROUPS),
                                   ps[:, n % 2, :, 0:GROUP], ACT.Copy).then_inc(ev, 1)

        @block.vector
        def _(v):
            v.memset(raw[:, :, 0:1], 0.0).then_inc(own, 1)
            v.memset(mu[:, 0:CH_RR], 0.0).then_inc(own, 1)
            v.memset(cT[:, :, 0:PAD], 0.0).then_inc(own, 1)
            v.sem_inc(sh, 2)
            v.wait_ge(own, 3)
            v.wait_ge(mus, 16)
            with v.Fori(0, STEPS) as i:
                for n in range(2 * CPL):
                    v.wait_ge(ev, i * (2 * CPL) + n + 3)
                    v.wait_ge(sh, i * (2 * CPL) + n + 2)
                    v.tensor_tensor(tmp[:, :], raw[:, n % 2, 0:T], raw[:, n % 2, 1:1 + T], ALU.subtract).then_inc(used, 1)
                    v.wait_ge(used, i * (2 * CPL) + n + 1)
                    out = cT[:, bass.ds(i * (2 * CPL) + n, 1), PAD:TP].rearrange("p a j -> p (a j)")
                    col = i * (2 * CPL) + n
                    v.scalar_tensor_tensor(out, tmp[:, :], mu[:, bass.ds(col, 1)], raw[:, n % 2, 1:1 + T],
                                           ALU.mult, ALU.add).then_inc(sh, 1)


def mix(nc, sems, t, d):
    names = ("x_par x_bias x_st x_lora x_sg x_mmw x_mma x_mmg x_th x_tha x_qk x_lgt x_va x_ss x_rn x_kkr "
             "x_rec x_exp x_csd x_ar x_bk x_mmM x_msk x_mmA x_tt x_tok x_tinit x_x1 x_x1c x_yy x_tup x_W "
             "x_Wc x_U x_Uc x_Y x_Yc x_S x_S0 x_Sn x_sums x_sqr x_vr x_sd x_rk x_mx "
             "x_pe x_pn x_tp x_tpc x_O x_att x_v x_a x_init x_kb x_es x_yc x_vm x_fin")
    s = dict(zip([n[2:] for n in names.split()], sems(*names.split())))
    NV, NA = t["mix_counts"]
    with ExitStack() as ctx:
        sb = lambda n, sh, dt=F32: ctx.enter_context(nc.sbuf_tensor(n, sh, dt))
        ident, cT = t["ident"], t["cT"]
        headones, upper, lower = sb("headones", [P, P]), sb("upper", [P, 2, P]), sb("lower", [P, P])
        lev = sb("lev", [P, len(LEVELS), 2, P], U8)
        reset = sb("reset", [P, PAIRS * P])
        wup, gup = sb("wup", [P, 2, RD]), sb("gup", [P, RD])
        par = sb("par", [P, 9, PAIRS])
        hw0, ha0, kkw, hka, rkw, lng, lnb, omk = (par[:, n] for n in range(8))
        sink = sb("sink", [P, HEADS])
        bias = sb("bias", [P, HEADS, BAND])
        qs, kb = sb("qs", [P, PAIRS, P]), sb("kb", [P, KV, 2, BAND])
        lg = sb("lg", [P, HEADS, BAND])
        lev_in = lg[:, :, :].rearrange("p h k -> p (h k)")[:, 0:len(LEVELS) * 2 * P].rearrange("p (l a j) -> p l a j", l=len(LEVELS), a=2)
        st8 = sb("st8", [P, 5, HEADS])
        mx, nmx, dsk, es, ls = (st8[:, n] for n in range(5))
        vas, vtok = sb("vas", [P, P]), sb("vtok", [P, 3, P])
        pTm = sb("pTm", [META, HEADS, P])
        lora, sg = sb("lora", [P, P]), sb("sg", [P, P])
        wide = lambda n: sb(n, [P, PAIRS, P])
        th, tha, lw, cs = wide("th"), wide("tha"), wide("lw"), wide("cs")
        ep, em, kk, kp, tmp = wide("ep"), wide("em"), wide("kk"), wide("kp"), wide("tmp")
        ar, bt, kt = sb("ar", [P, PAIRS, 2, 2, P]), wide("bt"), wide("kt")
        el4 = sb("el4", [P, 2, PAIRS])
        ecm, elast = el4[:, 0], el4[:, 1]
        mats = sb("mats", [P, HEADS, 2, 2, P])
        A, X1, T2 = sb("A_m", [P, HEADS, P]), sb("X1_m", [P, HEADS, P]), sb("T_m", [P, 2, HEADS, P])
        Tm, TT = T2[:, 0], T2[:, 1]
        pT = T2
        btok, ktok, rvtok, rv, rkb = wide("btok"), wide("ktok"), wide("rvtok"), wide("rv"), wide("rkb")
        W, U = (A[:, 4 * n:4 * n + 4].rearrange("p a (b k) -> p (a b) k", k=HD) for n in range(2))
        S, S0 = sb("S_m", [P, PAIRS, HD]), sb("S0_m", [P, PAIRS, HD])
        WT = A[:, 4:8]
        yT = X1[:, 0:4]
        bank = [ctx.enter_context(nc.psum_tensor(f"mix_ps{n}", [P, 512], F32)) for n in range(8)]
        wide_ps = lambda n: bank[n][:, :].rearrange("p (c j) -> p c j", c=PAIRS)
        RING = (3, 4, 7, 2)
        PASSES = len(LEVELS) + 1
        PASSES_0 = META.bit_length() - 2
        block = ctx.enter_context(nc.Block())

        TURNED = range(1, PASSES - 1)
        UPDATES = 4 + 2 * len(TURNED)

        def products(m):
            return 2 * PASSES_0 + 2 * PASSES * m if not isinstance(m, int) or m >= 0 else 0

        def firsts(m, l, g, turned=0):
            before = 4 * PASSES_0 + (2 * PASSES + 2 * len(TURNED)) * m if not isinstance(m, int) or m >= 0 else 0
            own = (g, 2 + 4 * (l - 1) + 2 * g + turned, 2 + 4 * len(TURNED) + g)
            return before + 1 + own[0 if l == 0 else 1 if l < PASSES - 1 else 2]

        def updates(m):
            return 4 + 2 * PASSES_0 + UPDATES * m if not isinstance(m, int) or m >= 0 else 0

        def cols(ch, i, n=1):
            return cT[:, ch:ch + n, bass.ds(i * P, P)]

        def apart(eng):
            eng.sem_inc(t["tick"], 1)

        def blk(ch, i):
            return cols(ch, i).rearrange("p a j -> p (a j)")

        def hp(h):
            return slice(HD * (h % 2), HD * (h % 2) + HD)

        @block.sync
        def _(sp):
            for dst, name in ((headones[:, :], "c_headones"), (upper[:, :, :], "c_upper"), (lower[:, :], "c_lower"),
                              (lev_in, "c_lev"), (reset[:, :], "c_reset")):
                sp.dma_start(dst, d[name]).then_inc(s["par"], 16)
            sp.wait_ge(s["init"], 1)
            sp.dma_start(wup[0:64, 0], d["w_decay_up"][0]).then_inc(s["par"], 16)
            sp.dma_start(wup[64:128, 1], d["w_aaa_up"][0]).then_inc(s["par"], 16)
            sp.dma_start(gup[:, :], d["w_gate_up"][0]).then_inc(s["par"], 16)
            for dst, name in ((hw0, "w0"), (ha0, "a0"), (kkw, "k_k"), (hka, "k_a"), (lng, "ln_x_g"), (lnb, "ln_x_b")):
                sp.dma_start(dst, d[name].rearrange("l (c p) -> p (l c)", p=P), allow_slow_non_contiguous=True).then_inc(s["par"], 16)
            sp.dma_start(rkw, d["r_k"].rearrange("l (c a) k -> (a k) (l c)", a=2), allow_slow_non_contiguous=True).then_inc(s["par"], 16)
            sp.dma_start(sink[:, :], d["attn_sinks"][0:1, :].broadcast_to([P, HEADS])).then_inc(s["par"], 16)
            zeros = cT[:, 0:D // HD, 0:HD]
            with sp.Fori(SURE, BLOCKS) as n:
                sp.dma_start(d["y_rows"].rearrange("(n p) (c j) -> n p c j", p=P, j=HD)[bass.ds(n, 1)], zeros).then_inc(t["y_zeroed"], 16)
            bv = d["c_bias"].rearrange("(b p) n -> b p n", p=P)
            sp.dma_start(bias[:, :, :], bv[1]).then_inc(s["bias"], 16)
            with sp.Fori(2, NBLK) as i:
                sp.wait_ge(s["lgt"], (i - 1) * HEADS)
                sp.dma_start(bias[:, :, :], bv[bass.ds(i, 1)]).then_inc(s["bias"], 16)
            sp.wait_ge(t["y_zeroed"], 16 * (BLOCKS - SURE))

        N_PAR = 16 * 16

        @block.scalar
        def _(act):
            act.wait_ge(s["par"], N_PAR)
            act.wait_ge(s["init"], 4)
            for g in range(KV):
                for half in range(2):
                    act.activation(kb[HD * half:HD * half + HD, g, half, 2 * P:BAND], cT[HD * g:HD * g + HD, CH_K, PAD:P], ACT.Copy).then_inc(s["a"], 1)
            act.wait_ge(s["qk"], 1)
            act.activation(vtok[0:META, 2], bank[0][0:META, 0:P], ACT.Copy).then_inc(s["vm"], 1)
            base = 4
            act.sem_inc(s["att"], 1)

            def stage_low(j, first=False):
                if not first:
                    act.wait_ge(s["mma"], j)
                apart(act)
                act.activation(lora[0:64, :], cT[0:64, CH_WA, bass.ds(j * P, P)], ACT.Tanh).then_inc(s["lora"], 1)
                act.activation(lora[64:128, :], cT[64:128, CH_WA, bass.ds(j * P, P)], ACT.Copy).then_inc(s["lora"], 1)

            def stage_gate(j, link):
                apart(act)
                link(act.activation(sg[:, :], blk(CH_G, j), ACT.Tanh, scale=0.5))
                act.activation(sg[:, :], sg[:, :], ACT.Copy, scale=0.5, bias=0.5).then_inc(s["sg"], 1)

            def stage_attention(j, link):
                act.wait_ge(s["qk"], (j - 1) * HEADS + 1)
                apart(act)
                act.activation(qs[:, :, :], cols(CH_Q, j, 4), ACT.Copy).then_inc(s["st"], 1)
                link(act.activation(kb[:, :, :, 0:P], kb[:, :, :, P:2 * P], ACT.Copy))
                for g in range(KV):
                    for half in range(2):
                        act.activation(kb[HD * half:HD * half + HD, g, half, P:2 * P], cT[HD * g:HD * g + HD, CH_K, bass.ds(j * P, P)],
                                       ACT.Copy).then_inc(s["kb"], 1)

            def stage_v(j):
                apart(act)
                act.activation(vas[:, :], blk(CH_V, j), ACT.Copy).then_inc(s["va"], 1)
                act.activation(rv[:, :, :], cols(CH_RV, j, 4), ACT.Copy).then_inc(s["va"], 1)

            def low_rank(j):
                act.wait_ge(s["mmw"], j + 1)
                for p in range(PAIRS):
                    act.activation(th[:, p], wide_ps(0)[:, p], ACT.Tanh, scale=0.5, bias=hw0[:, p:p + 1]).then_inc(s["th"], 1)
                act.wait_ge(s["mma"], j + 1)
                for p in range(PAIRS):
                    act.activation(tha[:, p], wide_ps(1)[:, p], ACT.Tanh, scale=0.5, bias=ha0[:, p:p + 1]).then_inc(s["tha"], 1)

            def decays(j):
                act.wait_ge(s["csd"], j + 1)
                act.activation(ecm, cs[:, :, P // 2 - 1], ACT.Exp).then_inc(s["exp"], 1)
                act.activation(ep[:, :, :], lw[:, :, :], ACT.Exp).then_inc(s["exp"], 1)
                act.activation(em[:, :, :], tmp[:, :, :], ACT.Exp, scale=-1.0).then_inc(s["exp"], 1)
                act.wait_ge(s["exp"], 4 * j + 1)
                act.activation(cs[:, :, :], tmp[:, :, :], ACT.Exp).then_inc(s["exp"], 1)

            def key_norm(j):
                act.wait_ge(s["rn"], 2 * j + 1)
                act.activation(kp[:, :, :], kp[:, :, :], ACT.Sqrt).then_inc(s["rec"], 1)

            def body(i, base, first=False, last_block=False):
                m, prep = i - 1, not last_block
                link = Chain(act, s["a"], base)
                act.wait_ge(s["tt"], 4 * i + 2)
                act.activation(rvtok[:, :, :], wide_ps(0), ACT.Copy).then_inc(s["tok"], 1)
                link(act.activation(vtok[:, 0], vtok[:, 1], ACT.Copy))
                act.activation(vtok[:, 1], bank[1][:, 0:P], ACT.Copy).then_inc(s["tok"], 1)
                if prep:
                    stage_low(i + 1)
                act.wait_ge(s["tt"], 4 * i + 4)
                act.activation(btok[:, :, :], wide_ps(0), ACT.Copy).then_inc(s["tok"], 1)
                act.activation(ktok[:, :, :], wide_ps(1), ACT.Copy).then_inc(s["tok"], 1)
                for l in range(PASSES_0 if first else PASSES):
                    for g in range(2):
                        hs = slice(4 * g, 4 * g + 4)
                        act.wait_ge(s["x1"], firsts(m, l, g))
                        act.activation(X1[:, hs], wide_ps(3 + g), ACT.Copy).then_inc(s["x1c"], 1)
                        if l in TURNED:
                            act.wait_ge(s["x1"], firsts(m, l, g, 1))
                            act.activation(TT[:, hs], wide_ps(7 if g == 0 else 2), ACT.Copy).then_inc(s["x1c"], 1)
                    if l == 0 and prep:
                        low_rank(i + 1)
                    if l == 1:
                        if not first:
                            act.wait_ge(s["mx"], m + 1)
                            act.activation(es, dsk, ACT.Exp).then_inc(s["es"], 1)
                            for h in range(HEADS):
                                act.activation(lg[:, h], lg[:, h], ACT.Exp, bias=nmx[:, h:h + 1], accum_out=ls[:, h:h + 1]).then_inc(s["pe"], 1)
                        act.wait_ge(s["W"], 2 * i + 1)
                        act.activation(WT, wide_ps(0), ACT.Copy).then_inc(s["Wc"], 1)
                    if l == 2:
                        if prep:
                            decays(i + 1)
                        act.wait_ge(s["W"], 2 * i + 2)
                        act.activation(W[:, :, :], bank[1][:, :].rearrange("p (h k) -> p h k", h=HEADS), ACT.Copy).then_inc(s["Wc"], 1)
                    if l == 3 and prep:
                        stage_attention(i + 1, link)
                    if l == 4 and prep:
                        key_norm(i + 1)
                    if l >= 4:
                        n = 2 << l
                        for g in range(2):
                            act.wait_ge(s["yy"], products(m) + 2 * l + g + 1)
                            hs = slice(4 * g, 4 * g + 4)
                            y, yt = wide_ps(5 + g), wide_ps(7 if g == 0 else 2)
                            for b in range(0, P, 2 * n):
                                if l == 4:
                                    act.activation(Tm[b + n:b + 2 * n, hs, b:b + n], y[b + n:b + 2 * n, :, b:b + n], ACT.Copy).then_inc(s["tinit"], 1)
                                act.activation(TT[b:b + n, hs, b + n:b + 2 * n], yt[b:b + n, :, b + n:b + 2 * n], ACT.Copy).then_inc(s["tinit"], 1)
                if first:
                    for g in range(2):
                        act.wait_ge(s["x1"], 4 * PASSES_0 - 2 + g + 1)
                        act.activation(TT[:, 4 * g:4 * g + 4], wide_ps(7 if g == 0 else 2), ACT.Copy).then_inc(s["x1c"], 1)
                    stage_attention(i + 1, link)
                    stage_gate(i + 1, link)
                    key_norm(i + 1)
                act.wait_ge(s["U"], i + 1)
                act.activation(U[:, :, :], bank[1][:, :].rearrange("p (h k) -> p h k", h=HEADS), ACT.Copy).then_inc(s["Uc"], 1)
                if prep:
                    stage_v(i + 1)
                if first:
                    return link.n
                act.wait_ge(s["Y"], m + 1)
                act.activation(yT, wide_ps(3), ACT.Copy).then_inc(s["Yc"], 1)
                for n in range(4):
                    act.wait_ge(s["tp"], 6 * m + n + 1)
                    act.activation(pT[:, n // 2, 4 * (n % 2):4 * (n % 2) + 4], wide_ps((0, 1, 2, 7)[n]), ACT.Copy).then_inc(s["tpc"], 1)
                    if n == 1:
                        act.wait_ge(s["yc"], m + 1)
                        act.activation(tmp[:, :, :], yT, ACT.Square).then_inc(s["sqr"], 1)
                for n in range(2):
                    act.wait_ge(s["tp"], 6 * m + 5 + n)
                    act.activation(pTm[:, 4 * n:4 * n + 4], wide_ps(3 + 1 * n)[0:META], ACT.Copy).then_inc(s["tpc"], 1)
                act.wait_ge(s["vr"], m + 1)
                act.activation(th[:, :, :], th[:, :, :], ACT.Sqrt).then_inc(s["sd"], 1)
                act.wait_ge(s["O"], m + 1)
                apart(act)
                act.activation(cols(CH_Q, i, 4), wide_ps(1), ACT.Copy).then_inc(s["att"], 1)
                if prep:
                    act.wait_ge(s["mmg"], m + 1)
                    stage_gate(i + 1, link)
                return link.n

            link = Chain(act, s["a"], base)
            act.wait_ge(s["init"], 9)
            stage_low(0, first=True)
            low_rank(0)
            stage_v(0)
            decays(0)
            key_norm(0)
            base += link.n
            base += body(0, base, first=True)
            with act.Fori(1, NBLK - 1) as i:
                assert body(i, (i - 1) * NA + base) == NA, "steps of a block"
            body(NBLK - 1, (NBLK - 2) * NA + base, last_block=True)

        @block.vector
        def _(v):
            v.memset(wup[:, :, :], 0.0).then_inc(s["init"], 1)
            v.memset(kb[:, :, :, :], 0.0).then_inc(s["init"], 1)
            v.memset(vtok[:, 1], 0.0).then_inc(s["init"], 1)
            v.memset(S[:, :, :], 0.0).then_inc(s["init"], 1)
            v.memset(ar[:, :, :, :, :], 0.0).then_inc(s["init"], 1)
            v.wait_ge(s["par"], N_PAR)
            v.tensor_scalar(par[:, 0:2], par[:, 0:2], 0.5, None, ALU.mult).then_inc(s["init"], 1)
            v.tensor_scalar(hka, hka, 0.5, None, ALU.mult).then_inc(s["init"], 1)
            v.wait_ge(s["init"], 7)
            v.tensor_copy(lev[:, :, :, :], lev_in).then_inc(s["init"], 1)
            v.wait_ge(s["init"], 8)
            v.tensor_scalar(omk, hka, -1.0, 1.0, ALU.mult, ALU.add).then_inc(s["init"], 1)
            v.wait_ge(s["init"], 9)
            v.sem_inc(s["fin"], 1)
            flat = lambda x: x[:, :, :].rearrange("p c j -> p (c j)")

            def decays(j, link):
                v.wait_ge(s["th"], 4 * j + 4)
                link(v.tensor_scalar(lw[:, :, :], th[:, :, :], -0.5 * DECAY, -0.5 * DECAY, ALU.mult, ALU.add))
                link(v.tensor_tensor_scan(flat(cs), reset[:, :], flat(lw), 0.0, ALU.mult, ALU.add))
                for p in range(PAIRS):
                    link.add(v.tensor_scalar(tmp[:, p], cs[:, p], cs[:, p, P // 2 - 1:P // 2], None, ALU.subtract))
                link.join()
                v.tensor_tensor(lw[:, :, :], tmp[:, :, :], lw[:, :, :], ALU.subtract).then_inc(s["csd"], 1)

            def keys(j, link):
                for p in range(PAIRS):
                    link.add(v.tensor_scalar(kk[:, p], blk(CH_RK + p, j), kkw[:, p:p + 1], None, ALU.mult))
                link.join()
                v.tensor_tensor(kp[:, :, :], kk[:, :, :], kk[:, :, :], ALU.mult).then_inc(s["kkr"], 1)

            def key_norm(j):
                v.wait_ge(s["ss"], j + 1)
                v.tensor_scalar(kp[:, :, :], wide_ps(0), 1e-24, None, ALU.max).then_inc(s["rn"], 1)

            def factors(j, link):
                v.wait_ge(s["rec"], j + 1)
                link(v.reciprocal(kp[:, :, :], kp[:, :, :]))
                v.tensor_tensor(kk[:, :, :], kk[:, :, :], kp[:, :, :], ALU.mult).then_inc(s["rn"], 1)
                v.wait_ge(s["rn"], 2 * j + 2)
                v.wait_ge(s["tha"], 4 * j + 4)
                for p in range(PAIRS):
                    link.add(v.tensor_scalar(kp[:, p], tha[:, p], hka[:, p:p + 1], omk[:, p:p + 1], ALU.mult, ALU.add))
                link.add(v.tensor_scalar(th[:, :, :], tha[:, :, :], 0.5, 0.5, ALU.mult, ALU.add))
                link.join()
                link.add(v.tensor_tensor(kp[:, :, :], kp[:, :, :], cols(CH_RK, j, 4), ALU.mult))
                link(v.tensor_tensor(th[:, :, :], th[:, :, :], kk[:, :, :], ALU.mult))
                v.wait_ge(s["exp"], 4 * j + 4)
                v.tensor_tensor(bt[:, :, :], th[:, :, :], em[:, :, :], ALU.mult).then_inc(s["bk"], 1)
                v.tensor_tensor(kt[:, :, :], kp[:, :, :], em[:, :, :], ALU.mult).then_inc(s["bk"], 1)

            def reads(j, e):
                v.scalar_tensor_tensor(ar[hp(e), :, e, 0], kk[hp(e)], -1.0, ep[hp(e)], ALU.mult, ALU.mult).then_inc(s["ar"], 1)
                v.tensor_tensor(ar[hp(e), :, e, 1], cols(CH_RR, j, 4)[hp(e)], cs[hp(e)], ALU.mult).then_inc(s["ar"], 1)

            def start_state(j, link):
                link.add(v.tensor_copy(elast, cs[:, :, P - 1]))
                v.tensor_tensor(S0[:, :, :], S[:, :, :], ecm.unsqueeze(2).broadcast_to([P, PAIRS, HD]), ALU.mult).then_inc(s["S0"], 1)

            def bonus_terms(j, link):
                link(v.tensor_tensor(rkb[:, :, :], kp[:, :, :], cols(CH_RR, j, 4), ALU.mult))
                for p in range(PAIRS):
                    v.tensor_scalar(rkb[:, p], rkb[:, p], rkw[:, p:p + 1], None, ALU.mult).then_inc(s["rk"], 1)

            def body(i, base, first=False, last_block=False):
                m, prep = i - 1, not last_block
                link = Chain(v, s["v"], base)
                if not first:
                    v.wait_ge(s["bias"], 16 * m + 16)
                for h in () if first else range(HEADS):
                    v.wait_ge(s["qk"], HEADS * m + h + 2)
                    v.scalar_tensor_tensor(lg[:, h], bank[RING[h % 4]][:, 0:BAND], SCALE, bias[:, h], ALU.mult, ALU.add).then_inc(s["lgt"], 1)
                for h in range(HEADS):
                    v.wait_ge(s["mmM"], HEADS * i + h + 1)
                    src = bank[RING[h % 4]][:, :].rearrange("p (m c) -> p m c", m=2)
                    v.tensor_tensor(mats[:, h].rearrange("p m a j -> p m (a j)"), src,
                                    upper[:, :, :].rearrange("p a j -> p (a j)").unsqueeze(1).broadcast_to([P, 2, 2 * P]),
                                    ALU.mult).then_inc(s["msk"], 1)
                for g in range(2):
                    hs = slice(4 * g, 4 * g + 4)
                    link.add(v.tensor_copy(Tm[:, hs], ident[:, :].unsqueeze(1).broadcast_to([P, 4, P])))
                    link.add(v.tensor_copy(TT[:, hs], ident[:, :].unsqueeze(1).broadcast_to([P, 4, P])))
                    v.wait_ge(s["mmA"], 2 * i + g + 1)
                    link.add(v.tensor_tensor(A[:, g:HEADS:2], wide_ps(5 + g), lower[:, :].unsqueeze(1).broadcast_to([P, 4, P]), ALU.mult))
                v.wait_ge(s["msk"], HEADS * i + HEADS)
                link.join()
                mask = lambda l, tr: lev[:, l, tr].unsqueeze(1).broadcast_to([P, 4, P])
                apart(v)
                for g in range(2):
                    hs = slice(4 * g, 4 * g + 4)
                    v.copy_predicated(Tm[:, hs], mask(0, 0), A[:, hs]).then_inc(s["tup"], 1)
                    v.copy_predicated(TT[:, hs], mask(0, 1), mats[:, hs, 0, 0]).then_inc(s["tup"], 1)
                if not first:
                    v.wait_ge(s["lgt"], HEADS * m + HEADS)
                    link(v.tensor_reduce(mx, lg[:, :, :], AX.X, ALU.max))
                    link(v.tensor_tensor(mx, mx, sink[:, :], ALU.max))
                    link.add(v.tensor_scalar(nmx, mx, -1.0, None, ALU.mult))
                    link(v.tensor_tensor(dsk, sink[:, :], mx, ALU.subtract))
                    v.sem_inc(s["mx"], 1)
                for l in range(1, PASSES_0 + 1 if first else PASSES - 1):
                    for g in range(2):
                        hs = slice(4 * g, 4 * g + 4)
                        v.wait_ge(s["yy"], products(m) + 2 * (l - 1) + g + 1)
                        apart(v)
                        v.copy_predicated(Tm[:, hs], mask(l, 0), wide_ps(5 + g)).then_inc(s["tup"], 1)
                    if l == 1 and prep:
                        decays(i + 1, link)
                    if l == 2:
                        if prep:
                            keys(i + 1, link)
                        if not first:
                            v.wait_ge(s["pe"], HEADS * m + HEADS)
                            v.wait_ge(s["es"], m + 1)
                            link(v.tensor_tensor(ls, ls, es, ALU.add))
                            link(v.reciprocal(ls, ls))
                    if l == 3 and prep:
                        key_norm(i + 1)
                if not first:
                    v.tensor_tensor(lg[:, :, :], lg[:, :, :], ls.unsqueeze(2).broadcast_to([P, HEADS, BAND]), ALU.mult).then_inc(s["pn"], 1)
                if prep:
                    factors(i + 1, link)
                v.wait_ge(s["S"], i + 1)
                if prep:
                    v.wait_ge(s["bk"], 2 * i + 4)
                v.tensor_tensor(S[:, :, :], S0[:, :, :], bank[4][:, 0:PAIRS * HD].rearrange("p (c k) -> p c k", c=PAIRS), ALU.add).then_inc(s["Sn"], 1)
                if first:
                    v.wait_ge(s["Sn"], i + 1)
                    link(v.tensor_tensor(S[:, :, :], S[:, :, :], elast.unsqueeze(2).broadcast_to([P, PAIRS, HD]), ALU.mult))
                    reads(i + 1, 0)
                    reads(i + 1, 1)
                    start_state(i + 1, link)
                    bonus_terms(i + 1, link)
                    return link.n
                v.wait_ge(s["sums"], 3 * m + 1)
                v.scalar_tensor_tensor(yT, wide_ps(5), -1.0 / HD, yT, ALU.mult, ALU.add).then_inc(s["yc"], 1)
                v.wait_ge(s["Sn"], i + 1)
                link(v.tensor_tensor(S[:, :, :], S[:, :, :], elast.unsqueeze(2).broadcast_to([P, PAIRS, HD]), ALU.mult))
                if prep:
                    reads(i + 1, 0)
                    reads(i + 1, 1)
                v.wait_ge(s["sums"], 3 * m + 2)
                v.tensor_scalar(th[:, :, :], wide_ps(6), 1.0 / HD, LN_EPS, ALU.mult, ALU.add).then_inc(s["vr"], 1)
                if prep:
                    start_state(i + 1, link)
                v.wait_ge(s["sums"], 3 * m + 3)
                link.add(v.tensor_tensor(lw[:, :, :], cols(CH_RV, i, 4), wide_ps(5), ALU.mult))
                if prep:
                    bonus_terms(i + 1, link)
                v.wait_ge(s["sd"], m + 1)
                link(v.reciprocal(th[:, :, :], th[:, :, :]))
                link(v.tensor_tensor(yT, yT, th[:, :, :], ALU.mult))
                for p in range(PAIRS):
                    link.add(v.tensor_scalar(yT[:, p], yT[:, p], lng[:, p:p + 1], lnb[:, p:p + 1], ALU.mult, ALU.add))
                link.join()
                link(v.tensor_tensor(yT, yT, lw[:, :, :], ALU.add))
                v.wait_ge(s["mmg"], m + 1)
                v.tensor_tensor(cols(CH_RR, i, 4), yT, wide_ps(6), ALU.mult).then_inc(s["fin"], 1)
                return link.n

            link = Chain(v, s["v"])
            decays(0, link)
            keys(0, link)
            key_norm(0)
            factors(0, link)
            reads(0, 0)
            reads(0, 1)
            start_state(0, link)
            base = link.n
            base += body(0, base, first=True)
            with v.Fori(1, NBLK - 1) as i:
                assert body(i, (i - 1) * NV + base) == NV, "steps of a block"
            body(NBLK - 1, (NBLK - 2) * NV + base, last_block=True)

        @block.tensor
        def _(pe):
            pe.wait_ge(s["par"], N_PAR)
            pe.transpose(bank[0][0:META, 0:P], cT[:, CH_V, PAD:P], ident[:, :]).then_inc(s["qk"], 1)
            pe.wait_ge(s["vm"], 1)

            def low_rank(j):
                pe.wait_ge(s["lora"], 2 * j + 2)
                for n, sem in enumerate((s["mmw"], s["mma"])):
                    for p in range(PAIRS):
                        last = pe.matmul(wide_ps(n)[:, p], wup[:, n, p * P:(p + 1) * P], lora[:, :], start=True, stop=True)
                    last.then_inc(sem, 1)

            def key_sums(j):
                pe.wait_ge(s["kkr"], j + 1)
                pe.matmul(bank[0][:, :], headones[:, :], kp[:, :, :].rearrange("p c j -> p (c j)"), start=True, stop=True).then_inc(s["ss"], 1)

            def body(i, first=False, last_block=False):
                m, prep = i - 1, not last_block
                if not first:
                    pe.wait_ge(s["st"], m + 1)
                    pe.wait_ge(s["kb"], 4 * m + 4)
                    pe.wait_ge(s["Sn"], i)
                for h in range(HEADS):
                    if h >= 4 and not first:
                        pe.wait_ge(s["lgt"], HEADS * m + h - 3)
                    if not first:
                        pe.matmul(bank[RING[h % 4]][:, 0:BAND], qs[:, h // 2, :], kb[:, h // 4, h % 2, :], start=True, stop=True).then_inc(s["qk"], 1)
                    if h == 3:
                        pe.wait_ge(s["va"], 2 * i + 2)
                        pe.wait_ge(s["rn"], 2 * i + 1)
                        for p in range(PAIRS):
                            last = pe.transpose(wide_ps(0)[:, p], rv[:, p], ident[:, :])
                        last.then_inc(s["tt"], 1)
                        pe.wait_ge(s["tha"], 4 * i + 4)
                        if not first:
                            pe.wait_ge(s["att"], m + 1)
                        pe.transpose(bank[1][:, 0:P], vas[:, :], ident[:, :]).then_inc(s["tt"], 1)
                pe.wait_ge(s["ar"], 4 * i + 4)
                pe.wait_ge(s["bk"], 2 * i + 2)
                for h in range(HEADS):
                    p = h // 2
                    if h < 4 and not first:
                        pe.wait_ge(s["lgt"], HEADS * m + 5 + h)
                    if h >= 4:
                        pe.wait_ge(s["msk"], HEADS * i + h - 3)
                    both = ar[:, p, h % 2].rearrange("k a j -> k (a j)")
                    pe.matmul(bank[RING[h % 4]][:, 0:2 * P], bt[:, p], both, start=True, stop=True)
                    pe.matmul(bank[RING[h % 4]][:, 2 * P:4 * P], kt[:, p], both, start=True, stop=True).then_inc(s["mmM"], 1)
                    if h == 3:
                        pe.wait_ge(s["tok"], 4 * i + 2)
                        for n, src in enumerate((bt, kt)):
                            for q in range(PAIRS):
                                last = pe.transpose(wide_ps(n)[:, q], src[:, q], ident[:, :])
                            last.then_inc(s["tt"], 1)
                if not first:
                    pe.wait_ge(s["fin"], m + 1)
                for g in range(2):
                    for h in range(g, HEADS, 2):
                        last = pe.matmul(wide_ps(5 + g)[:, h // 2], ar[:, h // 2, g, 0], bt[:, h // 2], start=True, stop=True)
                    last.then_inc(s["mmA"], 1)
                pe.wait_ge(s["msk"], HEADS * i + HEADS)
                for l in range(PASSES_0 if first else PASSES):
                    for g in range(2):
                        hs = range(4 * g, 4 * g + 4)
                        if l < PASSES - 1:
                            pe.wait_ge(s["tup"], updates(m) + (2 * g + 2 if l == 0 else 4 + 2 * (l - 1) + g + 1))
                        else:
                            pe.wait_ge(s["tinit"], 10 * m + 4 * g + 4)
                        for h in hs:
                            last = pe.matmul(wide_ps(3 + g)[:, h % 4], mats[:, h, 0, 0], Tm[:, h], start=True, stop=True)
                        last.then_inc(s["x1"], 1)
                        if l in TURNED:
                            for h in hs:
                                last = pe.transpose(wide_ps(7 if g == 0 else 2)[:, h % 4], Tm[:, h], ident[:, :])
                            last.then_inc(s["x1"], 1)
                    for g in range(2):
                        hs = range(4 * g, 4 * g + 4)
                        pe.wait_ge(s["x1c"], firsts(m, l, g, 1))
                        if l < PASSES - 1:
                            for h in hs:
                                last = pe.matmul(wide_ps(5 + g)[:, h % 4], TT[:, h], X1[:, h], start=True, stop=True)
                        if l >= PASSES - 2:
                            for h in hs:
                                last = pe.matmul(wide_ps(7 if g == 0 else 2)[:, h % 4], X1[:, h], TT[:, h], start=True, stop=True)
                        last.then_inc(s["yy"], 1)
                    if l == 0:
                        pe.wait_ge(s["tok"], 4 * i + 4)
                        if prep:
                            low_rank(i + 1)
                    if l == 1:
                        if prep:
                            pe.wait_ge(s["th"], 4 * i + 8)
                        pe.wait_ge(s["S0"], i + 1)
                        for h in range(HEADS):
                            o = wide_ps(0)[hp(h), h // 2]
                            pe.matmul(o, S0[:, h // 2], ar[:, h // 2, h % 2, 0], start=True, stop=False)
                            last = pe.matmul(o, rvtok[:, h // 2, hp(h)], mats[:, h, 1, 0], start=False, stop=True)
                        last.then_inc(s["W"], 1)
                    if l == 2:
                        pe.wait_ge(s["Wc"], 2 * i + 1)
                        if prep:
                            pe.wait_ge(s["tha"], 4 * i + 8)
                        for p in range(PAIRS):
                            last = pe.transpose(wide_ps(1)[:, p], WT[:, p], ident[:, :])
                        last.then_inc(s["W"], 1)
                    if l == 3 and prep:
                        key_sums(i + 1)
                if first:
                    for g in range(2):
                        pe.wait_ge(s["tup"], updates(m) + 4 + 2 * (PASSES_0 - 1) + g + 1)
                        for h in range(4 * g, 4 * g + 4):
                            last = pe.transpose(wide_ps(7 if g == 0 else 2)[:, h % 4], Tm[:, h], ident[:, :])
                        last.then_inc(s["x1"], 1)
                    key_sums(i + 1)
                pe.wait_ge(s["Wc"], 2 * i + 2)
                if first:
                    pe.wait_ge(s["x1c"], 4 * PASSES_0)
                else:
                    pe.wait_ge(s["tinit"], 10 * m + 10)
                for h in range(HEADS):
                    last = pe.matmul(bank[1][:, HD * h:HD * h + HD], TT[:, h], W[:, h], start=True, stop=True)
                last.then_inc(s["U"], 1)
                pe.wait_ge(s["Uc"], i + 1)
                apart(pe)
                for h in () if first else range(HEADS):
                    v_h = rvtok[:, h // 2, hp(h)]
                    o = wide_ps(3)[hp(h), h // 2]
                    pe.matmul(o, S0[:, h // 2], ar[:, h // 2, h % 2, 1], start=True, stop=False)
                    pe.matmul(o, U[:, h], mats[:, h, 0, 1], start=False, stop=False)
                    last = pe.matmul(o, v_h, mats[:, h, 1, 1], start=False, stop=True)
                if not first:
                    last.then_inc(s["Y"], 1)
                for h in range(HEADS):
                    o = bank[4][hp(h), HD * (h // 2):HD * (h // 2) + HD]
                    pe.matmul(o, btok[:, h // 2, hp(h)], U[:, h], start=True, stop=False)
                    last = pe.matmul(o, ktok[:, h // 2, hp(h)], rvtok[:, h // 2, hp(h)], start=False, stop=True)
                last.then_inc(s["S"], 1)
                if first:
                    return
                pe.wait_ge(s["Yc"], m + 1)
                pe.matmul(bank[5][:, :], headones[:, :], yT.rearrange("p c j -> p (c j)"), start=True, stop=True).then_inc(s["sums"], 1)
                pe.wait_ge(s["pn"], m + 1)
                if prep:
                    pe.wait_ge(s["rn"], 2 * i + 3)
                for n in range(4):
                    part, g = n // 2, n % 2
                    for h in range(4 * g, 4 * g + 4):
                        last = pe.transpose(wide_ps((0, 1, 2, 7)[n])[:, h % 4], lg[:, h, part * P:(part + 1) * P], ident[:, :])
                    last.then_inc(s["tp"], 1)
                pe.wait_ge(s["sqr"], m + 1)
                pe.matmul(bank[6][:, :], headones[:, :], tmp[:, :, :].rearrange("p c j -> p (c j)"), start=True, stop=True).then_inc(s["sums"], 1)
                pe.wait_ge(s["rk"], 4 * m + 4)
                pe.matmul(bank[5][:, :], headones[:, :], rkb[:, :, :].rearrange("p c j -> p (c j)"), start=True, stop=True).then_inc(s["sums"], 1)
                for g in range(2):
                    if g == 1:
                        pe.wait_ge(s["Sn"], i + 1)
                    for h in range(4 * g, 4 * g + 4):
                        last = pe.transpose(wide_ps(3 + g)[0:META, h % 4], lg[:, h, 2 * P:BAND], ident[:, :])
                    last.then_inc(s["tp"], 1)
                pe.wait_ge(s["sg"], m + 1)
                pe.wait_ge(s["vr"], m + 1)
                for p in range(PAIRS):
                    last = pe.matmul(wide_ps(6)[:, p], gup[:, p * P:(p + 1) * P], sg[:, :], start=True, stop=True)
                last.then_inc(s["mmg"], 1)
                pe.wait_ge(s["tpc"], 6 * m + 6)
                for g in range(KV):
                    for e in range(2):
                        o = wide_ps(1)[HD * e:HD * e + HD, 2 * g:2 * g + 2]
                        hs = slice(4 * g + e, 4 * g + 4, 2)
                        vc = slice(HD * g, HD * g + HD)
                        pe.matmul(o, vtok[:, 0, vc], pT[:, 0, hs], start=True, stop=False)
                        pe.matmul(o, vtok[:, 1, vc], pT[:, 1, hs], start=False, stop=False)
                        last = pe.matmul(o, vtok[0:META, 2, vc], pTm[:, hs], start=False, stop=True)
                last.then_inc(s["O"], 1)

            low_rank(0)
            pe.wait_ge(s["th"], 4)
            key_sums(0)
            body(0, first=True)
            with pe.Fori(1, NBLK - 1) as i:
                body(i)
            body(NBLK - 1, last_block=True)


def merge(nc, sems, t, d):
    lg0, lg1, lo0, lo1, xl0, xl1, mm, th, sm, dn = sems(*(f"g_{k}" for k in "lg0 lg1 lo0 lo1 xl0 xl1 mm th sm dn".split()))
    ldg, ldo = (lg0, lg1), (lo0, lo1)
    HALF = SEQ // 2
    CPL = 2
    UNITS = 2 * CPL * 2
    STEPS = KD // (2 * CPL)
    K2 = RD // P
    with ExitStack() as ctx:
        sb = lambda n, s, dt=F32: ctx.enter_context(nc.sbuf_tensor(n, s, dt))
        xnT = sb("xnT2", [P, KD, SEQ])
        w = sb("w_merge", [P, 2, 2 * KD + 2 * K2, CPL * P])
        bank = [ctx.enter_context(nc.psum_tensor(f"mrg_ps{n}", [P, 4, 512], F32)) for n in range(2)]
        cT = t["cT"]
        g2 = cT[:, CH_WA:CH_WA + 2, 0:2 * HALF].rearrange("p u (b j) -> p u b j", b=2)
        m2 = cT[:, CH_K, 0:2 * HALF].rearrange("p (b j) -> p b j", b=2)
        gates = d["w_in"].rearrange("l (c p) n -> p (l c) n", p=P)
        woa = d["w_o_attn"].rearrange("l (c p) n -> p (l c) n", p=P)
        wor = d["w_o_rwkv"].rearrange("l (c p) n -> p (l c) n", p=P)
        block = ctx.enter_context(nc.Block())

        @block.sync
        def _(sp):
            def load_out(half, j):
                c = bass.ds(j * P, CPL * P)
                sp.dma_start(w[:, half, 2 * KD:2 * KD + K2], woa[:, :, c]).then_inc(ldo[half], 16)
                sp.dma_start(w[:, half, 2 * KD + K2:], wor[:, :, c]).then_inc(ldo[half], 16)

            def load_gates(half, j):
                for b in range(2):
                    sp.dma_start(w[:, half, b * KD:(b + 1) * KD], gates[:, :, bass.ds(GATE0 + b * D + j * P, CPL * P)]).then_inc(ldg[half], 16)

            xsp = d["xn_spill"].rearrange("p (c j) -> p c j", c=KD)
            load_out(0, 0)
            load_gates(0, 0)
            for part, sem in enumerate((xl0, xl1)):
                c = slice(part * HALF, (part + 1) * HALF)
                sp.dma_start(xnT[:, :, c], xsp[:, :, c]).then_inc(sem, 16)
            load_out(1, CPL)
            load_gates(1, CPL)
            with sp.Fori(1, STEPS) as i:
                for half in range(2):
                    sp.wait_ge(mm, (i - 1) * UNITS + (half + 1) * UNITS // 2)
                    load_out(half, i * (2 * CPL) + half * CPL)
                    load_gates(half, i * (2 * CPL) + half * CPL)
            sp.dma_start(t["wout"][:, :, :], d["w_out"].rearrange("l (c p) n -> p (l c) n", p=P)).then_inc(t["wout_loaded"], 16)

        @block.tensor
        def _(pe):
            pe.sem_inc(dn, 2)
            with pe.Fori(0, STEPS) as i:
                for n in range(UNITS):
                    half, c, part = n // (2 * CPL), (n // 2) % CPL, n % 2
                    if n % (2 * CPL) == 0:
                        pe.wait_ge(ldo[half], (i + 1) * 32)
                    pe.wait_ge(dn, i * UNITS + n + 1)
                    wc = slice(c * P, (c + 1) * P)
                    rows = slice(part * HALF, (part + 1) * HALF)
                    real = slice(P + part * HALF, P + (part + 1) * HALF)
                    ps = bank[n % 2]
                    for b, ch in enumerate((CH_Q, CH_RR)):
                        for k in range(K2):
                            pe.matmul(ps[:, 2 + b], w[:, half, 2 * KD + b * K2 + k, wc], cT[:, ch + k, real],
                                      start=(k == 0), stop=(k == K2 - 1))
                    if n % (2 * CPL) == 0:
                        pe.wait_ge(ldg[half], (i + 1) * 32)
                    if n < 2:
                        pe.wait_ge(xl1 if part else xl0, 16)
                    for b in range(2):
                        for k in range(KD):
                            last = pe.matmul(ps[:, b], w[:, half, b * KD + k, wc], xnT[:, k, rows], start=(k == 0), stop=(k == KD - 1))
                    last.then_inc(mm, 1)

        @block.scalar
        def _(act):
            with act.Fori(0, STEPS) as i:
                for n in range(UNITS):
                    act.wait_ge(mm, i * UNITS + n + 1)
                    act.wait_ge(dn, i * UNITS + n + 1)
                    act.activation(g2[:, n % 2], bank[n % 2][:, 0:2], ACT.Tanh, scale=0.5).then_inc(th, 1)

        @block.vector
        def _(v):
            with v.Fori(0, STEPS) as i:
                for n in range(UNITS):
                    c, part = n // 2, n % 2
                    v.wait_ge(th, i * UNITS + n + 1)
                    v.wait_ge(dn, i * UNITS + n + 2)
                    for b in range(2):
                        v.scalar_tensor_tensor(m2[:, b], g2[:, n % 2, b], 1.0, bank[n % 2][:, 2 + b], ALU.add, ALU.mult).then_inc(sm, 1)
                    v.wait_ge(sm, (i * UNITS + n) * 2 + 2)
                    out = cT[:, bass.ds(CH_MIX + i * (2 * CPL) + c, 1), P + part * HALF:P + (part + 1) * HALF]
                    v.tensor_tensor(out.rearrange("p a j -> p (a j)"), m2[:, 0], m2[:, 1], ALU.add).then_inc(dn, 1)


def route(nc, sems, t, d):
    names = "r_ld r_x0 r_x1 r_ms r_mm r_h r_sq r_m r_sd r_xn r_st0 r_st1 r_tp r_xt r_lg r_e r_ex r_oh r_rk r_v"
    ld, x0, x1, msr, mm, hd, sqd, msd, sdd, xnd, st0, st1, tp, xt, lgd, eg, ex, oh, rk, own = sems(*names.split())
    NV = t["route_count"]
    tick = t["tick"]
    with ExitStack() as ctx:
        sb = lambda n, s, dt=F32: ctx.enter_context(nc.sbuf_tensor(n, s, dt))
        ident, cT = t["ident"], t["cT"]
        wout = t["wout"]
        wr = sb("w_router", [P, KD, NG + E])
        br = sb("b_router", [P, NG + E])
        gf = sb("g_ffn", [P, D])
        iota, before, ones = sb("iota", [P, E]), sb("before", [P, P]), sb("ones", [P, P])
        ms = sb("ms", [P, 2, KD, P])
        xb = sb("xb", [P, 2, D])
        h1 = sb("h1", [P, 2, D])
        xn = sb("xn2", [P, 2, D])
        sq = sb("sq2", [P, D])
        x2T = sb("x2T", [P, KD, P])
        sc = sb("sc", [P, 16])
        ss, rs, m0, sg, e2, dv, exv, g1, gidx, ones1 = (sc[:, n:n + 1] for n in range(10))
        gl8, el, m8 = sb("gl8", [P, 8]), sb("el", [P, NG, EG]), sb("m8", [P, 8])
        i8 = sb("i8", [P, 8], U32)
        pen, junk = sb("pen", [P, NG]), sb("junk", [P, 8])
        o12, om, pr = sb("o12", [P, TOPK, E]), sb("om", [P, E]), sb("pr", [P, TOPK, E])
        R, carry = sb("R", [P, E]), t["carry"]
        ps_h = [ctx.enter_context(nc.psum_tensor(f"h_ps{n}", [P, D], F32)) for n in range(2)]
        ps_t = ctx.enter_context(nc.psum_tensor("t_ps", [P, KD, P], F32))
        ps_l = ctx.enter_context(nc.psum_tensor("l_ps", [P, 512], F32))
        ps_r = ctx.enter_context(nc.psum_tensor("r_ps", [P, 512], F32))
        xv = d["x"].rearrange("b (n p) d -> (b n) p d", p=P)
        h1v, xn2v = (d[n].rearrange("(n p) d -> n p d", p=P) for n in ("h1_rows", "xn2_rows"))
        block = ctx.enter_context(nc.Block())
        STEPS = NB // 2

        @block.sync
        def _(sp):
            sp.dma_start(wr[:, :, 0:NG], d["w_grp"].rearrange("l (c p) n -> p (l c) n", p=P)).then_inc(ld, 16)
            sp.dma_start(wr[:, :, NG:], d["w_exp"].rearrange("l (c p) n -> p (l c) n", p=P)).then_inc(ld, 16)
            sp.dma_start(br[:, 0:NG], d["b_grp"][0:1, :].broadcast_to([P, NG])).then_inc(ld, 16)
            sp.dma_start(br[:, NG:], d["b_exp"][0:1, :].broadcast_to([P, E])).then_inc(ld, 16)
            sp.dma_start(gf[:, :], d["norm_ffn_g"][0:1, :].broadcast_to([P, D])).then_inc(ld, 16)
            sp.dma_start(iota[:, :], d["c_iota"]).then_inc(ld, 16)
            sp.dma_start(before[:, :], d["c_upper"][:, 0]).then_inc(ld, 16)
            with sp.Fori(0, STEPS) as i:
                for u, (sx, st) in enumerate(((x0, st0), (x1, st1))):
                    sp.wait_ge(hd, 2 * i + u + 1)
                    sp.dma_start(xb[:, u], xv[bass.ds(2 * i + u, 1)]).then_inc(sx, 16)
                for u, st in enumerate((st0, st1)):
                    sp.wait_ge(hd, 2 * i + u + 3)
                    sp.dma_start(h1v[bass.ds(2 * i + u, 1)], h1[:, u]).then_inc(st, 16)
                    sp.wait_ge(xnd, 2 * i + u + 1)
                    sp.dma_start(xn2v[bass.ds(2 * i + u, 1)], xn[:, u]).then_inc(st, 16)
            sp.wait_ge(st0, 32 * STEPS + 32)
            sp.wait_ge(st1, 32 * STEPS + 32)


        @block.scalar
        def _(act):
            act.sem_inc(mm, 2)

            def stationary(n, u):
                act.wait_ge(mm, n + 1)
                act.sem_inc(tick, 1)
                act.activation(ms[:, u], cT[:, CH_MIX:CH_MIX + KD, bass.ds(P + n * P, P)], ACT.Copy).then_inc(msr, 1)

            def norm(n, u):
                act.wait_ge(hd, n + 3)
                act.activation(sq[:, :], h1[:, u], ACT.Square, accum_out=ss).then_inc(sqd, 1)
                act.wait_ge(msd, n + 1)
                act.activation(rs, ss, ACT.Sqrt).then_inc(sdd, 1)

            def step(n, u, ahead=2):
                act.wait_ge(tp, n + 1)
                act.wait_ge(lgd, n + 1)
                act.activation(x2T[:, :, :], ps_t[:, :, :], ACT.Copy).then_inc(xt, 1)
                if ahead > 0:
                    norm(n + 1, (u + 1) % 2)
                if ahead > 1:
                    stationary(n + 2, u)
                act.wait_ge(eg, n + 1)
                act.activation(junk[:, :], gl8[:, :], ACT.Exp, bias=m0, accum_out=sg).then_inc(ex, 1)
                act.activation(exv, dv, ACT.Exp).then_inc(ex, 1)

            stationary(0, 0)
            stationary(1, 1)
            norm(0, 0)
            step(0, 0)
            with act.Fori(0, STEPS - 2) as i:
                for k in range(2):
                    step(2 * i + k + 1, (k + 1) % 2)
            for n in range(NB - 3, NB):
                step(n, n % 2, min(2, NB - 1 - n))

        @block.vector
        def _(v):
            v.memset(gl8[:, :], NEG).then_inc(own, 1)
            v.memset(ones[:, :], 1.0).then_inc(own, 1)
            v.memset(carry[:, :], 0.0).then_inc(own, 1)
            v.sem_inc(hd, 2)
            v.sem_inc(sdd, 1)
            v.sem_inc(lgd, 1)
            v.wait_ge(ld, 7 * 16)
            def norm(n, u, pair, link):
                v.wait_ge(x1 if u else x0, 16 * pair + 16)
                v.wait_ge(mm, n + 3)
                v.wait_ge(st1 if u else st0, 32 * pair + 32)
                for hf in range(2):
                    c = slice(hf * 512, hf * 512 + 512)
                    link.add(v.scalar_tensor_tensor(h1[:, u, c], ps_h[u][:, c], 0.5, xb[:, u, c], ALU.mult, ALU.add))
                link.join()
                v.sem_inc(hd, 1)
                v.wait_ge(sqd, n + 1)
                v.tensor_scalar(ss, ss, 1.0 / D, EPS, ALU.mult, ALU.add).then_inc(msd, 1)
                v.wait_ge(sdd, n + 2)
                link(v.reciprocal(rs, rs))
                v.scalar_tensor_tensor(xn[:, u], h1[:, u], rs, gf[:, :], ALU.mult, ALU.mult).then_inc(xnd, 1)

            def router(n, link):
                v.wait_ge(lgd, n + 2)
                link.add(v.tensor_tensor(gl8[:, 0:NG], ps_l[:, 0:NG], br[:, 0:NG], ALU.add))
                link(v.tensor_tensor(el[:, :, :].rearrange("p g e -> p (g e)"), ps_l[:, NG:NG + E], br[:, NG:], ALU.add))
                v.sem_inc(tick, 1)
                link(v.max(m8[:, :], gl8[:, :]))
                v.sem_inc(tick, 1)
                link.add(v.max_index(i8[:, :], m8[:, :], gl8[:, :]))
                link(v.tensor_scalar(m0, m8[:, 0:1], -1.0, None, ALU.mult))
                link(v.tensor_copy(gidx, i8[:, 0:1]))
                link(v.tensor_scalar(pen[:, :], iota[:, 0:NG], gidx, NEG, ALU.not_equal, ALU.mult))
                link(v.tensor_tensor(el[:, :, :], el[:, :, :], pen[:, :].unsqueeze(2).broadcast_to([P, NG, EG]), ALU.add))
                flat = el[:, :, :].rearrange("p g e -> p (g e)")
                v.sem_inc(tick, 1)
                link(v.max(m8[:, :], flat))
                v.sem_inc(tick, 1)
                link.add(v.max_index(i8[:, :], m8[:, :], flat))
                link(v.tensor_tensor(dv, m8[:, 1:2], m8[:, 0:1], ALU.subtract))
                v.sem_inc(eg, 1)
                e_n = t["eids"][:, bass.ds(n, 1), :].rearrange("p a k -> p (a k)")
                link(v.tensor_copy(e_n, i8[:, 0:TOPK]))
                for k in range(TOPK):
                    link.add(v.tensor_scalar(o12[:, k], iota[:, :], t["eids"][:, bass.ds(n, 1), k], None, ALU.is_equal))
                link.join()
                v.tensor_tensor(om[:, :], o12[:, 0], o12[:, 1], ALU.add).then_inc(oh, 1)
                v.wait_ge(ex, 2 * n + 2)
                link(v.tensor_scalar(g1, exv, 1.0, None, ALU.add))
                link(v.tensor_tensor(g1, g1, sg, ALU.mult))
                link(v.reciprocal(g1, g1))
                link.add(v.tensor_scalar(t["wts"][:, bass.ds(n, 1), 0], g1, 0.5, None, ALU.mult))
                link(v.tensor_scalar(t["wts"][:, bass.ds(n, 1), 1], g1, exv, 0.5, ALU.mult, ALU.mult))

            def ranks(n, link):
                v.wait_ge(rk, n + 1)
                link(v.tensor_tensor(R[:, :], ps_r[:, 0:E], carry[:, :], ALU.add))
                link.add(v.tensor_tensor(pr[:, :, :], o12[:, :, :], R[:, :].unsqueeze(1).broadcast_to([P, TOPK, E]), ALU.mult))
                link(v.tensor_tensor(carry[:, :], carry[:, :], ps_r[:, E:2 * E], ALU.add))
                link(v.tensor_reduce(t["ranks"][:, bass.ds(n, 1), :].rearrange("p a k -> p (a k)"), pr[:, :, :], AX.X, ALU.add))

            link = Chain(v, own, 3)
            norm(0, 0, 0, link)
            norm(1, 1, 0, link)
            router(0, link)
            base = 3 + link.n
            with v.Fori(0, STEPS - 1) as i:
                link = Chain(v, own, i * NV + base)
                for k in range(2):
                    n = 2 * i + k + 1
                    norm(n + 1, k, i + 1, link)
                    ranks(n - 1, link)
                    router(n, link)
            assert link.n == NV, link.n
            link = Chain(v, own, (STEPS - 1) * NV + base)
            ranks(NB - 2, link)
            router(NB - 1, link)
            ranks(NB - 1, link)

        @block.gpsimd
        def _(pool):
            pool.sem_inc(st0, 32)
            pool.sem_inc(st1, 32)

        @block.tensor
        def _(pe):
            pe.wait_ge(ld, 7 * 16)
            pe.wait_ge(t["wout_loaded"], 16)
            pe.wait_ge(own, 3)

            def product(n, u):
                pe.wait_ge(msr, n + 1)
                pe.wait_ge(hd, n + 1)
                for hf in range(2):
                    for k in range(KD):
                        last = pe.matmul(ps_h[u][:, hf * 512:hf * 512 + 512], ms[:, u, k], wout[:, k, hf * 512:hf * 512 + 512],
                                         start=(k == 0), stop=(k == KD - 1))
                last.then_inc(mm, 1)

            def router(n, u):
                pe.wait_ge(xnd, n + 1)
                for k in range(KD):
                    last = pe.transpose(ps_t[:, k], xn[:, u, k * P:(k + 1) * P], ident[:, :])
                last.then_inc(tp, 1)
                pe.wait_ge(xt, n + 1)
                for k in range(KD):
                    last = pe.matmul(ps_l[:, 0:NG + E], x2T[:, k], wr[:, k], start=(k == 0), stop=(k == KD - 1))
                last.then_inc(lgd, 1)

            def ranks(n):
                pe.wait_ge(oh, n + 1)
                pe.matmul(ps_r[:, 0:E], before[:, :], om[:, :], start=True, stop=True)
                pe.matmul(ps_r[:, E:2 * E], ones[:, :], om[:, :], start=True, stop=True).then_inc(rk, 1)

            product(0, 0)
            product(1, 1)
            router(0, 0)
            with pe.Fori(0, STEPS - 1) as i:
                for k in range(2):
                    n = 2 * i + k + 1
                    product(n + 1, k)
                    ranks(n - 1)
                    router(n, (k + 1) % 2)
            ranks(NB - 2)
            router(NB - 1, (NB - 1) % 2)
            ranks(NB - 1)


def table(nc, sems, t, d):
    ld, own, zs, sc, sl, known = sems("t_ld", "t_own", "t_zs", "t_sc", "t_sl", "t_known")
    R2 = NB * TOPK
    with ExitStack() as ctx:
        sb = lambda n, s, dt=F32: ctx.enter_context(nc.sbuf_tensor(n, s, dt))
        iota, over, blockno = sb("iota_t", [P, E]), sb("over", [P, NB]), sb("blockno", [P, BLOCKS])
        tokno = sb("tokno", [P, NB], I32)
        zero = sb("zero", [P, BLOCKS], I32)
        cmp, nblk, end, start = sb("cmp", [P, E, NB]), sb("nblk", [P, E]), sb("end", [P, E]), sb("start", [P, E])
        one = sb("one_t", [P, E])
        oh, rb, pos = sb("oh_t", [P, R2, E]), sb("rb", [P, R2]), sb("pos", [P, R2])
        rc = sb("rc", [P, R2, NB])
        sidx = sb("sidx", [P, R2], I32)
        be, bc = sb("be", [1, BLOCKS]), sb("bc", [1, BLOCKS, E])
        block = ctx.enter_context(nc.Block())
        eids, ranks = (t[n][:, :, :].rearrange("p n k -> p (n k)") for n in ("eids", "ranks"))

        @block.sync
        def _(sp):
            sp.dma_start(iota[:, :], d["c_iota"]).then_inc(ld, 16)
            sp.dma_start(over[:, :], d["c_over"]).then_inc(ld, 16)
            sp.dma_start(blockno[:, :], d["c_blockno"]).then_inc(ld, 16)
            sp.dma_start(tokno[:, :], d["c_tokno"]).then_inc(ld, 16)
            sp.wait_ge(own, 1)
            sp.dma_start(d["slot_tok"].rearrange("(p b) a -> p (b a)", p=P), zero[:, :]).then_inc(zs, 16)
            sp.wait_ge(known, 1)
            for n in range(EARLY):
                load_weights(sp, t, d, sp.value_load(t["bexp"][0:1, n:n + 1], min_val=0, max_val=E - 1), n)
            sp.wait_ge(sc, 16 * R2)
            sp.dma_start(t["slots"][:, 0:BLOCKS], d["slot_tok"].rearrange("(p b) a -> p (b a)", p=P)).then_inc(sl, 16)
            sp.wait_ge(sl, 16)

        @block.vector
        def _(v):
            link = Chain(v, own)
            link.add(v.memset(zero[:, :], 0))
            link.add(v.memset(t["slots"][:, BLOCKS:], 0))
            link.add(v.memset(t["wts"][:, NB:], 0.0))
            link(v.memset(one[:, :], 1.0))
            v.wait_ge(ld, 64)
            wide = lambda x, n: x.unsqueeze(2).broadcast_to([P, x.shape[1], n])
            rows = lambda x, n: x.unsqueeze(1).broadcast_to([P, n, x.shape[1]])
            link(v.tensor_tensor(cmp[:, :, :], wide(t["carry"][:, :], NB), rows(over[:, :], E), ALU.is_gt))
            link(v.tensor_reduce(nblk[:, :], cmp[:, :, :], AX.X, ALU.add))
            link(v.tensor_tensor_scan(end[:, :], one[:, :], nblk[:, :], 0.0, ALU.mult, ALU.add))
            link(v.tensor_tensor(start[:, :], end[:, :], nblk[:, :], ALU.subtract))
            link(v.tensor_copy(t["used"][:, :], end[0:1, E - 1:E]))
            link(v.tensor_tensor(bc[:, :, :], end[0:1, :].unsqueeze(1).broadcast_to([1, BLOCKS, E]),
                                 blockno[0:1, :].unsqueeze(2).broadcast_to([1, BLOCKS, E]), ALU.is_le))
            link(v.tensor_reduce(be[:, :], bc[:, :, :], AX.X, ALU.add))
            link(v.tensor_scalar(t["bexp"][:, :], be[:, :], float(E - 1), None, ALU.min))
            v.sem_inc(known, 1)
            link(v.tensor_tensor(oh[:, :, :], wide(eids, E), rows(iota[:, :], R2), ALU.is_equal))
            link(v.tensor_tensor(oh[:, :, :], oh[:, :, :], rows(start[:, :], R2), ALU.mult))
            link(v.tensor_reduce(rb[:, :], oh[:, :, :], AX.X, ALU.add))
            link(v.tensor_tensor(rc[:, :, :], wide(ranks, NB), rows(over[:, :], R2), ALU.is_ge))
            link(v.tensor_reduce(pos[:, :], rc[:, :, :], AX.X, ALU.add))
            link(v.tensor_scalar(pos[:, :], pos[:, :], 1.0, None, ALU.subtract))
            link(v.tensor_tensor(rb[:, :], rb[:, :], pos[:, :], ALU.add))
            link(v.scalar_tensor_tensor(pos[:, :], pos[:, :], -float(P), ranks, ALU.mult, ALU.add))
            link.add(v.scalar_tensor_tensor(sidx[:, :], pos[:, :], float(BLOCKS), rb[:, :], ALU.mult, ALU.add))
            link(v.scalar_tensor_tensor(t["ydest"][:, :], rb[:, :], float(P), pos[:, :], ALU.mult, ALU.add))
            t["table_own"] = link.n

        @block.gpsimd
        def _(pool):
            pool.wait_ge(own, t["table_own"])
            pool.wait_ge(zs, 16)
            for n in range(R2):
                pool.indirect_dma_start(d["slot_tok"], bass.IndirectOffsetOnAxis(sidx[:, n:n + 1], 0),
                                        tokno[:, n // TOPK:n // TOPK + 1], None).then_inc(sc, 16)


def load_weights(sp, t, d, e, u):
    eg, eu = (d[n].rearrange("l e (p c) f -> (l e) p (c f)", p=P) for n in ("e_gate", "e_up"))
    ed = d["e_down"].rearrange("l e (p c) n -> (l e) p (c n)", p=P)
    sp.dma_start(t["w_gu"][:, u, 0].rearrange("p c f -> p (c f)"), eg[bass.ds(e, 1)]).then_inc(t["wgu"][u], 16)
    sp.dma_start(t["w_gu"][:, u, 1].rearrange("p c f -> p (c f)"), eu[bass.ds(e, 1)]).then_inc(t["wgu"][u], 16)
    sp.dma_start(t["w_dn"][:, u].rearrange("p c n -> p (c n)"), ed[bass.ds(e, 1)]).then_inc(t["wdn"][u], 16)


def experts(nc, sems, t, d):
    wgu, wdn = t["wgu"], t["wdn"]
    xg, yst = sems(*(f"e_xg{u}" for u in range(DEPTH_W))), sems("e_yst0", "e_yst1")
    ix, tp, xt, mm, th, hm, ht, hc, dm, ye, own = sems(*(f"e_{k}" for k in "ix tp xt mm th hm ht hc dm ye own".split()))
    FK = F // P
    tick = t["tick"]
    with ExitStack() as ctx:
        sb = lambda n, s, dt=F32: ctx.enter_context(nc.sbuf_tensor(n, s, dt))
        ident = t["ident"]
        w, wd = t["w_gu"], t["w_dn"]
        idx = [sb(f"idx{u}", [P, 1], I32) for u in range(DEPTH_W)]
        xr = [sb(f"xr{u}", [P, D]) for u in range(DEPTH_W)]
        xT = sb("xT", [P, 2, KD, P])
        sg, hmid = sb("sg_e", [P, 2, F]), sb("hmid", [P, 2, F])
        hT = sb("hT", [P, 2, FK, P])
        y = sb("y", [P, 2, D])
        ps_x = ctx.enter_context(nc.psum_tensor("x_ps", [P, KD, P], F32))
        ps_h = ctx.enter_context(nc.psum_tensor("hh_ps", [P, 2, 2, F], F32))
        ps_t = ctx.enter_context(nc.psum_tensor("ht_ps", [P, 512], F32))
        ps_y = ctx.enter_context(nc.psum_tensor("y_ps", [P, D], F32))
        yv = d["y_rows"].rearrange("(n p) d -> n p d", p=P)
        block = ctx.enter_context(nc.Block())

        def turns(n):
            return n // DEPTH_W + 1

        def both(eng, run):
            used = eng.value_load(t["used"][0:1, 0:1], min_val=0, max_val=BLOCKS)
            run(0, SURE)
            with eng.If(used > SURE):
                run(SURE, BLOCKS)
            apart(eng)

        def apart(eng):
            eng.sem_inc(tick, 1)

        @block.sync
        def _(sp):
            def store(n, u):
                sp.wait_ge(ye, 2 * n + 3)
                sp.dma_start(yv[bass.ds(n, 1)], y[:, u % 2]).then_inc(yst[u % 2], 16)

            sp.sem_inc(yst[0], 16)
            sp.sem_inc(yst[1], 16)

            def run(lo, hi):
                for n in range(lo or EARLY, lo + DEPTH_W):
                    e = sp.value_load(t["bexp"][0:1, n:n + 1], min_val=0, max_val=E - 1)
                    if lo:
                        sp.wait_ge(dm, n - 1)
                    else:
                        sp.wait_ge(xg[n - EARLY], 16)
                    load_weights(sp, t, d, e, n % DEPTH_W)
                with sp.Fori(lo // DEPTH_W + 1, hi // DEPTH_W) as i:
                    for u in range(DEPTH_W):
                        n = i * DEPTH_W + u
                        e = sp.value_load(t["bexp"][0:1, bass.ds(n, 1)], min_val=0, max_val=E - 1)
                        sp.wait_ge(dm, n - 1)
                        load_weights(sp, t, d, e, u)
                        store(n - DEPTH_W, u)
                if not lo:
                    sp.dma_start(t["h1_sb"][:, :, :], d["h1_rows"].rearrange("(n p) d -> p n d", p=P)).then_inc(t["h1_loaded"], 16)
                for n in range(hi - DEPTH_W, hi):
                    store(n, n % DEPTH_W)
                for k in range(2):
                    sp.wait_ge(yst[k], 16 * (hi // 2 + 1))

            both(sp, run)
            sp.wait_ge(t["h1_loaded"], 16)

        @block.gpsimd
        def _(pool):
            for u in range(DEPTH_W):
                pool.tensor_copy(idx[u][:, :], t["slots"][:, u:u + 1]).then_inc(ix, 1)

            def run(lo, hi):
                with pool.Fori(lo // DEPTH_W, hi // DEPTH_W) as i:
                    for u in range(DEPTH_W):
                        n = i * DEPTH_W + u
                        pool.wait_ge(ix, n + 1)
                        pool.wait_ge(tp, n + 1)
                        pool.sem_inc(tick, 1)
                        pool.indirect_dma_start(xr[u][:, :], None, d["xn2_rows"], bass.IndirectOffsetOnAxis(idx[u][:, :], 0)).then_inc(xg[u], 16)
                        pool.wait_ge(xg[u], 16 * i + 16)
                        nxt = t["slots"][:, bass.ds(n + DEPTH_W, 1)]
                        pool.tensor_copy(idx[u][:, :], nxt).then_inc(ix, 1)

            both(pool, run)

        @block.tensor
        def _(pe):
            pe.sem_inc(tp, DEPTH_W)
            pe.sem_inc(dm, 2)
            pe.sem_inc(xt, 2)

            def turn(n, u, i):
                pe.wait_ge(xg[u], i)
                pe.wait_ge(xt, 2 * n + 2)
                for k in range(KD):
                    last = pe.transpose(ps_x[:, k], xr[u][:, k:D:KD], ident[:, :])
                last.then_inc(tp, 1)

            def up(n, u, i):
                pe.wait_ge(wgu[u], i)
                pe.wait_ge(xt, 2 * n + 4)
                pe.wait_ge(hm, n + 1)
                for k in range(KD):
                    last = pe.matmul(ps_h[:, u % 2].rearrange("p a f -> p (a f)"), xT[:, u % 2, k], w[:, u, :, k], start=(k == 0), stop=(k == KD - 1))
                last.then_inc(mm, 1)

            def turn_hidden(n, u):
                pe.wait_ge(hm, n + 3)
                pe.wait_ge(hc, n + 1)
                for k in range(FK):
                    last = pe.transpose(ps_t[:, k * P:(k + 1) * P], hmid[:, u % 2, k:F:FK], ident[:, :])
                last.then_inc(ht, 1)

            def down(n, u, i):
                pe.wait_ge(wdn[u], i)
                pe.wait_ge(hc, n + 2)
                pe.wait_ge(ye, 2 * n + 1)
                for hf in range(2):
                    c = slice(hf * 512, hf * 512 + 512)
                    for k in range(FK):
                        last = pe.matmul(ps_y[:, c], hT[:, u % 2, k], wd[:, u, k, c], start=(k == 0), stop=(k == FK - 1))
                last.then_inc(dm, 1)

            def step(n, u, rounds):
                up(n, u, 32 * rounds[0])
                down(n - 1, (u - 1) % DEPTH_W, 16 * rounds[1])
                if rounds[2] is not None:
                    turn(n + 1, (u + 1) % DEPTH_W, 16 * rounds[2])
                turn_hidden(n, u)

            def run(lo, hi):
                turn(lo, 0, 16 * turns(lo))
                up(lo, 0, 32 * turns(lo))
                turn(lo + 1, 1, 16 * turns(lo + 1))
                turn_hidden(lo, 0)
                last_turn = hi // DEPTH_W - 1
                with pe.Fori(lo // DEPTH_W, last_turn) as i:
                    for u in range(1, DEPTH_W + 1):
                        n = i * DEPTH_W + u
                        step(n, u % DEPTH_W, [i + 1 + (u + k) // DEPTH_W for k in (0, -1, 1)])
                for n in range(last_turn * DEPTH_W + 1, hi):
                    step(n, n % DEPTH_W, [turns(n), turns(n - 1), turns(n + 1) if n + 1 < hi else None])
                down(hi - 1, (hi - 1) % DEPTH_W, 16 * turns(hi - 1))

            both(pe, run)

        @block.scalar
        def _(act):
            def take_x(n, u):
                act.wait_ge(tp, n + DEPTH_W + 1)
                act.wait_ge(mm, n + 1)
                for hf in range(2):
                    c = slice(hf * KD // 2, (hf + 1) * KD // 2)
                    act.activation(xT[:, u % 2, c], ps_x[:, c], ACT.Copy).then_inc(xt, 1)

            act.sem_inc(mm, 2)
            act.sem_inc(hc, 1)

            def body(n, u, i, more=True):
                act.wait_ge(mm, n + 3)
                act.wait_ge(hm, n + 1)
                act.activation(sg[:, u % 2], ps_h[:, u % 2, 0], ACT.Tanh, scale=0.5).then_inc(th, 1)
                if more:
                    take_x(n + 1, u + 1)
                act.wait_ge(ht, n + 1)
                act.wait_ge(dm, n + 1)
                act.activation(hT[:, u % 2].rearrange("p k j -> p (k j)"), ps_t[:, 0:F], ACT.Copy).then_inc(hc, 1)

            def run(lo, hi):
                take_x(lo, 0)
                with act.Fori(lo // DEPTH_W, hi // DEPTH_W - 1) as i:
                    for u in range(DEPTH_W):
                        body(i * DEPTH_W + u, u, i)
                for n in range(hi - DEPTH_W, hi):
                    body(n, n % DEPTH_W, None, n + 1 < hi)

            both(act, run)

        @block.vector
        def _(v):
            v.sem_inc(hm, 2)
            v.sem_inc(ye, 1)

            def hidden(n, u):
                v.wait_ge(th, n + 1)
                v.scalar_tensor_tensor(sg[:, u % 2], sg[:, u % 2], 1.0, ps_h[:, u % 2, 0], ALU.add, ALU.mult).then_inc(own, 1)
                v.wait_ge(own, n + 1)
                v.tensor_tensor(hmid[:, u % 2], sg[:, u % 2], ps_h[:, u % 2, 1], ALU.mult).then_inc(hm, 1)

            def take_y(n, u, rounds):
                v.wait_ge(dm, n + 3)
                v.wait_ge(yst[u % 2], 16 * rounds)
                for hf in range(2):
                    c = slice(hf * 512, hf * 512 + 512)
                    v.tensor_copy(y[:, u % 2, c], ps_y[:, c]).then_inc(ye, 1)

            def run(lo, hi):
                hidden(lo, 0)
                last_turn = hi // DEPTH_W - 1
                with v.Fori(lo // DEPTH_W, last_turn) as i:
                    for u in range(1, DEPTH_W + 1):
                        n = i * DEPTH_W + u
                        hidden(n, u % DEPTH_W)
                        take_y(n - 1, (u - 1) % DEPTH_W, i * 2 + (u - 1) // 2 + 1)
                for n in range(last_turn * DEPTH_W + 1, hi):
                    hidden(n, n % DEPTH_W)
                    take_y(n - 1, (n - 1) % DEPTH_W, (n - 1) // 2 + 1)
                take_y(hi - 1, (hi - 1) % DEPTH_W, (hi - 1) // 2 + 1)

            both(v, run)


def combine(nc, sems, t, d):
    DEPTH = 4
    names = "ld s0 s1 sm sq sd own ms dg mm".split()
    ld, s0, s1, smd, sqd, sdd, own, msd, dg, mm = sems(*(f"c_{k}" for k in names))
    rows = sems(*(f"c_rows{u}" for u in range(DEPTH)))
    NV = t["combine_count"]
    with ExitStack() as ctx:
        sb = lambda n, s, dt=F32: ctx.enter_context(nc.sbuf_tensor(n, s, dt))
        ident, h = t["ident"], t["h1_sb"]
        g = sb("g_final", [P, D])
        ya = [[sb(f"y{n}_{k}", [P, D]) for k in range(TOPK)] for n in range(NB)]
        diag = sb("diag", [P, 2, TOPK, P])
        o = sb("o_c", [P, 2, D])
        sq = sb("sq_c", [P, D])
        sc = sb("sc_c", [P, 2, 2])
        ps_y, ps_s = (ctx.enter_context(nc.psum_tensor(n, [P, 2, D], F32)) for n in ("yy_ps", "sum_ps"))
        ov = d["out"].rearrange("b (n p) d -> (b n) p d", p=P)
        block = ctx.enter_context(nc.Block())

        @block.sync
        def _(sp):
            sp.dma_start(g[:, :], d["norm_final_g"].rearrange("(a n) -> a n", a=1).broadcast_to([P, D])).then_inc(ld, 16)
            with sp.Fori(0, NB // 2) as i:
                for u, st in enumerate((s0, s1)):
                    sp.wait_ge(msd, 2 * i + u + 1)
                    sp.dma_start(ov[bass.ds(2 * i + u, 1)], o[:, u]).then_inc(st, 16)
            sp.wait_ge(s0, 16 * (NB // 2) + 16)
            sp.wait_ge(s1, 16 * (NB // 2) + 16)

        @block.gpsimd
        def _(pool):
            pool.sem_inc(s0, 16)
            pool.sem_inc(s1, 16)
            for n in range(NB):
                if n >= DEPTH:
                    pool.wait_ge(rows[n % DEPTH], 32 * (n // DEPTH))
                for k in range(TOPK):
                    pool.indirect_dma_start(ya[n][k][:, :], None, d["y_rows"],
                                            bass.IndirectOffsetOnAxis(t["ydest"][:, n * TOPK + k:n * TOPK + k + 1], 0)).then_inc(rows[n % DEPTH], 16)

        @block.tensor
        def _(pe):
            for n in range(NB):
                pe.wait_ge(dg, 2 * n + 2)
                pe.wait_ge(rows[n % DEPTH], 32 * (n // DEPTH) + 32)
                if n >= 2:
                    pe.wait_ge(smd, n - 1)
                for hf in range(2):
                    c = slice(hf * 512, hf * 512 + 512)
                    for k in range(TOPK):
                        last = pe.matmul(ps_y[:, n % 2, c], diag[:, n % 2, k], ya[n][k][:, c], start=(k == 0), stop=(k == TOPK - 1))
                last.then_inc(mm, 1)

        @block.scalar
        def _(act):
            with act.Fori(0, NB // 2) as i:
                for u in range(2):
                    n = 2 * i + u
                    act.wait_ge(smd, n + 1)
                    act.activation(sq[:, :], ps_s[:, u], ACT.Square, accum_out=sc[:, u, 0:1]).then_inc(sdd, 1)
                    act.wait_ge(sqd, n + 1)
                    act.activation(sc[:, u, 1:2], sc[:, u, 0:1], ACT.Sqrt).then_inc(sdd, 1)

        @block.vector
        def _(v):
            def diagonals(n, u):
                for k in range(TOPK):
                    v.tensor_scalar(diag[:, u, k], ident[:, :], t["wts"][:, bass.ds(n, 1), k], None, ALU.mult).then_inc(dg, 1)

            def add_up(n, u, link):
                v.wait_ge(mm, n + 1)
                diagonals(n + 1, (u + 1) % 2)
                v.wait_ge(mm, n + 2)
                hn = h[:, bass.ds(n, 1)].rearrange("p a d -> p (a d)")
                for hf in range(2):
                    c = slice(hf * 512, hf * 512 + 512)
                    link.add(v.tensor_tensor(ps_s[:, u, c], ps_y[:, u, c], hn[:, c], ALU.add))
                link.join()
                v.sem_inc(smd, 1)

            def norm(n, u, pair, link):
                v.wait_ge(sdd, 2 * n + 1)
                v.tensor_scalar(sc[:, u, 0:1], sc[:, u, 0:1], 1.0 / D, EPS, ALU.mult, ALU.add).then_inc(sqd, 1)
                v.wait_ge(sdd, 2 * n + 2)
                link(v.reciprocal(sc[:, u, 1:2], sc[:, u, 1:2]))
                v.wait_ge(s1 if u else s0, 16 * pair + 16)
                for hf in range(2):
                    c = slice(hf * 512, hf * 512 + 512)
                    link.add(v.scalar_tensor_tensor(o[:, u, c], ps_s[:, u, c], sc[:, u, 1:2], g[:, c], ALU.mult, ALU.mult))
                link.join()
                v.sem_inc(msd, 1)

            v.sem_inc(mm, 1)
            v.wait_ge(ld, 16)
            v.wait_ge(t["h1_loaded"], 16)
            diagonals(0, 0)
            link = Chain(v, own)
            add_up(0, 0, link)
            base = link.n
            pairs = NB // 2
            with v.Fori(0, pairs - 1) as i:
                link = Chain(v, own, i * NV + base)
                for u in range(2):
                    add_up(2 * i + u + 1, (u + 1) % 2, link)
                    norm(2 * i + u, u, i, link)
            assert link.n == NV, link.n
            link = Chain(v, own, (pairs - 1) * NV + base)
            add_up(NB - 1, 1, link)
            norm(NB - 2, 0, pairs - 1, link)
            norm(NB - 1, 1, pairs - 1, link)


def program(nc, d):
    with ExitStack() as ctx:
        def sems(*names):
            return [ctx.enter_context(nc.semaphore(n)) for n in names]

        sb = lambda n, s, dt=F32: ctx.enter_context(nc.sbuf_tensor(n, s, dt))

        t = {"ident": sb("ident", [P, P]), "carry": sb("carry", [P, E]), "eids": sb("eids", [P, NB, TOPK]),
             "ranks": sb("ranks", [P, NB, TOPK]), "wts": sb("wts", [P, NB + 1, TOPK]), "bexp": sb("bexp", [1, BLOCKS], I32), "used": sb("used", [1, 1], I32),
             "slots": sb("slots", [P, BLOCKS + 4], I32), "ydest": sb("ydest", [P, NB * TOPK], I32)}
        t["tick"], = sems("tick")
        t["mix_counts"] = (41, 3)
        t["route_count"] = 52
        t["combine_count"] = 10
        with nc.sbuf_tensor("cT", [P, CHUNKS, TP], F32) as cT:
            t["cT"] = cT
            t["spilled"], *t["w_in_loaded"] = sems("spilled", "w_in_0", "w_in_1")
            t["w_cols"] = 2 * P
            with nc.sbuf_tensor("xnT", [P, KD, TG], F32) as xnT, nc.sbuf_tensor("w_in_sb", [P, 2, KD, t["w_cols"]], F32) as w_in_sb:
                t["xnT"], t["w_in_sb"] = xnT, w_in_sb
                norm_and_turn(nc, sems, t, d)
                project(nc, sems, t, d)
            t["y_zeroed"], = sems("y_zeroed")
            mix(nc, sems, t, d)
            t["wout_loaded"], = sems("wout_loaded")
            with nc.sbuf_tensor("wout", [P, KD, D], F32) as wout:
                t["wout"] = wout
                merge(nc, sems, t, d)
                route(nc, sems, t, d)
        t["wgu"], t["wdn"] = (sems(*(f"e_{k}{u}" for u in range(DEPTH_W))) for k in ("wgu", "wdn"))
        t["h1_loaded"], = sems("h1_loaded")
        t["h1_sb"] = sb("h1_sb", [P, NB, D])
        with nc.sbuf_tensor("w_gu", [P, DEPTH_W, 2, KD, F], F32) as w_gu, nc.sbuf_tensor("w_dn", [P, DEPTH_W, F // P, D], F32) as w_dn:
            t["w_gu"], t["w_dn"] = w_gu, w_dn
            table(nc, sems, t, d)
            experts(nc, sems, t, d)
        combine(nc, sems, t, d)


_INS = ["x", "meta_tokens", "norm_mix_g", "w_in", "shift_mu", "w0", "w_decay_up", "a0", "w_aaa_up", "w_gate_up",
        "k_k", "k_a", "r_k", "ln_x_g", "ln_x_b", "attn_sinks", "w_o_attn", "w_o_rwkv", "w_out", "norm_ffn_g",
        "w_grp", "b_grp", "w_exp", "b_exp", "e_gate", "e_up", "e_down", "norm_final_g"]


def kernel(**inputs):
    import numpy as _np
    import concourse.bacc as _bacc
    from concourse import mybir as _mybir
    from concourse.bass_utils import run_bass_kernel_spmd as _run

    nc = _bacc.Bacc("TRN2", target_bir_lowering=False, num_devices=1)
    arrays, d = {}, {}
    named = [(n, inputs[n]) for n in _INS] + [("c_" + n, a) for n, a in constants().items()]
    for name, a in named:
        a = _np.ascontiguousarray(a)
        arrays["in_" + name] = a
        d[name] = nc.dram_tensor("in_" + name, a.shape, _mybir.dt.from_np(a.dtype), kind="ExternalInput").ap()
    d["out"] = nc.dram_tensor("out", (1, SEQ, D), F32, kind="ExternalOutput").ap()
    for name, shape, dt in SCRATCH:
        d[name] = nc.dram_tensor(name, shape, dt, kind="Internal").ap()
    program(nc, d)
    r = _run(nc, [arrays], core_ids=[0])
    return r.results[0]["out"]


SCRATCH = [("xn_spill", (P, KD * SEQ), F32), ("xn2_rows", (SEQ, D), F32), ("h1_rows", (SEQ, D), F32),
           ("slot_tok", (BLOCKS * P, 1), I32), ("y_rows", (BLOCKS * P, D), F32)]
```

```python
from contextlib import ExitStack

import numpy as np
import concourse.bass as bass
from concourse import mybir

F32 = mybir.dt.float32
F32R = mybir.dt.float32r
I32 = mybir.dt.int32
U32 = mybir.dt.uint32
U8 = mybir.dt.uint8
ACT = mybir.ActivationFunctionType
ALU = mybir.AluOpType
AX = mybir.AxisListType

P = 128
D = 1024
KD = D // P
SEQ = 1024
META = 16
NB = SEQ // P
T = META + SEQ
PAD = P - META
TP = T + PAD
NBLK = TP // P
GROUP = 348
NGROUPS = 3
TG = GROUP * NGROUPS
HEADS = 8
HD = 64
PAIRS = HEADS // 2
KV = 2
RD = HEADS * HD
SCALE = HD ** -0.5
BAND = 2 * P + META
CH_Q, CH_K, CH_V, CH_RR, CH_RK, CH_RV, CH_WA, CH_G, CHUNKS = 0, 4, 5, 6, 10, 14, 18, 19, 20
CH_MIX = CH_RK
GATE0 = CHUNKS * P
EPS = 1e-6
LN_EPS = 64e-5
DECAY = float(np.exp(-0.5))
E = 32
NG = 4
EG = E // NG
F = 256
TOPK = 2
BLOCKS = -(-(SEQ * TOPK + E * (P - 1)) // P)
SURE = E
DEPTH_W = 4
MIX_LOADS = 16
EARLY = 2
NEG = -1e30
LEVELS = [1, 2, 4, 8, 16]


def constants():
    i = np.arange(P)
    row, col = i[:, None], i[None, :]
    c = {}
    c["ident"] = np.eye(P, dtype=np.float32)
    c["headones"] = (row // HD == col // HD).astype(np.float32)
    upper = np.stack([row < col, row <= col], 1)
    c["upper"] = upper.astype(np.float32)
    c["lower"] = (row > col).astype(np.float32)
    low = [((row // n) % 2 == 1) & (col // n == row // n - 1) for n in LEVELS]
    c["lev"] = np.stack([np.stack([m, m.T], 1) for m in low], 1).astype(np.float32)
    q, k = np.arange(P)[:, None], np.arange(2 * P)[None, :]
    diff = q + P - k
    m = np.arange(META)[None, :]
    slopes = 2.0 ** (-8.0 * (np.arange(HEADS) + 1) / HEADS)
    bias = np.zeros((NBLK, P, HEADS, BAND), np.float32)
    for b in range(NBLK):
        seen = (diff >= 0) & (diff < P) & (((b - 1) * P + k) >= P)
        far = np.minimum(b * P + q - PAD - m, P)
        for h in range(HEADS):
            bias[b, :, h, :2 * P] = np.where(seen, -slopes[h] * diff, NEG)
            bias[b, :, h, 2 * P:] = np.where(far >= 0, -slopes[h] * far, NEG)
    c["bias"] = bias.reshape(NBLK * P, HEADS * BAND)
    reset = np.ones((P, PAIRS, P), np.float32)
    reset[:, :, 0] = 0.0
    c["reset"] = reset.reshape(P, PAIRS * P)
    c["iota"] = np.tile(np.arange(E, dtype=np.float32), (P, 1))
    c["blockno"] = np.tile(np.arange(BLOCKS, dtype=np.float32), (P, 1))
    c["over"] = np.tile(P * np.arange(NB, dtype=np.float32), (P, 1))
    c["tokno"] = (np.arange(NB)[None, :] * P + np.arange(P)[:, None]).astype(np.int32)
    return c


class Chain:

    def __init__(self, eng, sem, base=0):
        self.eng, self.sem, self.base, self.n = eng, sem, base, 0

    def add(self, ins):
        self.n += 1
        return ins.then_inc(self.sem, 1)

    def join(self):
        self.eng.wait_ge(self.sem, self.base + self.n)

    def __call__(self, ins):
        self.add(ins)
        self.join()


def norm_and_turn(nc, sems, t, d):
    xa, loaded, squared, scaled, turned, taken, split, own, sp0, sp1 = sems(
        "n_xa", "loaded", "squared", "scaled", "turned", "taken", "split", "own", "n_sp0", "n_sp1")
    GROUPS = 2
    PER = NB // GROUPS
    with ExitStack() as ctx:
        sb = lambda n, s, dt=F32: ctx.enter_context(nc.sbuf_tensor(n, s, dt))
        xall = t["cT"][:, 0:NB, 0:D]
        xmeta = sb("xmeta", [META, D])
        gmix = sb("gmix", [P, KD])
        eps, zero = sb("eps", [P, 1]), sb("zero_x", [P, KD, TG - T])
        sq = sb("sq", [P, D])
        ssq = sb("ssq", [P, NB + 1])
        rstd = sb("rstd", [P, NB + 1])
        xs = sb("xs", [P, 2, D])
        xf = sb("xf", [P, 2, KD, P])
        ps = ctx.enter_context(nc.psum_tensor("turn_ps", [P, 2, KD, P], F32))
        ident, xh, xl = t["ident"], t["xh"], t["xl"]
        block = ctx.enter_context(nc.Block())

        def measured(g):
            return slice(0 if g == 0 else 1 + g * PER, 1 + (g + 1) * PER)

        def tiles(eng, g):
            if g == 0:
                yield META, xmeta[:, :], 0, 0
            with eng.Fori(g * PER // 2, (g + 1) * PER // 2) as j:
                for u in range(2):
                    i = 2 * j + u
                    yield P, xall[:, bass.ds(i, 1), :].rearrange("p a d -> p (a d)"), i + 1, (u + 1) % 2

        @block.sync
        def _(sp):
            xv = d["x"].rearrange("b (n p) d -> p (b n) d", p=P)
            sp.dma_start(xmeta[:, :], d["meta_tokens"][:, :]).then_inc(xa, 16)
            sp.dma_start(xall[:, 0:PER], xv[:, 0:PER]).then_inc(xa, 16)
            sp.dma_start(gmix[:, :], d["norm_mix_g"].rearrange("l (c p) -> p (l c)", p=P), allow_slow_non_contiguous=True).then_inc(loaded, 16)
            sp.dma_start(ident[:, :], d["c_ident"]).then_inc(loaded, 16)
            sp.dma_start(xall[:, PER:], xv[:, PER:]).then_inc(loaded, 16)
            for half in range(2):
                load_w_in(sp, t, d, half, half * P)
            spill = d["xn_spill"].rearrange("p (c j) -> p c j", c=KD)
            with sp.Fori(0, NB // 2) as j:
                for u in range(2):
                    i = 2 * j + u
                    sp.wait_ge(taken, 2 * KD + KD * (i + 2))
                    sp.dma_start(spill[:, :, bass.ds(i * P, P)], xf[:, (u + 1) % 2]).then_inc(sp1 if u == 0 else sp0, 16)
            sp.wait_ge(sp0, 16 + 16 * (NB // 2))
            sp.wait_ge(sp1, 16 + 16 * (NB // 2))

        @block.scalar
        def _(act):
            act.wait_ge(own, 5)
            for g in range(GROUPS):
                act.wait_ge(loaded if g else xa, 48 if g else 32)
                for rows, src, n, _ in tiles(act, g):
                    act.wait_ge(squared, n + g + 1)
                    act.activation(sq[0:rows, :], src, ACT.Square, accum_out=ssq[0:rows, bass.ds(n, 1)]).then_inc(squared, 1)
                act.wait_ge(squared, 1 + 1 + (g + 1) * PER + g)
                act.activation(rstd[:, measured(g)], ssq[:, measured(g)], ACT.Sqrt, scale=1.0 / D, bias=eps[:, :]).then_inc(squared, 1)

            def take(rows, n, u):
                act.wait_ge(turned, n + 3)
                act.wait_ge(split, 2 * n + 2)
                for c in range(KD):
                    act.activation(xf[:, u, c, 0:rows], ps[:, u, c, 0:rows], ACT.Copy, scale=gmix[:, c:c + 1]).then_inc(taken, 1)

            take(META, 0, 0)
            with act.Fori(0, NB // 2) as j:
                for u in range(2):
                    act.wait_ge(sp1 if u == 0 else sp0, 16 * j + 16)
                    take(P, 2 * j + u + 1, (u + 1) % 2)

        @block.gpsimd
        def _(pool):
            pool.sem_inc(sp0, 16)
            pool.sem_inc(sp1, 16)

        @block.vector
        def _(v):
            v.memset(zero[:, :, :], 0.0).then_inc(own, 1)
            v.memset(ssq[:, :], 1.0).then_inc(own, 1)
            v.memset(eps[:, :], EPS).then_inc(own, 1)
            v.wait_ge(own, 3)
            v.tensor_copy(xh[:, :, T:TG], zero[:, :, :]).then_inc(own, 1)
            v.tensor_copy(xl[:, :, T:TG], zero[:, :, :]).then_inc(own, 1)
            v.sem_inc(squared, 1)
            v.sem_inc(scaled, 1)
            v.sem_inc(split, 4)

            def scale(rows, src, n, u):
                v.wait_ge(turned, n + 1)
                v.tensor_scalar(xs[0:rows, u], src, rstd[0:rows, bass.ds(n, 1)], None, ALU.mult).then_inc(scaled, 1)

            def parts(rows, col, n, u):
                v.wait_ge(taken, 2 * KD + KD * (n + 1))
                hi, lo = (x[:, :, bass.ds(col, rows)] for x in (xh, xl))
                v.tensor_copy(hi, xf[:, u, :, 0:rows]).then_inc(split, 1)
                v.wait_ge(split, 4 + 2 * n + 1)
                v.tensor_tensor(lo, xf[:, u, :, 0:rows], hi.bitcast(F32), ALU.subtract).then_inc(split, 1)

            def scale_pair(j):
                for u in range(2):
                    i = 2 * j + u
                    scale(P, xall[:, bass.ds(i, 1), :].rearrange("p a d -> p (a d)"), i + 1, (u + 1) % 2)

            def parts_pair(j):
                for u in range(2):
                    parts(P, META + (2 * j + u) * P, 2 * j + u + 1, (u + 1) % 2)

            for g in range(GROUPS):
                v.wait_ge(squared, 1 + 1 + (g + 1) * PER + g + 1)
                v.reciprocal(rstd[:, measured(g)], rstd[:, measured(g)]).then_inc(own, 1)
                v.wait_ge(own, 5 + g + 1)
                if g == 0:
                    scale(META, xmeta[:, :], 0, 0)
                    parts(META, 0, 0, 0)
                    scale_pair(0)
                with v.Fori(max(0, g * PER // 2 - 1), (g + 1) * PER // 2 - 1) as j:
                    scale_pair(j + 1)
                    parts_pair(j)
            parts_pair(NB // 2 - 1)

        @block.tensor
        def _(pe):
            pe.sem_inc(turned, 2)
            pe.sem_inc(taken, 2 * KD)
            pe.wait_ge(loaded, 48)
            for g in range(GROUPS):
                for rows, _, n, u in tiles(pe, g):
                    pe.wait_ge(scaled, n + 2)
                    pe.wait_ge(taken, KD * n + KD)
                    for c in range(KD):
                        last = pe.transpose(ps[:, u, c, 0:rows], xs[0:rows, u, c * P:(c + 1) * P], ident[0:rows, 0:rows])
                    last.then_inc(turned, 1)


def load_w_in(sp, t, d, half, col):
    wv = d["w_in"].rearrange("l (c p) n -> p (l c) n", p=P)
    sp.dma_start(t["w_in_sb"][:, half], wv[:, :, bass.ds(col, P)]).then_inc(t["w_in_loaded"][half], 16)


def load_mix_tables(sp, t, d):
    for n in ("headones", "upper", "lower", "reset"):
        sp.dma_start(t[n], d["c_" + n]).then_inc(t["mix_par"], 16)
    sp.dma_start(t["gup"], d["w_gate_up"][0]).then_inc(t["mix_par"], 16)
    for at, n in ((0, "w0"), (1, "a0"), (2, "k_k"), (3, "k_a"), (5, "ln_x_g"), (6, "ln_x_b")):
        sp.dma_start(t["par"][:, at], d[n].rearrange("l (c p) -> p (l c)", p=P), allow_slow_non_contiguous=True).then_inc(t["mix_par"], 16)
    sp.dma_start(t["par"][:, 4], d["r_k"].rearrange("l (c a) k -> (a k) (l c)", a=2), allow_slow_non_contiguous=True).then_inc(t["mix_par"], 16)
    sp.dma_start(t["sink"], d["attn_sinks"][0:1, :].broadcast_to([P, HEADS])).then_inc(t["mix_par"], 16)


def project(nc, sems, t, d):
    mm, ev, sh, used, own, wh_done, wl_done = sems("p_mm", "p_ev", "p_sh", "p_used", "p_own", "p_wh", "p_wl")
    loaded = t["w_in_loaded"]
    STEPS = CHUNKS // 2
    with ExitStack() as ctx:
        sb = lambda n, s, dt=F32: ctx.enter_context(nc.sbuf_tensor(n, s, dt))
        w = t["w_in_sb"]
        wh, wl = sb("wh", [P, 2, KD, P], F32R), sb("wl", [P, 2, KD, P], F32R)
        raw = sb("raw", [P, 2, 1 + TG])
        tmp = sb("shift_tmp", [P, T])
        mu = sb("mu", [P, CHUNKS])
        ps = ctx.enter_context(nc.psum_tensor("proj_ps", [P, 2, NGROUPS, 512], F32))
        xh, xl, cT = t["xh"], t["xl"], t["cT"]
        block = ctx.enter_context(nc.Block())

        @block.sync
        def _(sp):
            sp.dma_start(mu[:, CH_RR:CHUNKS], d["shift_mu"].rearrange("l (c p) -> p (l c)", p=P), allow_slow_non_contiguous=True).then_inc(own, 16)
            load_mix_tables(sp, t, d)
            with sp.Fori(1, STEPS) as i:
                for u in range(2):
                    sp.wait_ge(wl_done, 2 * (i - 1) + u + 1)
                    load_w_in(sp, t, d, u, i * (2 * P) + u * P)
            sp.wait_ge(own, 4 + 16)
            sp.dma_start(t["wup"][0:64, 0], d["w_decay_up"][0]).then_inc(t["mix_par"], 16)
            sp.dma_start(t["wup"][64:128, 1], d["w_aaa_up"][0]).then_inc(t["mix_par"], 16)

        @block.tensor
        def _(pe):
            with pe.Fori(0, STEPS) as i:
                for u in range(2):
                    n = 2 * i + u
                    pe.wait_ge(wl_done, n + 1)
                    pe.wait_ge(ev, n + 1)
                    for g in range(NGROUPS):
                        cols = slice(g * GROUP, (g + 1) * GROUP)
                        for k in range(KD):
                            for a, b in ((wh, xh), (wl, xh), (wh, xl)):
                                last = pe.matmul(ps[:, u, g, 0:GROUP], a[:, u, k], b[:, k, cols],
                                                 start=(k == 0 and a is wh and b is xh), stop=(k == KD - 1 and b is xl))
                    last.then_inc(mm, 1)

        @block.scalar
        def _(act):
            act.sem_inc(ev, 2)

            def high(turn, n, u):
                act.wait_ge(loaded[u], 16 * turn)
                act.activation(wh[:, u], w[:, u], ACT.Copy).then_inc(wh_done, 1)

            def take(n, u):
                act.wait_ge(mm, n + 1)
                act.wait_ge(sh, n + 1)
                act.activation(raw[:, u, 1:1 + TG].rearrange("p (g j) -> p g j", g=NGROUPS),
                               ps[:, u, :, 0:GROUP], ACT.Copy).then_inc(ev, 1)

            high(1, 0, 0)
            high(1, 1, 1)
            with act.Fori(0, STEPS - 1) as i:
                for u in range(2):
                    take(2 * i + u, u)
                    high(i + 2, 2 * i + u + 2, u)
            for n in range(CHUNKS - 2, CHUNKS):
                take(n, n % 2)

        @block.vector
        def _(v):
            def low(n, u):
                v.wait_ge(wh_done, n + 1)
                v.tensor_tensor(wl[:, u], w[:, u], wh[:, u].bitcast(F32), ALU.subtract).then_inc(wl_done, 1)

            def shift(n, u):
                v.wait_ge(ev, n + 3)
                v.wait_ge(sh, n + 2)
                v.tensor_tensor(tmp[:, :], raw[:, u, 0:T], raw[:, u, 1:1 + T], ALU.subtract).then_inc(used, 1)
                v.wait_ge(used, n + 1)
                out = cT[:, bass.ds(n, 1), PAD:TP].rearrange("p a j -> p (a j)")
                v.scalar_tensor_tensor(out, tmp[:, :], mu[:, bass.ds(n, 1)], raw[:, u, 1:1 + T], ALU.mult, ALU.add).then_inc(sh, 1)

            v.sem_inc(sh, 2)
            low(0, 0)
            low(1, 1)
            v.memset(raw[:, :, 0:1], 0.0).then_inc(own, 1)
            v.memset(mu[:, 0:CH_RR], 0.0).then_inc(own, 1)
            v.memset(cT[:, :, 0:PAD], 0.0).then_inc(own, 1)
            v.memset(t["wup"], 0.0).then_inc(own, 1)
            v.wait_ge(own, 4 + 16)
            with v.Fori(0, STEPS - 1) as i:
                for u in range(2):
                    low(2 * i + u + 2, u)
                    shift(2 * i + u, u)
            for n in range(CHUNKS - 2, CHUNKS):
                shift(n, n % 2)


def mix(nc, sems, t, d):
    names = ("x_bias x_st x_lora x_sg x_mmw x_mmg x_th x_qk x_lgt x_va x_ss x_rn x_kkr "
             "x_rec x_exp x_csd x_ar x_bk x_mmM x_msk x_mmA x_tt x_tok x_tinit x_x1 x_x1c x_yy x_tup x_W "
             "x_Wc x_U x_Uc x_Y x_Yc x_S x_S0 x_Sn x_sums x_unit x_rr x_lsd x_sqr x_vr x_sd x_rk x_mx "
             "x_pe x_pn x_tp x_tpc x_O x_att x_v x_a x_init x_yc x_vm x_fin")
    s = dict(zip([n[2:] for n in names.split()], sems(*names.split())))
    NV, NA = t["mix_counts"]
    with ExitStack() as ctx:
        sb = lambda n, sh, dt=F32: ctx.enter_context(nc.sbuf_tensor(n, sh, dt))
        ident, cT = t["ident"], t["cT"]
        headones, upper, lower, reset, wup, gup, par, sink = (
            t[n] for n in ("headones", "upper", "lower", "reset", "wup", "gup", "par", "sink"))
        lev = sb("lev", [P, len(LEVELS), 2, P], U8)
        hw0, ha0, kkw, hka, rkw, lng, lnb, omk = (par[:, n] for n in range(8))
        bias = sb("bias", [P, HEADS, BAND])
        qs, kb = sb("qs", [P, PAIRS, P]), sb("kb", [P, KV, 2, BAND])
        lg = sb("lg", [P, HEADS, BAND])
        lev_in = lg[:, :, :].rearrange("p h k -> p (h k)")[:, 0:len(LEVELS) * 2 * P].rearrange("p (l a j) -> p l a j", l=len(LEVELS), a=2)
        st8 = sb("st8", [P, 5, HEADS])
        mx, nmx, dsk, es, ls = (st8[:, n] for n in range(5))
        vas, vtok = sb("vas", [P, P]), sb("vtok", [P, 3, P])
        pTm = sb("pTm", [META, HEADS, P])
        lora, sg = sb("lora", [P, P]), sb("sg", [P, P])
        wide = lambda n: sb(n, [P, PAIRS, P])
        th, tha, lw, cs = wide("th"), wide("tha"), wide("lw"), wide("cs")
        ep, em, kk, kp, tmp = wide("ep"), wide("em"), wide("kk"), wide("kp"), wide("tmp")
        ar, bt, kt = sb("ar", [P, PAIRS, 2, 2, P]), wide("bt"), wide("kt")
        el4 = sb("el4", [P, 2, PAIRS])
        ecm, elast = el4[:, 0], el4[:, 1]
        mats = sb("mats", [P, HEADS, 2, 2, P])
        A, X1, T2 = sb("A_m", [P, HEADS, P]), sb("X1_m", [P, HEADS, P]), sb("T_m", [P, 2, HEADS, P])
        Tm, TT = T2[:, 0], T2[:, 1]
        pT = T2
        btok, ktok, rvtok, rv, rkb = wide("btok"), wide("ktok"), wide("rvtok"), wide("rv"), wide("rkb")
        W, U = (A[:, 4 * n:4 * n + 4].rearrange("p a (b k) -> p (a b) k", k=HD) for n in range(2))
        S, S0 = sb("S_m", [P, PAIRS, HD]), sb("S0_m", [P, PAIRS, HD])
        WT = A[:, 4:8]
        yT = X1[:, 0:4]
        bank = [ctx.enter_context(nc.psum_tensor(f"mix_ps{n}", [P, 512], F32)) for n in range(8)]
        wide_ps = lambda n: bank[n][:, :].rearrange("p (c j) -> p c j", c=PAIRS)
        RING = (3, 4, 7, 2)
        PASSES = len(LEVELS) + 1
        PASSES_0 = META.bit_length() - 2
        block = ctx.enter_context(nc.Block())

        TURNED = range(1, PASSES - 1)
        UPDATES = 4 + 2 * len(TURNED)

        def products(m):
            return 2 * PASSES_0 + 2 * PASSES * m if not isinstance(m, int) or m >= 0 else 0

        def firsts(m, l, g, turned=0):
            before = 4 * PASSES_0 + (2 * PASSES + 2 * len(TURNED)) * m if not isinstance(m, int) or m >= 0 else 0
            own = (g, 2 + 4 * (l - 1) + 2 * g + turned, 2 + 4 * len(TURNED) + g)
            return before + 1 + own[0 if l == 0 else 1 if l < PASSES - 1 else 2]

        def updates(m):
            return 4 + 2 * PASSES_0 + UPDATES * m if not isinstance(m, int) or m >= 0 else 0

        def cols(ch, i, n=1):
            return cT[:, ch:ch + n, bass.ds(i * P, P)]

        def apart(eng):
            eng.sem_inc(t["tick"], 1)

        def blk(ch, i):
            return cols(ch, i).rearrange("p a j -> p (a j)")

        def hp(h):
            return slice(HD * (h % 2), HD * (h % 2) + HD)

        @block.sync
        def _(sp):
            sp.dma_start(lev_in, d["c_lev"]).then_inc(t["mix_par"], 16)
            zeros = cT[:, 0:D // HD, 0:HD]
            with sp.Fori(SURE, BLOCKS) as n:
                sp.dma_start(d["y_rows"].rearrange("(n p) (c j) -> n p c j", p=P, j=HD)[bass.ds(n, 1)], zeros).then_inc(t["y_zeroed"], 16)
            bv = d["c_bias"].rearrange("(b p) n -> b p n", p=P)
            sp.dma_start(bias[:, :, :], bv[1]).then_inc(s["bias"], 16)
            with sp.Fori(2, NBLK) as i:
                sp.wait_ge(s["lgt"], (i - 1) * HEADS)
                sp.dma_start(bias[:, :, :], bv[bass.ds(i, 1)]).then_inc(s["bias"], 16)
            sp.wait_ge(t["y_zeroed"], 16 * (BLOCKS - SURE))

        @block.scalar
        def _(act):
            act.wait_ge(t["mix_par"], 16 * MIX_LOADS)
            act.wait_ge(s["init"], 3)
            for g in range(KV):
                for half in range(2):
                    act.activation(kb[HD * half:HD * half + HD, g, half, 2 * P:BAND], cT[HD * g:HD * g + HD, CH_K, PAD:P], ACT.Copy).then_inc(s["a"], 1)
            act.wait_ge(s["qk"], 1)
            act.activation(vtok[0:META, 2], bank[0][0:META, 0:P], ACT.Copy).then_inc(s["vm"], 1)
            base = 4
            act.sem_inc(s["att"], 1)

            def stage_low(j, first=False):
                if not first:
                    act.wait_ge(s["mmw"], 2 * j)
                apart(act)
                act.activation(lora[0:64, :], cT[0:64, CH_WA, bass.ds(j * P, P)], ACT.Tanh).then_inc(s["lora"], 1)
                act.activation(lora[64:128, :], cT[64:128, CH_WA, bass.ds(j * P, P)], ACT.Copy).then_inc(s["lora"], 1)

            def stage_gate(j, link):
                apart(act)
                link(act.activation(sg[:, :], blk(CH_G, j), ACT.Tanh, scale=0.5))
                act.activation(sg[:, :], sg[:, :], ACT.Copy, scale=0.5, bias=0.5).then_inc(s["sg"], 1)

            def stage_attention(j, link):
                act.wait_ge(s["qk"], (j - 1) * HEADS + 1)
                apart(act)
                act.activation(qs[:, :, :], cols(CH_Q, j, 4), ACT.Copy).then_inc(s["st"], 1)
                link(act.activation(kb[:, :, :, 0:P], kb[:, :, :, P:2 * P], ACT.Copy))
                for g in range(KV):
                    for half in range(2):
                        act.activation(kb[HD * half:HD * half + HD, g, half, P:2 * P], cT[HD * g:HD * g + HD, CH_K, bass.ds(j * P, P)],
                                       ACT.Copy).then_inc(s["st"], 1)

            def stage_v(j):
                apart(act)
                act.activation(vas[:, :], blk(CH_V, j), ACT.Copy).then_inc(s["va"], 1)
                act.activation(rv[:, :, :], cols(CH_RV, j, 4), ACT.Copy).then_inc(s["va"], 1)

            def low_rank(j):
                act.wait_ge(s["mmw"], 2 * j + 1)
                for p in range(PAIRS):
                    act.activation(th[:, p], wide_ps(0)[:, p], ACT.Tanh, scale=0.5, bias=hw0[:, p:p + 1]).then_inc(s["th"], 1)
                act.wait_ge(s["mmw"], 2 * j + 2)
                for p in range(PAIRS):
                    act.activation(tha[:, p], wide_ps(1)[:, p], ACT.Tanh, scale=0.5, bias=ha0[:, p:p + 1]).then_inc(s["th"], 1)

            def decays(j):
                act.wait_ge(s["csd"], j + 1)
                act.activation(ecm, cs[:, :, P // 2 - 1], ACT.Exp).then_inc(s["exp"], 1)
                act.activation(ep[:, :, :], lw[:, :, :], ACT.Exp).then_inc(s["exp"], 1)
                act.activation(em[:, :, :], tmp[:, :, :], ACT.Exp, scale=-1.0).then_inc(s["exp"], 1)
                act.wait_ge(s["exp"], 4 * j + 1)
                act.activation(cs[:, :, :], tmp[:, :, :], ACT.Exp).then_inc(s["exp"], 1)

            def key_norm(j):
                act.wait_ge(s["rn"], 2 * j + 1)
                act.activation(kp[:, :, :], kp[:, :, :], ACT.Sqrt).then_inc(s["rec"], 1)

            def body(i, base, first=False, last_block=False):
                m, prep = i - 1, not last_block
                link = Chain(act, s["a"], base)
                act.wait_ge(s["tt"], 4 * i + 2)
                act.activation(rvtok[:, :, :], wide_ps(0), ACT.Copy).then_inc(s["tok"], 1)
                link(act.activation(vtok[:, 0], vtok[:, 1], ACT.Copy))
                act.activation(vtok[:, 1], bank[1][:, 0:P], ACT.Copy).then_inc(s["tok"], 1)
                if prep:
                    stage_low(i + 1)
                act.wait_ge(s["tt"], 4 * i + 4)
                act.activation(btok[:, :, :], wide_ps(0), ACT.Copy).then_inc(s["tok"], 1)
                act.activation(ktok[:, :, :], wide_ps(1), ACT.Copy).then_inc(s["tok"], 1)
                for l in range(PASSES_0 if first else PASSES):
                    for g in range(2):
                        hs = slice(4 * g, 4 * g + 4)
                        act.wait_ge(s["x1"], firsts(m, l, g))
                        act.activation(X1[:, hs], wide_ps(3 + g), ACT.Copy).then_inc(s["x1c"], 1)
                        if l in TURNED:
                            act.wait_ge(s["x1"], firsts(m, l, g, 1))
                            act.activation(TT[:, hs], wide_ps(7 if g == 0 else 2), ACT.Copy).then_inc(s["x1c"], 1)
                    if l == 0 and prep:
                        low_rank(i + 1)
                    if l == 1:
                        if not first:
                            act.wait_ge(s["mx"], m + 1)
                            act.activation(es, dsk, ACT.Exp).then_inc(s["pe"], 1)
                            for h in range(HEADS):
                                act.activation(lg[:, h], lg[:, h], ACT.Exp, bias=nmx[:, h:h + 1], accum_out=ls[:, h:h + 1]).then_inc(s["pe"], 1)
                        act.wait_ge(s["W"], 2 * i + 1)
                        act.activation(WT, wide_ps(0), ACT.Copy).then_inc(s["Wc"], 1)
                    if l == 2:
                        if prep:
                            decays(i + 1)
                        act.wait_ge(s["W"], 2 * i + 2)
                        act.activation(W[:, :, :], bank[1][:, :].rearrange("p (h k) -> p h k", h=HEADS), ACT.Copy).then_inc(s["Wc"], 1)
                    if l == 3 and prep:
                        stage_attention(i + 1, link)
                    if l == 4 and prep:
                        key_norm(i + 1)
                    if l >= 4:
                        n = 2 << l
                        for g in range(2):
                            act.wait_ge(s["yy"], products(m) + 2 * l + g + 1)
                            hs = slice(4 * g, 4 * g + 4)
                            y, yt = wide_ps(5 + g), wide_ps(7 if g == 0 else 2)
                            for b in range(0, P, 2 * n):
                                if l == 4:
                                    act.activation(Tm[b + n:b + 2 * n, hs, b:b + n], y[b + n:b + 2 * n, :, b:b + n], ACT.Copy).then_inc(s["tinit"], 1)
                                act.activation(TT[b:b + n, hs, b + n:b + 2 * n], yt[b:b + n, :, b + n:b + 2 * n], ACT.Copy).then_inc(s["tinit"], 1)
                if first:
                    for g in range(2):
                        act.wait_ge(s["x1"], 4 * PASSES_0 - 2 + g + 1)
                        act.activation(TT[:, 4 * g:4 * g + 4], wide_ps(7 if g == 0 else 2), ACT.Copy).then_inc(s["x1c"], 1)
                    stage_attention(i + 1, link)
                    stage_gate(i + 1, link)
                    key_norm(i + 1)
                act.wait_ge(s["U"], i + 1)
                act.activation(U[:, :, :], bank[1][:, :].rearrange("p (h k) -> p h k", h=HEADS), ACT.Copy).then_inc(s["Uc"], 1)
                if not first:
                    act.wait_ge(s["lsd"], m + 1)
                    for h in range(HEADS):
                        act.activation(lg[:, h], lg[:, h], ACT.Copy, scale=ls[:, h:h + 1]).then_inc(s["pn"], 1)
                if prep:
                    stage_v(i + 1)
                if first:
                    return link.n
                act.wait_ge(s["Y"], m + 1)
                act.activation(yT, wide_ps(3), ACT.Copy).then_inc(s["Yc"], 1)
                for n in range(4):
                    act.wait_ge(s["tp"], 6 * m + n + 1)
                    act.activation(pT[:, n // 2, 4 * (n % 2):4 * (n % 2) + 4], wide_ps((0, 1, 2, 7)[n]), ACT.Copy).then_inc(s["tpc"], 1)
                    if n == 1:
                        act.wait_ge(s["yc"], m + 1)
                        act.activation(tmp[:, :, :], yT, ACT.Square).then_inc(s["sqr"], 1)
                for n in range(2):
                    act.wait_ge(s["tp"], 6 * m + 5 + n)
                    act.activation(pTm[:, 4 * n:4 * n + 4], wide_ps(3 + 1 * n)[0:META], ACT.Copy).then_inc(s["tpc"], 1)
                act.wait_ge(s["vr"], m + 1)
                act.activation(th[:, :, :], th[:, :, :], ACT.Sqrt).then_inc(s["sd"], 1)
                act.wait_ge(s["O"], m + 1)
                apart(act)
                act.activation(cols(CH_Q, i, 4), wide_ps(1), ACT.Copy).then_inc(s["att"], 1)
                if prep:
                    act.wait_ge(s["mmg"], m + 1)
                    stage_gate(i + 1, link)
                return link.n

            link = Chain(act, s["a"], base)
            act.wait_ge(s["init"], 8)
            stage_low(0, first=True)
            low_rank(0)
            stage_v(0)
            decays(0)
            key_norm(0)
            base += link.n
            base += body(0, base, first=True)
            with act.Fori(1, NBLK - 1) as i:
                steps = body(i, (i - 1) * NA + base)
            assert steps == NA, steps
            body(NBLK - 1, (NBLK - 2) * NA + base, last_block=True)

        @block.vector
        def _(v):
            v.memset(kb[:, :, :, :], 0.0).then_inc(s["init"], 1)
            v.memset(vtok[:, 1], 0.0).then_inc(s["init"], 1)
            v.memset(S[:, :, :], 0.0).then_inc(s["init"], 1)
            v.memset(ar[:, :, :, :, :], 0.0).then_inc(s["init"], 1)
            v.wait_ge(t["mix_par"], 16 * MIX_LOADS)
            v.tensor_scalar(par[:, 0:2], par[:, 0:2], 0.5, None, ALU.mult).then_inc(s["init"], 1)
            v.tensor_scalar(hka, hka, 0.5, None, ALU.mult).then_inc(s["init"], 1)
            v.wait_ge(s["init"], 6)
            v.tensor_copy(lev[:, :, :, :], lev_in).then_inc(s["init"], 1)
            v.wait_ge(s["init"], 7)
            v.tensor_scalar(omk, hka, -1.0, 1.0, ALU.mult, ALU.add).then_inc(s["init"], 1)
            v.wait_ge(s["init"], 8)
            v.sem_inc(s["fin"], 1)
            flat = lambda x: x[:, :, :].rearrange("p c j -> p (c j)")

            def decays(j, link):
                v.wait_ge(s["th"], 8 * j + 4)
                link(v.tensor_scalar(lw[:, :, :], th[:, :, :], -0.5 * DECAY, -0.5 * DECAY, ALU.mult, ALU.add))
                link(v.tensor_tensor_scan(flat(cs), reset[:, :], flat(lw), 0.0, ALU.mult, ALU.add))
                for p in range(PAIRS):
                    link.add(v.tensor_scalar(tmp[:, p], cs[:, p], cs[:, p, P // 2 - 1:P // 2], None, ALU.subtract))
                link.join()
                v.tensor_tensor(lw[:, :, :], tmp[:, :, :], lw[:, :, :], ALU.subtract).then_inc(s["csd"], 1)

            def keys(j, link):
                if not isinstance(j, int) or j > 1:
                    v.wait_ge(s["rk"], 4 * (j - 1))
                for p in range(PAIRS):
                    link.add(v.tensor_scalar(kk[:, p], blk(CH_RK + p, j), kkw[:, p:p + 1], None, ALU.mult))
                link.join()
                v.tensor_tensor(kp[:, :, :], kk[:, :, :], kk[:, :, :], ALU.mult).then_inc(s["kkr"], 1)

            def key_norm(j):
                v.wait_ge(s["ss"], j + 1)
                v.tensor_scalar(kp[:, :, :], wide_ps(0), 1e-24, None, ALU.max).then_inc(s["rn"], 1)

            def factors(j, link):
                v.wait_ge(s["rec"], j + 1)
                link(v.reciprocal(kp[:, :, :], kp[:, :, :]))
                v.tensor_tensor(kk[:, :, :], kk[:, :, :], kp[:, :, :], ALU.mult).then_inc(s["rn"], 1)
                v.wait_ge(s["rn"], 2 * j + 2)
                v.wait_ge(s["th"], 8 * j + 8)
                for p in range(PAIRS):
                    link.add(v.tensor_scalar(kp[:, p], tha[:, p], hka[:, p:p + 1], omk[:, p:p + 1], ALU.mult, ALU.add))
                link.add(v.tensor_scalar(th[:, :, :], tha[:, :, :], 0.5, 0.5, ALU.mult, ALU.add))
                link.join()
                link.add(v.tensor_tensor(kp[:, :, :], kp[:, :, :], cols(CH_RK, j, 4), ALU.mult))
                link(v.tensor_tensor(th[:, :, :], th[:, :, :], kk[:, :, :], ALU.mult))
                v.wait_ge(s["exp"], 4 * j + 4)
                v.tensor_tensor(bt[:, :, :], th[:, :, :], em[:, :, :], ALU.mult).then_inc(s["bk"], 1)
                v.tensor_tensor(kt[:, :, :], kp[:, :, :], em[:, :, :], ALU.mult).then_inc(s["bk"], 1)

            def reads(j, e):
                v.scalar_tensor_tensor(ar[hp(e), :, e, 0], kk[hp(e)], -1.0, ep[hp(e)], ALU.mult, ALU.mult).then_inc(s["ar"], 1)
                v.tensor_tensor(ar[hp(e), :, e, 1], cols(CH_RR, j, 4)[hp(e)], cs[hp(e)], ALU.mult).then_inc(s["ar"], 1)

            def start_state(j, link):
                link.add(v.tensor_copy(elast, cs[:, :, P - 1]))
                v.tensor_tensor(S0[:, :, :], S[:, :, :], ecm.unsqueeze(2).broadcast_to([P, PAIRS, HD]), ALU.mult).then_inc(s["S0"], 1)

            def body(i, base, first=False, last_block=False):
                m, prep = i - 1, not last_block
                link = Chain(v, s["v"], base)
                if not first:
                    v.wait_ge(s["bias"], 16 * m + 16)
                for h in () if first else range(HEADS):
                    v.wait_ge(s["qk"], HEADS * m + h + 2)
                    v.scalar_tensor_tensor(lg[:, h], bank[RING[h % 4]][:, 0:BAND], SCALE, bias[:, h], ALU.mult, ALU.add).then_inc(s["lgt"], 1)
                for h in range(HEADS):
                    v.wait_ge(s["mmM"], HEADS * i + h + 1)
                    src = bank[RING[h % 4]][:, :].rearrange("p (m c) -> p m c", m=2)
                    v.tensor_tensor(mats[:, h].rearrange("p m a j -> p m (a j)"), src,
                                    upper[:, :, :].rearrange("p a j -> p (a j)").unsqueeze(1).broadcast_to([P, 2, 2 * P]),
                                    ALU.mult).then_inc(s["msk"], 1)
                for g in range(2):
                    hs = slice(4 * g, 4 * g + 4)
                    v.wait_ge(s["mmA"], 2 * i + g + 1)
                    link.add(v.tensor_tensor(A[:, g:HEADS:2], wide_ps(5 + g), lower[:, :].unsqueeze(1).broadcast_to([P, 4, P]), ALU.mult))
                v.wait_ge(s["msk"], HEADS * i + HEADS)
                v.wait_ge(s["unit"], 2 * i + 2)
                link.join()
                mask = lambda l, tr: lev[:, l, tr].unsqueeze(1).broadcast_to([P, 4, P])
                apart(v)
                for g in range(2):
                    hs = slice(4 * g, 4 * g + 4)
                    v.copy_predicated(Tm[:, hs], mask(0, 0), A[:, hs]).then_inc(s["tup"], 1)
                for g in range(2):
                    hs = slice(4 * g, 4 * g + 4)
                    v.copy_predicated(TT[:, hs], mask(0, 1), mats[:, hs, 0, 0]).then_inc(s["tup"], 1)
                if not first:
                    v.wait_ge(s["lgt"], HEADS * m + HEADS)
                    link(v.tensor_reduce(mx, lg[:, :, :], AX.X, ALU.max))
                    link(v.tensor_tensor(mx, mx, sink[:, :], ALU.max))
                    link.add(v.tensor_scalar(nmx, mx, -1.0, None, ALU.mult))
                    link(v.tensor_tensor(dsk, sink[:, :], mx, ALU.subtract))
                    v.sem_inc(s["mx"], 1)
                for l in range(1, PASSES_0 + 1 if first else PASSES - 1):
                    for g in range(2):
                        hs = slice(4 * g, 4 * g + 4)
                        v.wait_ge(s["yy"], products(m) + 2 * (l - 1) + g + 1)
                        apart(v)
                        v.copy_predicated(Tm[:, hs], mask(l, 0), wide_ps(5 + g)).then_inc(s["tup"], 1)
                    if l == 1 and prep:
                        decays(i + 1, link)
                    if l == 2:
                        if prep:
                            keys(i + 1, link)
                        if not first:
                            v.wait_ge(s["pe"], (HEADS + 1) * (m + 1))
                            link(v.tensor_tensor(ls, ls, es, ALU.add))
                            v.reciprocal(ls, ls).then_inc(s["lsd"], 1)
                    if l == 3 and prep:
                        key_norm(i + 1)
                if prep:
                    factors(i + 1, link)
                v.wait_ge(s["S"], i + 1)
                if prep:
                    v.wait_ge(s["bk"], 2 * i + 4)
                v.tensor_tensor(S[:, :, :], S0[:, :, :], bank[4][:, 0:PAIRS * HD].rearrange("p (c k) -> p c k", c=PAIRS), ALU.add).then_inc(s["Sn"], 1)
                if first:
                    v.wait_ge(s["Sn"], i + 1)
                    link(v.tensor_tensor(S[:, :, :], S[:, :, :], elast.unsqueeze(2).broadcast_to([P, PAIRS, HD]), ALU.mult))
                    reads(i + 1, 0)
                    reads(i + 1, 1)
                    start_state(i + 1, link)
                    return link.n
                v.wait_ge(s["sums"], 3 * m + 1)
                v.scalar_tensor_tensor(yT, wide_ps(5), -1.0 / HD, yT, ALU.mult, ALU.add).then_inc(s["yc"], 1)
                v.wait_ge(s["Sn"], i + 1)
                link(v.tensor_tensor(S[:, :, :], S[:, :, :], elast.unsqueeze(2).broadcast_to([P, PAIRS, HD]), ALU.mult))
                if prep:
                    reads(i + 1, 0)
                    reads(i + 1, 1)
                v.wait_ge(s["sums"], 3 * m + 2)
                v.tensor_scalar(th[:, :, :], wide_ps(6), 1.0 / HD, LN_EPS, ALU.mult, ALU.add).then_inc(s["vr"], 1)
                if prep:
                    start_state(i + 1, link)
                v.wait_ge(s["sums"], 3 * m + 3)
                link(v.tensor_tensor(lw[:, :, :], cols(CH_RV, i, 4), wide_ps(5), ALU.mult))
                for p in range(PAIRS):
                    link.add(v.tensor_scalar(lw[:, p], lw[:, p], lnb[:, p:p + 1], None, ALU.add))
                v.wait_ge(s["sd"], m + 1)
                link(v.reciprocal(th[:, :, :], th[:, :, :]))
                for p in range(PAIRS):
                    link.add(v.scalar_tensor_tensor(yT[:, p], yT[:, p], lng[:, p:p + 1], th[:, p], ALU.mult, ALU.mult))
                link.join()
                link(v.tensor_tensor(yT, yT, lw[:, :, :], ALU.add))
                v.wait_ge(s["mmg"], m + 1)
                v.tensor_tensor(cols(CH_RR, i, 4), yT, wide_ps(6), ALU.mult).then_inc(s["fin"], 1)
                return link.n

            link = Chain(v, s["v"])
            decays(0, link)
            keys(0, link)
            key_norm(0)
            factors(0, link)
            reads(0, 0)
            reads(0, 1)
            start_state(0, link)
            base = link.n
            base += body(0, base, first=True)
            with v.Fori(1, NBLK - 1) as i:
                steps = body(i, (i - 1) * NV + base)
            assert steps == NV, steps
            body(NBLK - 1, (NBLK - 2) * NV + base, last_block=True)

        @block.gpsimd
        def _(pool):
            def unit(j):
                for x in (Tm, TT):
                    pool.tensor_copy(x[:, :, :], ident[:, :].unsqueeze(1).broadcast_to([P, HEADS, P])).then_inc(s["unit"], 1)

            def bonus_terms(j):
                pool.wait_ge(s["bk"], 2 * j + 2)
                apart(pool)
                pool.tensor_tensor(rkb[:, :, :], kp[:, :, :], cols(CH_RR, j, 4), ALU.mult).then_inc(s["rr"], 1)
                pool.wait_ge(s["rr"], j)
                apart(pool)
                for p in range(PAIRS):
                    pool.tensor_scalar(rkb[:, p], rkb[:, p], rkw[:, p:p + 1], None, ALU.mult).then_inc(s["rk"], 1)

            pool.wait_ge(t["mix_par"], 16 * MIX_LOADS)
            unit(0)
            bonus_terms(1)
            pool.wait_ge(s["U"], 1)
            unit(1)
            with pool.Fori(1, NBLK - 1) as i:
                pool.wait_ge(s["sums"], 3 * i)
                bonus_terms(i + 1)
                pool.wait_ge(s["O"], i)
                apart(pool)
                unit(i + 1)

        @block.tensor
        def _(pe):
            pe.wait_ge(t["mix_par"], 16 * MIX_LOADS)
            pe.transpose(bank[0][0:META, 0:P], cT[:, CH_V, PAD:P], ident[:, :]).then_inc(s["qk"], 1)
            pe.wait_ge(s["vm"], 1)

            def low_rank(j):
                pe.wait_ge(s["lora"], 2 * j + 2)
                for n in range(2):
                    for p in range(PAIRS):
                        last = pe.matmul(wide_ps(n)[:, p], wup[:, n, p * P:(p + 1) * P], lora[:, :], start=True, stop=True)
                    last.then_inc(s["mmw"], 1)

            def key_sums(j):
                pe.wait_ge(s["kkr"], j + 1)
                pe.matmul(bank[0][:, :], headones[:, :], kp[:, :, :].rearrange("p c j -> p (c j)"), start=True, stop=True).then_inc(s["ss"], 1)

            def body(i, first=False, last_block=False):
                m, prep = i - 1, not last_block
                if not first:
                    pe.wait_ge(s["st"], 5 * m + 5)
                    pe.wait_ge(s["Sn"], i)
                for h in range(HEADS):
                    if h >= 4 and not first:
                        pe.wait_ge(s["lgt"], HEADS * m + h - 3)
                    if not first:
                        pe.matmul(bank[RING[h % 4]][:, 0:BAND], qs[:, h // 2, :], kb[:, h // 4, h % 2, :], start=True, stop=True).then_inc(s["qk"], 1)
                    if h == 3:
                        pe.wait_ge(s["va"], 2 * i + 2)
                        pe.wait_ge(s["rn"], 2 * i + 1)
                        for p in range(PAIRS):
                            last = pe.transpose(wide_ps(0)[:, p], rv[:, p], ident[:, :])
                        last.then_inc(s["tt"], 1)
                        pe.wait_ge(s["th"], 8 * i + 8)
                        if not first:
                            pe.wait_ge(s["att"], m + 1)
                        pe.transpose(bank[1][:, 0:P], vas[:, :], ident[:, :]).then_inc(s["tt"], 1)
                pe.wait_ge(s["ar"], 4 * i + 4)
                pe.wait_ge(s["bk"], 2 * i + 2)
                for h in range(HEADS):
                    p = h // 2
                    if h < 4 and not first:
                        pe.wait_ge(s["lgt"], HEADS * m + 5 + h)
                    if h >= 4:
                        pe.wait_ge(s["msk"], HEADS * i + h - 3)
                    both = ar[:, p, h % 2].rearrange("k a j -> k (a j)")
                    pe.matmul(bank[RING[h % 4]][:, 0:2 * P], bt[:, p], both, start=True, stop=True)
                    pe.matmul(bank[RING[h % 4]][:, 2 * P:4 * P], kt[:, p], both, start=True, stop=True).then_inc(s["mmM"], 1)
                    if h == 3:
                        pe.wait_ge(s["tok"], 4 * i + 2)
                        for n, src in enumerate((bt, kt)):
                            for q in range(PAIRS):
                                last = pe.transpose(wide_ps(n)[:, q], src[:, q], ident[:, :])
                            last.then_inc(s["tt"], 1)
                if not first:
                    pe.wait_ge(s["fin"], m + 1)
                for g in range(2):
                    for h in range(g, HEADS, 2):
                        last = pe.matmul(wide_ps(5 + g)[:, h // 2], ar[:, h // 2, g, 0], bt[:, h // 2], start=True, stop=True)
                    last.then_inc(s["mmA"], 1)
                pe.wait_ge(s["msk"], HEADS * i + HEADS)
                for l in range(PASSES_0 if first else PASSES):
                    for g in range(2):
                        hs = range(4 * g, 4 * g + 4)
                        if l < PASSES - 1:
                            pe.wait_ge(s["tup"], updates(m) + (g + 1 if l == 0 else 4 + 2 * (l - 1) + g + 1))
                        else:
                            pe.wait_ge(s["tinit"], 10 * m + 4 * g + 4)
                        for h in hs:
                            last = pe.matmul(wide_ps(3 + g)[:, h % 4], mats[:, h, 0, 0], Tm[:, h], start=True, stop=True)
                        last.then_inc(s["x1"], 1)
                        if l in TURNED:
                            for h in hs:
                                last = pe.transpose(wide_ps(7 if g == 0 else 2)[:, h % 4], Tm[:, h], ident[:, :])
                            last.then_inc(s["x1"], 1)
                    for g in range(2):
                        hs = range(4 * g, 4 * g + 4)
                        pe.wait_ge(s["x1c"], firsts(m, l, g, 1))
                        if l == 0:
                            pe.wait_ge(s["tup"], updates(m) + g + 3)
                        if l < PASSES - 1:
                            for h in hs:
                                last = pe.matmul(wide_ps(5 + g)[:, h % 4], TT[:, h], X1[:, h], start=True, stop=True)
                        if l >= PASSES - 2:
                            for h in hs:
                                last = pe.matmul(wide_ps(7 if g == 0 else 2)[:, h % 4], X1[:, h], TT[:, h], start=True, stop=True)
                        last.then_inc(s["yy"], 1)
                    if l == 0:
                        pe.wait_ge(s["tok"], 4 * i + 4)
                        if prep:
                            low_rank(i + 1)
                    if l == 1:
                        if prep:
                            pe.wait_ge(s["th"], 8 * i + 12)
                        pe.wait_ge(s["S0"], i + 1)
                        for h in range(HEADS):
                            o = wide_ps(0)[hp(h), h // 2]
                            pe.matmul(o, S0[:, h // 2], ar[:, h // 2, h % 2, 0], start=True, stop=False)
                            last = pe.matmul(o, rvtok[:, h // 2, hp(h)], mats[:, h, 1, 0], start=False, stop=True)
                        last.then_inc(s["W"], 1)
                    if l == 2:
                        pe.wait_ge(s["Wc"], 2 * i + 1)
                        if prep:
                            pe.wait_ge(s["th"], 8 * i + 16)
                        for p in range(PAIRS):
                            last = pe.transpose(wide_ps(1)[:, p], WT[:, p], ident[:, :])
                        last.then_inc(s["W"], 1)
                    if l == 3 and prep:
                        key_sums(i + 1)
                if first:
                    for g in range(2):
                        pe.wait_ge(s["tup"], updates(m) + 4 + 2 * (PASSES_0 - 1) + g + 1)
                        for h in range(4 * g, 4 * g + 4):
                            last = pe.transpose(wide_ps(7 if g == 0 else 2)[:, h % 4], Tm[:, h], ident[:, :])
                        last.then_inc(s["x1"], 1)
                    key_sums(i + 1)
                pe.wait_ge(s["Wc"], 2 * i + 2)
                if first:
                    pe.wait_ge(s["x1c"], 4 * PASSES_0)
                else:
                    pe.wait_ge(s["tinit"], 10 * m + 10)
                for h in range(HEADS):
                    last = pe.matmul(bank[1][:, HD * h:HD * h + HD], TT[:, h], W[:, h], start=True, stop=True)
                last.then_inc(s["U"], 1)
                pe.wait_ge(s["Uc"], i + 1)
                apart(pe)
                for h in () if first else range(HEADS):
                    v_h = rvtok[:, h // 2, hp(h)]
                    o = wide_ps(3)[hp(h), h // 2]
                    pe.matmul(o, S0[:, h // 2], ar[:, h // 2, h % 2, 1], start=True, stop=False)
                    pe.matmul(o, U[:, h], mats[:, h, 0, 1], start=False, stop=False)
                    last = pe.matmul(o, v_h, mats[:, h, 1, 1], start=False, stop=True)
                if not first:
                    last.then_inc(s["Y"], 1)
                for h in range(HEADS):
                    o = bank[4][hp(h), HD * (h // 2):HD * (h // 2) + HD]
                    pe.matmul(o, btok[:, h // 2, hp(h)], U[:, h], start=True, stop=False)
                    last = pe.matmul(o, ktok[:, h // 2, hp(h)], rvtok[:, h // 2, hp(h)], start=False, stop=True)
                last.then_inc(s["S"], 1)
                if first:
                    return
                pe.wait_ge(s["Yc"], m + 1)
                pe.matmul(bank[5][:, :], headones[:, :], yT.rearrange("p c j -> p (c j)"), start=True, stop=True).then_inc(s["sums"], 1)
                pe.wait_ge(s["pn"], HEADS * m + HEADS)
                if prep:
                    pe.wait_ge(s["rn"], 2 * i + 3)
                for n in range(4):
                    part, g = n // 2, n % 2
                    for h in range(4 * g, 4 * g + 4):
                        last = pe.transpose(wide_ps((0, 1, 2, 7)[n])[:, h % 4], lg[:, h, part * P:(part + 1) * P], ident[:, :])
                    last.then_inc(s["tp"], 1)
                pe.wait_ge(s["sqr"], m + 1)
                pe.matmul(bank[6][:, :], headones[:, :], tmp[:, :, :].rearrange("p c j -> p (c j)"), start=True, stop=True).then_inc(s["sums"], 1)
                pe.wait_ge(s["rk"], 4 * m + 4)
                pe.matmul(bank[5][:, :], headones[:, :], rkb[:, :, :].rearrange("p c j -> p (c j)"), start=True, stop=True).then_inc(s["sums"], 1)
                for g in range(2):
                    if g == 1:
                        pe.wait_ge(s["Sn"], i + 1)
                    for h in range(4 * g, 4 * g + 4):
                        last = pe.transpose(wide_ps(3 + g)[0:META, h % 4], lg[:, h, 2 * P:BAND], ident[:, :])
                    last.then_inc(s["tp"], 1)
                pe.wait_ge(s["sg"], m + 1)
                pe.wait_ge(s["vr"], m + 1)
                for p in range(PAIRS):
                    last = pe.matmul(wide_ps(6)[:, p], gup[:, p * P:(p + 1) * P], sg[:, :], start=True, stop=True)
                last.then_inc(s["mmg"], 1)
                pe.wait_ge(s["tpc"], 6 * m + 6)
                for g in range(KV):
                    for e in range(2):
                        o = wide_ps(1)[HD * e:HD * e + HD, 2 * g:2 * g + 2]
                        hs = slice(4 * g + e, 4 * g + 4, 2)
                        vc = slice(HD * g, HD * g + HD)
                        pe.matmul(o, vtok[:, 0, vc], pT[:, 0, hs], start=True, stop=False)
                        pe.matmul(o, vtok[:, 1, vc], pT[:, 1, hs], start=False, stop=False)
                        last = pe.matmul(o, vtok[0:META, 2, vc], pTm[:, hs], start=False, stop=True)
                last.then_inc(s["O"], 1)

            low_rank(0)
            pe.wait_ge(s["th"], 4)
            key_sums(0)
            body(0, first=True)
            with pe.Fori(1, NBLK - 1) as i:
                body(i)
            body(NBLK - 1, last_block=True)


def merge(nc, sems, t, d):
    lg0, lg1, lo0, lo1, xl0, xl1, mm, th, sm, dn = sems(*(f"g_{k}" for k in "lg0 lg1 lo0 lo1 xl0 xl1 mm th sm dn".split()))
    ldg, ldo = (lg0, lg1), (lo0, lo1)
    HALF = SEQ // 2
    CPL = 2
    UNITS = 2 * CPL * 2
    STEPS = KD // (2 * CPL)
    K2 = RD // P
    with ExitStack() as ctx:
        sb = lambda n, s, dt=F32: ctx.enter_context(nc.sbuf_tensor(n, s, dt))
        xnT = sb("xnT2", [P, KD, SEQ])
        w = sb("w_merge", [P, 2, 2 * KD + 2 * K2, CPL * P])
        bank = [ctx.enter_context(nc.psum_tensor(f"mrg_ps{n}", [P, 4, 512], F32)) for n in range(2)]
        cT = t["cT"]
        g2 = cT[:, CH_WA:CH_WA + 2, 0:2 * HALF].rearrange("p u (b j) -> p u b j", b=2)
        m2 = cT[:, CH_K, 0:2 * HALF].rearrange("p (b j) -> p b j", b=2)
        gates = d["w_in"].rearrange("l (c p) n -> p (l c) n", p=P)
        woa = d["w_o_attn"].rearrange("l (c p) n -> p (l c) n", p=P)
        wor = d["w_o_rwkv"].rearrange("l (c p) n -> p (l c) n", p=P)
        block = ctx.enter_context(nc.Block())

        @block.sync
        def _(sp):
            def load_out(half, j):
                c = bass.ds(j * P, CPL * P)
                sp.dma_start(w[:, half, 2 * KD:2 * KD + K2], woa[:, :, c]).then_inc(ldo[half], 16)
                sp.dma_start(w[:, half, 2 * KD + K2:], wor[:, :, c]).then_inc(ldo[half], 16)

            def load_gates(half, j):
                for b in range(2):
                    sp.dma_start(w[:, half, b * KD:(b + 1) * KD], gates[:, :, bass.ds(GATE0 + b * D + j * P, CPL * P)]).then_inc(ldg[half], 16)

            xsp = d["xn_spill"].rearrange("p (c j) -> p c j", c=KD)
            load_out(0, 0)
            load_gates(0, 0)
            for part, sem in enumerate((xl0, xl1)):
                c = slice(part * HALF, (part + 1) * HALF)
                sp.dma_start(xnT[:, :, c], xsp[:, :, c]).then_inc(sem, 16)
            load_out(1, CPL)
            load_gates(1, CPL)
            with sp.Fori(1, STEPS) as i:
                for half in range(2):
                    sp.wait_ge(mm, (i - 1) * UNITS + (half + 1) * UNITS // 2)
                    load_out(half, i * (2 * CPL) + half * CPL)
                    load_gates(half, i * (2 * CPL) + half * CPL)
            sp.dma_start(t["wout"][:, :, :], d["w_out"].rearrange("l (c p) n -> p (l c) n", p=P)).then_inc(t["wout_loaded"], 16)

        @block.tensor
        def _(pe):
            pe.sem_inc(dn, 2)
            with pe.Fori(0, STEPS) as i:
                for n in range(UNITS):
                    half, c, part = n // (2 * CPL), (n // 2) % CPL, n % 2
                    if n % (2 * CPL) == 0:
                        pe.wait_ge(ldo[half], (i + 1) * 32)
                    pe.wait_ge(dn, i * UNITS + n + 1)
                    wc = slice(c * P, (c + 1) * P)
                    rows = slice(part * HALF, (part + 1) * HALF)
                    real = slice(P + part * HALF, P + (part + 1) * HALF)
                    ps = bank[n % 2]
                    for b, ch in enumerate((CH_Q, CH_RR)):
                        for k in range(K2):
                            pe.matmul(ps[:, 2 + b], w[:, half, 2 * KD + b * K2 + k, wc], cT[:, ch + k, real],
                                      start=(k == 0), stop=(k == K2 - 1))
                    if n % (2 * CPL) == 0:
                        pe.wait_ge(ldg[half], (i + 1) * 32)
                    if n < 2:
                        pe.wait_ge(xl1 if part else xl0, 16)
                    for b in range(2):
                        for k in range(KD):
                            last = pe.matmul(ps[:, b], w[:, half, b * KD + k, wc], xnT[:, k, rows], start=(k == 0), stop=(k == KD - 1))
                    last.then_inc(mm, 1)

        @block.scalar
        def _(act):
            with act.Fori(0, STEPS) as i:
                for n in range(UNITS):
                    act.wait_ge(mm, i * UNITS + n + 1)
                    act.wait_ge(dn, i * UNITS + n + 1)
                    act.activation(g2[:, n % 2], bank[n % 2][:, 0:2], ACT.Tanh, scale=0.5).then_inc(th, 1)

        @block.vector
        def _(v):
            with v.Fori(0, STEPS) as i:
                for n in range(UNITS):
                    c, part = n // 2, n % 2
                    v.wait_ge(th, i * UNITS + n + 1)
                    v.wait_ge(dn, i * UNITS + n + 2)
                    for b in range(2):
                        v.scalar_tensor_tensor(m2[:, b], g2[:, n % 2, b], 1.0, bank[n % 2][:, 2 + b], ALU.add, ALU.mult).then_inc(sm, 1)
                    v.wait_ge(sm, (i * UNITS + n) * 2 + 2)
                    out = cT[:, bass.ds(CH_MIX + i * (2 * CPL) + c, 1), P + part * HALF:P + (part + 1) * HALF]
                    v.tensor_tensor(out.rearrange("p a j -> p (a j)"), m2[:, 0], m2[:, 1], ALU.add).then_inc(dn, 1)


def route(nc, sems, t, d):
    names = "r_ld r_x0 r_x1 r_ms r_mm r_h r_sq r_m r_sd r_xn r_st0 r_st1 r_tp r_xt r_lg r_e r_ex r_oh r_rk r_v"
    ld, x0, x1, msr, mm, hd, sqd, msd, sdd, xnd, st0, st1, tp, xt, lgd, eg, ex, oh, rk, own = sems(*names.split())
    NV = t["route_count"]
    tick = t["tick"]
    with ExitStack() as ctx:
        sb = lambda n, s, dt=F32: ctx.enter_context(nc.sbuf_tensor(n, s, dt))
        ident, cT = t["ident"], t["cT"]
        wout = t["wout"]
        wr = sb("w_router", [P, KD, NG + E])
        br = sb("b_router", [P, NG + E])
        gf = sb("g_ffn", [P, D])
        iota, before, ones = sb("iota", [P, E]), sb("before", [P, P]), sb("ones", [P, P])
        ms = sb("ms", [P, 2, KD, P])
        xb = sb("xb", [P, 2, D])
        h1 = sb("h1", [P, 2, D])
        xn = sb("xn2", [P, 2, D])
        sq = sb("sq2", [P, D])
        x2T = sb("x2T", [P, KD, P])
        sc = sb("sc", [P, 16])
        ss, rs, m0, sg, e2, dv, exv, g1, gidx, ones1 = (sc[:, n:n + 1] for n in range(10))
        gl8, el, m8 = sb("gl8", [P, 8]), sb("el", [P, NG, EG]), sb("m8", [P, 8])
        i8 = sb("i8", [P, 8], U32)
        pen, junk = sb("pen", [P, NG]), sb("junk", [P, 8])
        o12, om, pr = sb("o12", [P, TOPK, E]), sb("om", [P, E]), sb("pr", [P, TOPK, E])
        R, carry = sb("R", [P, E]), t["carry"]
        ps_h = [ctx.enter_context(nc.psum_tensor(f"h_ps{n}", [P, D], F32)) for n in range(2)]
        ps_t = ctx.enter_context(nc.psum_tensor("t_ps", [P, KD, P], F32))
        ps_l = ctx.enter_context(nc.psum_tensor("l_ps", [P, 512], F32))
        ps_r = ctx.enter_context(nc.psum_tensor("r_ps", [P, 512], F32))
        xv = d["x"].rearrange("b (n p) d -> (b n) p d", p=P)
        h1v, xn2v = (d[n].rearrange("(n p) d -> n p d", p=P) for n in ("h1_rows", "xn2_rows"))
        block = ctx.enter_context(nc.Block())
        STEPS = NB // 2

        @block.sync
        def _(sp):
            sp.dma_start(wr[:, :, 0:NG], d["w_grp"].rearrange("l (c p) n -> p (l c) n", p=P)).then_inc(ld, 16)
            sp.dma_start(wr[:, :, NG:], d["w_exp"].rearrange("l (c p) n -> p (l c) n", p=P)).then_inc(ld, 16)
            sp.dma_start(br[:, 0:NG], d["b_grp"][0:1, :].broadcast_to([P, NG])).then_inc(ld, 16)
            sp.dma_start(br[:, NG:], d["b_exp"][0:1, :].broadcast_to([P, E])).then_inc(ld, 16)
            sp.dma_start(gf[:, :], d["norm_ffn_g"][0:1, :].broadcast_to([P, D])).then_inc(ld, 16)
            sp.dma_start(iota[:, :], d["c_iota"]).then_inc(ld, 16)
            sp.dma_start(before[:, :], d["c_upper"][:, 0]).then_inc(ld, 16)
            with sp.Fori(0, STEPS) as i:
                for u, (sx, st) in enumerate(((x0, st0), (x1, st1))):
                    sp.wait_ge(hd, 2 * i + u + 1)
                    sp.dma_start(xb[:, u], xv[bass.ds(2 * i + u, 1)]).then_inc(sx, 16)
                for u, st in enumerate((st0, st1)):
                    sp.wait_ge(hd, 2 * i + u + 3)
                    sp.dma_start(h1v[bass.ds(2 * i + u, 1)], h1[:, u]).then_inc(st, 16)
                    sp.wait_ge(xnd, 2 * i + u + 1)
                    sp.dma_start(xn2v[bass.ds(2 * i + u, 1)], xn[:, u]).then_inc(st, 16)
            sp.wait_ge(st0, 32 * STEPS + 32)
            sp.wait_ge(st1, 32 * STEPS + 32)


        @block.scalar
        def _(act):
            act.sem_inc(mm, 2)

            def stationary(n, u):
                act.wait_ge(mm, n + 1)
                act.sem_inc(tick, 1)
                act.activation(ms[:, u], cT[:, CH_MIX:CH_MIX + KD, bass.ds(P + n * P, P)], ACT.Copy).then_inc(msr, 1)

            def norm(n, u):
                act.wait_ge(hd, n + 3)
                act.activation(sq[:, :], h1[:, u], ACT.Square, accum_out=ss).then_inc(sqd, 1)
                act.wait_ge(msd, n + 1)
                act.activation(rs, ss, ACT.Sqrt).then_inc(sdd, 1)

            def step(n, u, ahead=2):
                act.wait_ge(tp, n + 1)
                act.wait_ge(lgd, n + 1)
                act.activation(x2T[:, :, :], ps_t[:, :, :], ACT.Copy).then_inc(xt, 1)
                if ahead > 1:
                    stationary(n + 2, u)
                if ahead > 0:
                    norm(n + 1, (u + 1) % 2)
                act.wait_ge(eg, n + 1)
                act.activation(junk[:, :], gl8[:, :], ACT.Exp, bias=m0, accum_out=sg).then_inc(ex, 1)
                act.activation(exv, dv, ACT.Exp).then_inc(ex, 1)

            stationary(0, 0)
            stationary(1, 1)
            norm(0, 0)
            step(0, 0)
            with act.Fori(0, STEPS - 2) as i:
                for k in range(2):
                    step(2 * i + k + 1, (k + 1) % 2)
            for n in range(NB - 3, NB):
                step(n, n % 2, min(2, NB - 1 - n))

        @block.vector
        def _(v):
            v.memset(gl8[:, :], NEG).then_inc(own, 1)
            v.memset(ones[:, :], 1.0).then_inc(own, 1)
            v.memset(carry[:, :], 0.0).then_inc(own, 1)
            v.sem_inc(hd, 2)
            v.sem_inc(sdd, 1)
            v.sem_inc(lgd, 1)
            v.wait_ge(ld, 7 * 16)
            def norm(n, u, pair, link):
                v.wait_ge(x1 if u else x0, 16 * pair + 16)
                v.wait_ge(mm, n + 3)
                v.wait_ge(st1 if u else st0, 32 * pair + 32)
                for hf in range(2):
                    c = slice(hf * 512, hf * 512 + 512)
                    link.add(v.scalar_tensor_tensor(h1[:, u, c], ps_h[u][:, c], 0.5, xb[:, u, c], ALU.mult, ALU.add))
                link.join()
                v.sem_inc(hd, 1)
                v.wait_ge(sqd, n + 1)
                v.tensor_scalar(ss, ss, 1.0 / D, EPS, ALU.mult, ALU.add).then_inc(msd, 1)
                v.wait_ge(sdd, n + 2)
                link(v.reciprocal(rs, rs))
                v.scalar_tensor_tensor(xn[:, u], h1[:, u], rs, gf[:, :], ALU.mult, ALU.mult).then_inc(xnd, 1)

            def router(n, link):
                v.wait_ge(lgd, n + 2)
                link.add(v.tensor_tensor(gl8[:, 0:NG], ps_l[:, 0:NG], br[:, 0:NG], ALU.add))
                link(v.tensor_tensor(el[:, :, :].rearrange("p g e -> p (g e)"), ps_l[:, NG:NG + E], br[:, NG:], ALU.add))
                v.sem_inc(tick, 1)
                link(v.max(m8[:, :], gl8[:, :]))
                v.sem_inc(tick, 1)
                link.add(v.max_index(i8[:, :], m8[:, :], gl8[:, :]))
                link(v.tensor_scalar(m0, m8[:, 0:1], -1.0, None, ALU.mult))
                link(v.tensor_copy(gidx, i8[:, 0:1]))
                link(v.tensor_scalar(pen[:, :], iota[:, 0:NG], gidx, NEG, ALU.not_equal, ALU.mult))
                link(v.tensor_tensor(el[:, :, :], el[:, :, :], pen[:, :].unsqueeze(2).broadcast_to([P, NG, EG]), ALU.add))
                flat = el[:, :, :].rearrange("p g e -> p (g e)")
                v.sem_inc(tick, 1)
                link(v.max(m8[:, :], flat))
                v.sem_inc(tick, 1)
                link.add(v.max_index(i8[:, :], m8[:, :], flat))
                link(v.tensor_tensor(dv, m8[:, 1:2], m8[:, 0:1], ALU.subtract))
                v.sem_inc(eg, 1)
                e_n = t["eids"][:, bass.ds(n, 1), :].rearrange("p a k -> p (a k)")
                link(v.tensor_copy(e_n, i8[:, 0:TOPK]))
                for k in range(TOPK):
                    link.add(v.tensor_scalar(o12[:, k], iota[:, :], t["eids"][:, bass.ds(n, 1), k], None, ALU.is_equal))
                link.join()
                v.tensor_tensor(om[:, :], o12[:, 0], o12[:, 1], ALU.add).then_inc(oh, 1)
                v.wait_ge(ex, 2 * n + 2)
                link(v.tensor_scalar(g1, exv, 1.0, None, ALU.add))
                link(v.tensor_tensor(g1, g1, sg, ALU.mult))
                link(v.reciprocal(g1, g1))
                link.add(v.tensor_scalar(t["wts"][:, bass.ds(n, 1), 0], g1, 0.5, None, ALU.mult))
                link(v.tensor_scalar(t["wts"][:, bass.ds(n, 1), 1], g1, exv, 0.5, ALU.mult, ALU.mult))

            def ranks(n, link):
                v.wait_ge(rk, n + 1)
                link(v.tensor_tensor(R[:, :], ps_r[:, 0:E], carry[:, :], ALU.add))
                link.add(v.tensor_tensor(pr[:, :, :], o12[:, :, :], R[:, :].unsqueeze(1).broadcast_to([P, TOPK, E]), ALU.mult))
                link(v.tensor_tensor(carry[:, :], carry[:, :], ps_r[:, E:2 * E], ALU.add))
                link(v.tensor_reduce(t["ranks"][:, bass.ds(n, 1), :].rearrange("p a k -> p (a k)"), pr[:, :, :], AX.X, ALU.add))

            link = Chain(v, own, 3)
            norm(0, 0, 0, link)
            norm(1, 1, 0, link)
            router(0, link)
            base = 3 + link.n
            with v.Fori(0, STEPS - 1) as i:
                link = Chain(v, own, i * NV + base)
                for k in range(2):
                    n = 2 * i + k + 1
                    norm(n + 1, k, i + 1, link)
                    ranks(n - 1, link)
                    router(n, link)
            assert link.n == NV, link.n
            link = Chain(v, own, (STEPS - 1) * NV + base)
            ranks(NB - 2, link)
            router(NB - 1, link)
            ranks(NB - 1, link)

        @block.gpsimd
        def _(pool):
            pool.sem_inc(st0, 32)
            pool.sem_inc(st1, 32)

        @block.tensor
        def _(pe):
            pe.wait_ge(ld, 7 * 16)
            pe.wait_ge(t["wout_loaded"], 16)
            pe.wait_ge(own, 3)

            def product(n, u, turned=True):
                pe.wait_ge(msr, n + 1)
                pe.wait_ge(hd, n + 1)
                for hf in range(2):
                    if hf == 1 and turned:
                        turn(n - 1, (u + 1) % 2)
                    for k in range(KD):
                        last = pe.matmul(ps_h[u][:, hf * 512:hf * 512 + 512], ms[:, u, k], wout[:, k, hf * 512:hf * 512 + 512],
                                         start=(k == 0), stop=(k == KD - 1))
                last.then_inc(mm, 1)

            def turn(n, u):
                pe.wait_ge(xnd, n + 1)
                for k in range(KD):
                    last = pe.transpose(ps_t[:, k], xn[:, u, k * P:(k + 1) * P], ident[:, :])
                last.then_inc(tp, 1)

            def router(n):
                pe.wait_ge(xt, n + 1)
                for k in range(KD):
                    last = pe.matmul(ps_l[:, 0:NG + E], x2T[:, k], wr[:, k], start=(k == 0), stop=(k == KD - 1))
                last.then_inc(lgd, 1)

            def ranks(n):
                pe.wait_ge(oh, n + 1)
                pe.matmul(ps_r[:, 0:E], before[:, :], om[:, :], start=True, stop=True)
                pe.matmul(ps_r[:, E:2 * E], ones[:, :], om[:, :], start=True, stop=True).then_inc(rk, 1)

            product(0, 0, turned=False)
            product(1, 1)
            router(0)
            with pe.Fori(0, STEPS - 1) as i:
                for k in range(2):
                    n = 2 * i + k + 1
                    product(n + 1, k)
                    ranks(n - 1)
                    router(n)
            ranks(NB - 2)
            turn(NB - 1, (NB - 1) % 2)
            router(NB - 1)
            ranks(NB - 1)


def table(nc, sems, t, d):
    ld, own, zs, sc, sl = sems("t_ld", "t_own", "t_zs", "t_sc", "t_sl")
    R2 = NB * TOPK
    KNOWN = 12
    with ExitStack() as ctx:
        sb = lambda n, s, dt=F32: ctx.enter_context(nc.sbuf_tensor(n, s, dt))
        iota, over, blockno = sb("iota_t", [P, E]), sb("over", [P, NB]), sb("blockno", [P, BLOCKS])
        tokno = sb("tokno", [P, NB], I32)
        zero = sb("zero", [P, BLOCKS], I32)
        cmp, nblk, end, start = sb("cmp", [P, E, NB]), sb("nblk", [P, E]), sb("end", [P, E]), sb("start", [P, E])
        one = sb("one_t", [P, E])
        oh, rb, pos = sb("oh_t", [P, R2, E]), sb("rb", [P, R2]), sb("pos", [P, R2])
        rc = sb("rc", [P, R2, NB])
        sidx = sb("sidx", [P, R2], I32)
        be, bc = sb("be", [1, BLOCKS]), sb("bc", [1, BLOCKS, E])
        block = ctx.enter_context(nc.Block())
        eids, ranks = (t[n][:, :, :].rearrange("p n k -> p (n k)") for n in ("eids", "ranks"))

        @block.sync
        def _(sp):
            sp.dma_start(iota[:, :], d["c_iota"]).then_inc(ld, 16)
            sp.dma_start(over[:, :], d["c_over"]).then_inc(ld, 16)
            sp.dma_start(blockno[:, :], d["c_blockno"]).then_inc(ld, 16)
            sp.dma_start(tokno[:, :], d["c_tokno"]).then_inc(ld, 16)
            sp.wait_ge(own, 1)
            sp.dma_start(d["slot_tok"].rearrange("(p b) a -> p (b a)", p=P), zero[:, :]).then_inc(zs, 16)
            sp.wait_ge(own, KNOWN)
            for n in range(EARLY):
                load_weights(sp, t, d, sp.value_load(t["bexp"][0:1, n:n + 1], min_val=0, max_val=E - 1), n)
            sp.wait_ge(sc, 16 * R2)
            sp.dma_start(t["slots"][:, 0:BLOCKS], d["slot_tok"].rearrange("(p b) a -> p (b a)", p=P)).then_inc(sl, 16)
            sp.wait_ge(sl, 16)

        @block.vector
        def _(v):
            link = Chain(v, own)
            link.add(v.memset(zero[:, :], 0))
            link.add(v.memset(t["slots"][:, BLOCKS:], 0))
            link.add(v.memset(t["wts"][:, NB:], 0.0))
            link(v.memset(one[:, :], 1.0))
            v.wait_ge(ld, 64)
            wide = lambda x, n: x.unsqueeze(2).broadcast_to([P, x.shape[1], n])
            rows = lambda x, n: x.unsqueeze(1).broadcast_to([P, n, x.shape[1]])
            link(v.tensor_tensor(cmp[:, :, :], wide(t["carry"][:, :], NB), rows(over[:, :], E), ALU.is_gt))
            link(v.tensor_reduce(nblk[:, :], cmp[:, :, :], AX.X, ALU.add))
            link(v.tensor_tensor_scan(end[:, :], one[:, :], nblk[:, :], 0.0, ALU.mult, ALU.add))
            link(v.tensor_tensor(start[:, :], end[:, :], nblk[:, :], ALU.subtract))
            link(v.tensor_copy(t["used"][:, :], end[0:1, E - 1:E]))
            link(v.tensor_tensor(bc[:, :, :], end[0:1, :].unsqueeze(1).broadcast_to([1, BLOCKS, E]),
                                 blockno[0:1, :].unsqueeze(2).broadcast_to([1, BLOCKS, E]), ALU.is_le))
            link(v.tensor_reduce(be[:, :], bc[:, :, :], AX.X, ALU.add))
            link(v.tensor_scalar(t["bexp"][:, :], be[:, :], float(E - 1), None, ALU.min))
            assert link.n == KNOWN, link.n
            link(v.tensor_tensor(oh[:, :, :], wide(eids, E), rows(iota[:, :], R2), ALU.is_equal))
            link(v.tensor_tensor(oh[:, :, :], oh[:, :, :], rows(start[:, :], R2), ALU.mult))
            link(v.tensor_reduce(rb[:, :], oh[:, :, :], AX.X, ALU.add))
            link(v.tensor_tensor(rc[:, :, :], wide(ranks, NB), rows(over[:, :], R2), ALU.is_ge))
            link(v.tensor_reduce(pos[:, :], rc[:, :, :], AX.X, ALU.add))
            link(v.tensor_scalar(pos[:, :], pos[:, :], 1.0, None, ALU.subtract))
            link(v.tensor_tensor(rb[:, :], rb[:, :], pos[:, :], ALU.add))
            link(v.scalar_tensor_tensor(pos[:, :], pos[:, :], -float(P), ranks, ALU.mult, ALU.add))
            link.add(v.scalar_tensor_tensor(sidx[:, :], pos[:, :], float(BLOCKS), rb[:, :], ALU.mult, ALU.add))
            link(v.scalar_tensor_tensor(t["ydest"][:, :], rb[:, :], float(P), pos[:, :], ALU.mult, ALU.add))
            t["table_own"] = link.n

        @block.gpsimd
        def _(pool):
            pool.wait_ge(own, t["table_own"])
            pool.wait_ge(zs, 16)
            for n in range(R2):
                pool.indirect_dma_start(d["slot_tok"], bass.IndirectOffsetOnAxis(sidx[:, n:n + 1], 0),
                                        tokno[:, n // TOPK:n // TOPK + 1], None).then_inc(sc, 16)


def load_weights(sp, t, d, e, u):
    eg, eu = (d[n].rearrange("l e (p c) f -> (l e) p (c f)", p=P) for n in ("e_gate", "e_up"))
    ed = d["e_down"].rearrange("l e (p c) n -> (l e) p (c n)", p=P)
    sp.dma_start(t["w_gu"][:, u, 0].rearrange("p c f -> p (c f)"), eg[bass.ds(e, 1)]).then_inc(t["wgu"][u], 16)
    sp.dma_start(t["w_gu"][:, u, 1].rearrange("p c f -> p (c f)"), eu[bass.ds(e, 1)]).then_inc(t["wgu"][u], 16)
    sp.dma_start(t["w_dn"][:, u].rearrange("p c n -> p (c n)"), ed[bass.ds(e, 1)]).then_inc(t["wdn"][u], 16)


def experts(nc, sems, t, d):
    wgu, wdn = t["wgu"], t["wdn"]
    xg, yst = sems(*(f"e_xg{u}" for u in range(DEPTH_W))), sems("e_yst0", "e_yst1")
    ix, tp, xt, mm, th, hm, ht, hc, dm, ye, own = sems(*(f"e_{k}" for k in "ix tp xt mm th hm ht hc dm ye own".split()))
    FK = F // P
    tick = t["tick"]
    with ExitStack() as ctx:
        sb = lambda n, s, dt=F32: ctx.enter_context(nc.sbuf_tensor(n, s, dt))
        ident = t["ident"]
        w, wd = t["w_gu"], t["w_dn"]
        idx = [sb(f"idx{u}", [P, 1], I32) for u in range(DEPTH_W)]
        xr = [sb(f"xr{u}", [P, D]) for u in range(DEPTH_W)]
        xT = sb("xT", [P, 2, KD, P])
        sg, hmid = sb("sg_e", [P, 2, F]), sb("hmid", [P, 2, F])
        hT = sb("hT", [P, 2, FK, P])
        y = sb("y", [P, 2, D])
        ps_x = ctx.enter_context(nc.psum_tensor("x_ps", [P, KD, P], F32))
        ps_h = ctx.enter_context(nc.psum_tensor("hh_ps", [P, 2, 2, F], F32))
        ps_t = ctx.enter_context(nc.psum_tensor("ht_ps", [P, 512], F32))
        ps_y = ctx.enter_context(nc.psum_tensor("y_ps", [P, D], F32))
        yv = d["y_rows"].rearrange("(n p) d -> n p d", p=P)
        block = ctx.enter_context(nc.Block())

        def turns(n):
            return n // DEPTH_W + 1

        def both(eng, run):
            used = eng.value_load(t["used"][0:1, 0:1], min_val=0, max_val=BLOCKS)
            run(0, SURE)
            with eng.If(used > SURE):
                run(SURE, BLOCKS)
            apart(eng)

        def apart(eng):
            eng.sem_inc(tick, 1)

        @block.sync
        def _(sp):
            def store(n, u):
                sp.wait_ge(ye, 2 * n + 3)
                sp.dma_start(yv[bass.ds(n, 1)], y[:, u % 2]).then_inc(yst[u % 2], 16)

            sp.sem_inc(yst[0], 16)
            sp.sem_inc(yst[1], 16)

            def run(lo, hi):
                for n in range(lo or EARLY, lo + DEPTH_W):
                    e = sp.value_load(t["bexp"][0:1, n:n + 1], min_val=0, max_val=E - 1)
                    if lo:
                        sp.wait_ge(dm, n - 1)
                    else:
                        sp.wait_ge(xg[n - EARLY], 16)
                    load_weights(sp, t, d, e, n % DEPTH_W)
                with sp.Fori(lo // DEPTH_W + 1, hi // DEPTH_W) as i:
                    for u in range(DEPTH_W):
                        n = i * DEPTH_W + u
                        e = sp.value_load(t["bexp"][0:1, bass.ds(n, 1)], min_val=0, max_val=E - 1)
                        sp.wait_ge(dm, n - 1)
                        load_weights(sp, t, d, e, u)
                        store(n - DEPTH_W, u)
                if not lo:
                    sp.dma_start(t["h1_sb"][:, :, :], d["h1_rows"].rearrange("(n p) d -> p n d", p=P)).then_inc(t["h1_loaded"], 16)
                for n in range(hi - DEPTH_W, hi):
                    store(n, n % DEPTH_W)
                for k in range(2):
                    sp.wait_ge(yst[k], 16 * (hi // 2 + 1))

            both(sp, run)
            sp.wait_ge(t["h1_loaded"], 16)

        @block.gpsimd
        def _(pool):
            for u in range(DEPTH_W):
                pool.tensor_copy(idx[u][:, :], t["slots"][:, u:u + 1]).then_inc(ix, 1)

            def run(lo, hi):
                with pool.Fori(lo // DEPTH_W, hi // DEPTH_W) as i:
                    for u in range(DEPTH_W):
                        n = i * DEPTH_W + u
                        pool.wait_ge(ix, n + 1)
                        pool.wait_ge(tp, n + 1)
                        pool.sem_inc(tick, 1)
                        pool.indirect_dma_start(xr[u][:, :], None, d["xn2_rows"], bass.IndirectOffsetOnAxis(idx[u][:, :], 0)).then_inc(xg[u], 16)
                        pool.wait_ge(xg[u], 16 * i + 16)
                        nxt = t["slots"][:, bass.ds(n + DEPTH_W, 1)]
                        pool.tensor_copy(idx[u][:, :], nxt).then_inc(ix, 1)

            both(pool, run)

        @block.tensor
        def _(pe):
            pe.sem_inc(tp, DEPTH_W)
            pe.sem_inc(dm, 2)
            pe.sem_inc(xt, 2)

            def turn(n, u, i):
                pe.wait_ge(xg[u], i)
                pe.wait_ge(xt, 2 * n + 2)
                for k in range(KD):
                    last = pe.transpose(ps_x[:, k], xr[u][:, k:D:KD], ident[:, :])
                last.then_inc(tp, 1)

            def up(n, u, i):
                pe.wait_ge(wgu[u], i)
                pe.wait_ge(xt, 2 * n + 4)
                pe.wait_ge(hm, n + 1)
                for k in range(KD):
                    last = pe.matmul(ps_h[:, u % 2].rearrange("p a f -> p (a f)"), xT[:, u % 2, k], w[:, u, :, k], start=(k == 0), stop=(k == KD - 1))
                last.then_inc(mm, 1)

            def turn_hidden(n, u):
                pe.wait_ge(hm, n + 3)
                pe.wait_ge(hc, n + 1)
                for k in range(FK):
                    last = pe.transpose(ps_t[:, k * P:(k + 1) * P], hmid[:, u % 2, k:F:FK], ident[:, :])
                last.then_inc(ht, 1)

            def down(n, u, i):
                pe.wait_ge(wdn[u], i)
                pe.wait_ge(hc, n + 2)
                pe.wait_ge(ye, 2 * n + 1)
                for hf in range(2):
                    c = slice(hf * 512, hf * 512 + 512)
                    for k in range(FK):
                        last = pe.matmul(ps_y[:, c], hT[:, u % 2, k], wd[:, u, k, c], start=(k == 0), stop=(k == FK - 1))
                last.then_inc(dm, 1)

            def step(n, u, rounds):
                up(n, u, 32 * rounds[0])
                if rounds[2] is not None:
                    turn(n + 1, (u + 1) % DEPTH_W, 16 * rounds[2])
                down(n - 1, (u - 1) % DEPTH_W, 16 * rounds[1])
                turn_hidden(n, u)

            def run(lo, hi):
                turn(lo, 0, 16 * turns(lo))
                up(lo, 0, 32 * turns(lo))
                turn(lo + 1, 1, 16 * turns(lo + 1))
                turn_hidden(lo, 0)
                last_turn = hi // DEPTH_W - 1
                with pe.Fori(lo // DEPTH_W, last_turn) as i:
                    for u in range(1, DEPTH_W + 1):
                        n = i * DEPTH_W + u
                        step(n, u % DEPTH_W, [i + 1 + (u + k) // DEPTH_W for k in (0, -1, 1)])
                for n in range(last_turn * DEPTH_W + 1, hi):
                    step(n, n % DEPTH_W, [turns(n), turns(n - 1), turns(n + 1) if n + 1 < hi else None])
                down(hi - 1, (hi - 1) % DEPTH_W, 16 * turns(hi - 1))

            both(pe, run)

        @block.scalar
        def _(act):
            def take_x(n, u):
                act.wait_ge(tp, n + DEPTH_W + 1)
                act.wait_ge(mm, n + 1)
                for hf in range(2):
                    c = slice(hf * KD // 2, (hf + 1) * KD // 2)
                    act.activation(xT[:, u % 2, c], ps_x[:, c], ACT.Copy).then_inc(xt, 1)

            act.sem_inc(mm, 2)
            act.sem_inc(hc, 1)

            def body(n, u, i, more=True):
                act.wait_ge(mm, n + 3)
                act.wait_ge(hm, n + 1)
                act.activation(sg[:, u % 2], ps_h[:, u % 2, 0], ACT.Tanh, scale=0.5).then_inc(th, 1)
                if more:
                    take_x(n + 1, u + 1)
                act.wait_ge(ht, n + 1)
                act.wait_ge(dm, n + 1)
                act.activation(hT[:, u % 2].rearrange("p k j -> p (k j)"), ps_t[:, 0:F], ACT.Copy).then_inc(hc, 1)

            def run(lo, hi):
                take_x(lo, 0)
                with act.Fori(lo // DEPTH_W, hi // DEPTH_W - 1) as i:
                    for u in range(DEPTH_W):
                        body(i * DEPTH_W + u, u, i)
                for n in range(hi - DEPTH_W, hi):
                    body(n, n % DEPTH_W, None, n + 1 < hi)

            both(act, run)

        @block.vector
        def _(v):
            v.sem_inc(hm, 2)
            v.sem_inc(ye, 1)

            def hidden(n, u):
                v.wait_ge(th, n + 1)
                v.scalar_tensor_tensor(sg[:, u % 2], sg[:, u % 2], 1.0, ps_h[:, u % 2, 0], ALU.add, ALU.mult).then_inc(own, 1)
                v.wait_ge(own, n + 1)
                v.tensor_tensor(hmid[:, u % 2], sg[:, u % 2], ps_h[:, u % 2, 1], ALU.mult).then_inc(hm, 1)

            def take_y(n, u, rounds):
                v.wait_ge(dm, n + 3)
                v.wait_ge(yst[u % 2], 16 * rounds)
                for hf in range(2):
                    c = slice(hf * 512, hf * 512 + 512)
                    v.tensor_copy(y[:, u % 2, c], ps_y[:, c]).then_inc(ye, 1)

            def run(lo, hi):
                hidden(lo, 0)
                last_turn = hi // DEPTH_W - 1
                with v.Fori(lo // DEPTH_W, last_turn) as i:
                    for u in range(1, DEPTH_W + 1):
                        n = i * DEPTH_W + u
                        hidden(n, u % DEPTH_W)
                        take_y(n - 1, (u - 1) % DEPTH_W, i * 2 + (u - 1) // 2 + 1)
                for n in range(last_turn * DEPTH_W + 1, hi):
                    hidden(n, n % DEPTH_W)
                    take_y(n - 1, (n - 1) % DEPTH_W, (n - 1) // 2 + 1)
                take_y(hi - 1, (hi - 1) % DEPTH_W, (hi - 1) // 2 + 1)

            both(v, run)


def combine(nc, sems, t, d):
    DEPTH = 4
    names = "ld s0 s1 sm sq sd own ms dg mm".split()
    ld, s0, s1, smd, sqd, sdd, own, msd, dg, mm = sems(*(f"c_{k}" for k in names))
    rows = sems(*(f"c_rows{u}" for u in range(DEPTH)))
    NV = t["combine_count"]
    with ExitStack() as ctx:
        sb = lambda n, s, dt=F32: ctx.enter_context(nc.sbuf_tensor(n, s, dt))
        ident, h = t["ident"], t["h1_sb"]
        g = sb("g_final", [P, D])
        ya = [[sb(f"y{n}_{k}", [P, D]) for k in range(TOPK)] for n in range(NB)]
        diag = sb("diag", [P, 2, TOPK, P])
        o = sb("o_c", [P, 2, D])
        sq = sb("sq_c", [P, D])
        sc = sb("sc_c", [P, 2, 2])
        ps_y, ps_s = (ctx.enter_context(nc.psum_tensor(n, [P, 2, D], F32)) for n in ("yy_ps", "sum_ps"))
        ov = d["out"].rearrange("b (n p) d -> (b n) p d", p=P)
        block = ctx.enter_context(nc.Block())

        @block.sync
        def _(sp):
            sp.dma_start(g[:, :], d["norm_final_g"].rearrange("(a n) -> a n", a=1).broadcast_to([P, D])).then_inc(ld, 16)
            with sp.Fori(0, NB // 2) as i:
                for u, st in enumerate((s0, s1)):
                    sp.wait_ge(msd, 2 * i + u + 1)
                    sp.dma_start(ov[bass.ds(2 * i + u, 1)], o[:, u]).then_inc(st, 16)
            sp.wait_ge(s0, 16 * (NB // 2) + 16)
            sp.wait_ge(s1, 16 * (NB // 2) + 16)

        @block.gpsimd
        def _(pool):
            pool.sem_inc(s0, 16)
            pool.sem_inc(s1, 16)
            for n in range(NB):
                if n >= DEPTH:
                    pool.wait_ge(rows[n % DEPTH], 32 * (n // DEPTH))
                for k in range(TOPK):
                    pool.indirect_dma_start(ya[n][k][:, :], None, d["y_rows"],
                                            bass.IndirectOffsetOnAxis(t["ydest"][:, n * TOPK + k:n * TOPK + k + 1], 0)).then_inc(rows[n % DEPTH], 16)

        @block.tensor
        def _(pe):
            for n in range(NB):
                pe.wait_ge(dg, 2 * n + 2)
                pe.wait_ge(rows[n % DEPTH], 32 * (n // DEPTH) + 32)
                if n >= 2:
                    pe.wait_ge(smd, n - 1)
                for hf in range(2):
                    c = slice(hf * 512, hf * 512 + 512)
                    for k in range(TOPK):
                        last = pe.matmul(ps_y[:, n % 2, c], diag[:, n % 2, k], ya[n][k][:, c], start=(k == 0), stop=(k == TOPK - 1))
                last.then_inc(mm, 1)

        @block.scalar
        def _(act):
            with act.Fori(0, NB // 2) as i:
                for u in range(2):
                    n = 2 * i + u
                    act.wait_ge(smd, n + 1)
                    act.activation(sq[:, :], ps_s[:, u], ACT.Square, accum_out=sc[:, u, 0:1]).then_inc(sdd, 1)
                    act.wait_ge(sqd, n + 1)
                    act.activation(sc[:, u, 1:2], sc[:, u, 0:1], ACT.Sqrt).then_inc(sdd, 1)

        @block.vector
        def _(v):
            def diagonals(n, u):
                for k in range(TOPK):
                    v.tensor_scalar(diag[:, u, k], ident[:, :], t["wts"][:, bass.ds(n, 1), k], None, ALU.mult).then_inc(dg, 1)

            def add_up(n, u, link):
                v.wait_ge(mm, n + 1)
                diagonals(n + 1, (u + 1) % 2)
                v.wait_ge(mm, n + 2)
                hn = h[:, bass.ds(n, 1)].rearrange("p a d -> p (a d)")
                for hf in range(2):
                    c = slice(hf * 512, hf * 512 + 512)
                    link.add(v.tensor_tensor(ps_s[:, u, c], ps_y[:, u, c], hn[:, c], ALU.add))
                link.join()
                v.sem_inc(smd, 1)

            def norm(n, u, pair, link):
                v.wait_ge(sdd, 2 * n + 1)
                v.tensor_scalar(sc[:, u, 0:1], sc[:, u, 0:1], 1.0 / D, EPS, ALU.mult, ALU.add).then_inc(sqd, 1)
                v.wait_ge(sdd, 2 * n + 2)
                link(v.reciprocal(sc[:, u, 1:2], sc[:, u, 1:2]))
                v.wait_ge(s1 if u else s0, 16 * pair + 16)
                for hf in range(2):
                    c = slice(hf * 512, hf * 512 + 512)
                    link.add(v.scalar_tensor_tensor(o[:, u, c], ps_s[:, u, c], sc[:, u, 1:2], g[:, c], ALU.mult, ALU.mult))
                link.join()
                v.sem_inc(msd, 1)

            v.sem_inc(mm, 1)
            v.wait_ge(ld, 16)
            v.wait_ge(t["h1_loaded"], 16)
            diagonals(0, 0)
            link = Chain(v, own)
            add_up(0, 0, link)
            base = link.n
            pairs = NB // 2
            with v.Fori(0, pairs - 1) as i:
                link = Chain(v, own, i * NV + base)
                for u in range(2):
                    add_up(2 * i + u + 1, (u + 1) % 2, link)
                    norm(2 * i + u, u, i, link)
            assert link.n == NV, link.n
            link = Chain(v, own, (pairs - 1) * NV + base)
            add_up(NB - 1, 1, link)
            norm(NB - 2, 0, pairs - 1, link)
            norm(NB - 1, 1, pairs - 1, link)


def program(nc, d):
    with ExitStack() as ctx:
        def sems(*names):
            return [ctx.enter_context(nc.semaphore(n)) for n in names]

        sb = lambda n, s, dt=F32: ctx.enter_context(nc.sbuf_tensor(n, s, dt))

        t = {"ident": sb("ident", [P, P]), "carry": sb("carry", [P, E]), "eids": sb("eids", [P, NB, TOPK]),
             "ranks": sb("ranks", [P, NB, TOPK]), "wts": sb("wts", [P, NB + 1, TOPK]), "bexp": sb("bexp", [1, BLOCKS], I32), "used": sb("used", [1, 1], I32),
             "slots": sb("slots", [P, BLOCKS + 4], I32), "ydest": sb("ydest", [P, NB * TOPK], I32)}
        t["tick"], = sems("tick")
        t["mix_counts"] = (38, 3)
        t["route_count"] = 52
        t["combine_count"] = 10
        with nc.sbuf_tensor("cT", [P, CHUNKS, TP], F32) as cT:
            t["cT"] = cT
            t["w_in_loaded"] = sems("w_in_0", "w_in_1")
            t["mix_par"], t["y_zeroed"] = sems("mix_par", "y_zeroed")
            with ExitStack() as mixers:
                for n, shape in (("headones", [P, P]), ("upper", [P, 2, P]), ("lower", [P, P]), ("reset", [P, PAIRS * P]),
                                 ("wup", [P, 2, RD]), ("gup", [P, RD]), ("par", [P, 9, PAIRS]), ("sink", [P, HEADS])):
                    t[n] = mixers.enter_context(nc.sbuf_tensor(n, shape, F32))[:]
                with ExitStack() as inner:
                    for n, shape, dt in (("xh", [P, KD, TG], F32R), ("xl", [P, KD, TG], F32R), ("w_in_sb", [P, 2, KD, P], F32)):
                        t[n] = inner.enter_context(nc.sbuf_tensor(n, shape, dt))
                    norm_and_turn(nc, sems, t, d)
                    project(nc, sems, t, d)
                mix(nc, sems, t, d)
            t["wout_loaded"], = sems("wout_loaded")
            with nc.sbuf_tensor("wout", [P, KD, D], F32) as wout:
                t["wout"] = wout
                merge(nc, sems, t, d)
                route(nc, sems, t, d)
        t["wgu"], t["wdn"] = (sems(*(f"e_{k}{u}" for u in range(DEPTH_W))) for k in ("wgu", "wdn"))
        t["h1_loaded"], = sems("h1_loaded")
        t["h1_sb"] = sb("h1_sb", [P, NB, D])
        with nc.sbuf_tensor("w_gu", [P, DEPTH_W, 2, KD, F], F32) as w_gu, nc.sbuf_tensor("w_dn", [P, DEPTH_W, F // P, D], F32) as w_dn:
            t["w_gu"], t["w_dn"] = w_gu, w_dn
            table(nc, sems, t, d)
            experts(nc, sems, t, d)
        combine(nc, sems, t, d)


_INS = ["x", "meta_tokens", "norm_mix_g", "w_in", "shift_mu", "w0", "w_decay_up", "a0", "w_aaa_up", "w_gate_up",
        "k_k", "k_a", "r_k", "ln_x_g", "ln_x_b", "attn_sinks", "w_o_attn", "w_o_rwkv", "w_out", "norm_ffn_g",
        "w_grp", "b_grp", "w_exp", "b_exp", "e_gate", "e_up", "e_down", "norm_final_g"]


def kernel(**inputs):
    import numpy as _np
    import concourse.bacc as _bacc
    from concourse import mybir as _mybir
    from concourse.bass_utils import run_bass_kernel_spmd as _run

    nc = _bacc.Bacc("TRN2", target_bir_lowering=False, num_devices=1)
    arrays, d = {}, {}
    named = [(n, inputs[n]) for n in _INS] + [("c_" + n, a) for n, a in constants().items()]
    for name, a in named:
        a = _np.ascontiguousarray(a)
        arrays["in_" + name] = a
        d[name] = nc.dram_tensor("in_" + name, a.shape, _mybir.dt.from_np(a.dtype), kind="ExternalInput").ap()
    d["out"] = nc.dram_tensor("out", (1, SEQ, D), F32, kind="ExternalOutput").ap()
    for name, shape, dt in SCRATCH:
        d[name] = nc.dram_tensor(name, shape, dt, kind="Internal").ap()
    program(nc, d)
    r = _run(nc, [arrays], core_ids=[0])
    return r.results[0]["out"]


SCRATCH = [("xn_spill", (P, KD * SEQ), F32), ("xn2_rows", (SEQ, D), F32), ("h1_rows", (SEQ, D), F32),
           ("slot_tok", (BLOCKS * P, 1), I32), ("y_rows", (BLOCKS * P, D), F32)]
```
